# Optimizing a Trainium2 kernel written in Bass

```python
import math
import jax
import jax.numpy as jnp
from jax import lax
import numpy as np

D_MODEL = 1024
BATCH = 1
SEQ = 128
DEPTH = 2
DEC_BATCH = 1
DEC_SEQ = 256
PAST_LEN = 128

GRID_W = 64
N_EVEN = (DEPTH + 1) // 2
N_ODD = DEPTH // 2
RMS_EPS = 1e-6
NEG_INF = -1e30

SSD_INNER = D_MODEL
SSD_HEADDIM = 64
SSD_HEADS = SSD_INNER // SSD_HEADDIM
SSD_GROUPS = 2
SSD_STATE = 128
SSD_CONV = 5
SSD_CHUNK = 128
SSD_XBC = SSD_INNER + 2 * SSD_GROUPS * SSD_STATE

HY_CH = D_MODEL
HY_ORDER = 2
HY_SHORT = 3
HY_BANDS = 16
HY_FEAT = 1 + 2 * HY_BANDS
HY_HID = 64
HY_MIN_DECAY = abs(math.log(1e-2) / 1.5)
HY_MAX_DECAY = abs(math.log(1e-2) / 0.3)

EVEN_IN = SSD_INNER + SSD_XBC + SSD_HEADS + 3 * HY_CH
EVEN_OUT = SSD_INNER + HY_CH

HEAD_DIM = 64
NA_HEADS = D_MODEL // 128
NA_WIDTH = NA_HEADS * HEAD_DIM
NA_WIN_R = 8
NA_WIN_C = 16
NA_QCB = 16
NA_KCB = NA_QCB + NA_WIN_C

MLA_HEADS = D_MODEL // 128
MLA_Q_RANK = D_MODEL // 4
MLA_KV_RANK = D_MODEL // 8
MLA_NOPE = 64
MLA_ROPE = 32
MLA_V = 64
MLA_QK = MLA_NOPE + MLA_ROPE
ROPE_FREQS = MLA_ROPE // 4
ROPE_BASE = 10000.0

ODD_IN = 3 * NA_WIDTH + MLA_Q_RANK + MLA_KV_RANK + MLA_ROPE
ODD_OUT = NA_WIDTH + MLA_HEADS * MLA_V

MOE_GROUPS = 4
MOE_PER_GROUP = 8
MOE_EXPERTS = MOE_GROUPS * MOE_PER_GROUP
MOE_TOPK = 2
MOE_HIDDEN = D_MODEL // 4

ATTN_BLOCK = 128

kernel_name = 'hybrid_diffusion_prefix_step'

def rmsnorm(x, g):
    xf = x.astype(jnp.float32)
    y = xf * lax.rsqrt(jnp.mean(xf * xf, axis=-1, keepdims=True) + RMS_EPS)
    return (y * g.astype(jnp.float32)).astype(x.dtype)

def modulate(x, g, shift, scale):
    return rmsnorm(x, g) * (1.0 + scale[:, None]) + shift[:, None]

def dwconv_centred(x, w, b):
    k_w = w.shape[0]
    pad = k_w // 2
    L = x.shape[1]
    xp = jnp.pad(x, ((0, 0), (pad, pad), (0, 0)))
    y = b + xp[:, 0:L] * w[0]
    for k in range(1, k_w):
        y = y + xp[:, k:k + L] * w[k]
    return y

def merge_heads(o):
    b, h, L, d = o.shape
    return o.transpose(0, 2, 1, 3).reshape(b, L, h * d)

def softmax_attend(q, k, v, scale):
    b, h, Lq, dk = q.shape

    def attend(qb):
        s = jnp.einsum('bhqd,bhkd->bhqk', qb, k).astype(jnp.float32) * scale
        p = jax.nn.softmax(s, axis=-1).astype(v.dtype)
        return jnp.einsum('bhqk,bhkd->bhqd', p, v)

    if Lq <= ATTN_BLOCK or Lq % ATTN_BLOCK != 0:
        return attend(q)
    nb = Lq // ATTN_BLOCK
    qb = q.reshape(b, h, nb, ATTN_BLOCK, dk).transpose(2, 0, 1, 3, 4)
    out = lax.map(attend, qb)
    return out.transpose(1, 2, 0, 3, 4).reshape(b, h, Lq, v.shape[-1])

def axial_rope_tables(L):
    t = jnp.arange(L, dtype=jnp.int32)
    row = (t // GRID_W).astype(jnp.float32)
    col = (t % GRID_W).astype(jnp.float32)
    inv = ROPE_BASE ** (-jnp.arange(ROPE_FREQS, dtype=jnp.float32) / ROPE_FREQS)
    ang = jnp.stack([row[:, None] * inv, col[:, None] * inv], axis=1)
    return jnp.cos(ang), jnp.sin(ang)

def apply_axial_rope(x, cos, sin):
    shp = x.shape
    xr = x.astype(jnp.float32).reshape(shp[:-1] + (2, 2, ROPE_FREQS))
    x1, x2 = xr[..., 0, :], xr[..., 1, :]
    out = jnp.stack([x1 * cos - x2 * sin, x2 * cos + x1 * sin], axis=-2)
    return out.reshape(shp).astype(x.dtype)

def ssd_chunked(x, dt, Bm, Cm, A, init):
    b, L, H, P = x.shape
    G, N = Bm.shape[2], Bm.shape[3]
    T = SSD_CHUNK
    nc = L // T
    rep = H // G
    xdt = (x * dt[..., None]).reshape(b, nc, T, H, P)
    Bc = Bm.reshape(b, nc, T, G, N)
    Cc = Cm.reshape(b, nc, T, G, N)
    cs = jnp.cumsum((dt * A).reshape(b, nc, T, H), axis=2)
    causal = jnp.tril(jnp.ones((T, T), dtype=bool))[None, None, :, :, None]
    decay_in = jnp.exp(jnp.where(causal, cs[:, :, :, None, :] - cs[:, :, None, :, :], -jnp.inf))
    cb = jnp.repeat(jnp.einsum('bclgn,bcsgn->bclsg', Cc, Bc), rep, axis=-1)
    y_diag = jnp.einsum('bclsh,bcshp->bclhp', cb * decay_in, xdt)
    Bh = jnp.repeat(Bc, rep, axis=3)
    Ch = jnp.repeat(Cc, rep, axis=3)
    states = jnp.einsum('bclhn,bclhp->bchpn', Bh * jnp.exp(cs[:, :, -1:, :] - cs)[..., None], xdt)
    chunk_decay = jnp.exp(cs[:, :, -1, :])

    def step(carry, inp):
        st, dec = inp
        return carry * dec[:, :, None, None] + st, carry

    final, entering = lax.scan(step, init, (jnp.moveaxis(states, 1, 0), jnp.moveaxis(chunk_decay, 1, 0)))
    entering = jnp.moveaxis(entering, 0, 1)
    y_off = jnp.einsum('bclhn,bchpn->bclhp', Ch, entering) * jnp.exp(cs)[..., None]
    return (y_diag + y_off).reshape(b, L, H, P), final

def bidirectional_ssd(x, dt_raw, Bm, Cm, A_log, dt_bias, init):
    x, Bm, Cm = x.astype(jnp.float32), Bm.astype(jnp.float32), Cm.astype(jnp.float32)
    outs, finals = [], []
    for d in range(2):
        dt = jax.nn.softplus(dt_raw.astype(jnp.float32) + dt_bias[d].astype(jnp.float32))
        A = -jnp.exp(A_log[d].astype(jnp.float32))
        if d == 0:
            y, fin = ssd_chunked(x, dt, Bm, Cm, A, init[:, d].astype(jnp.float32))
        else:
            y, fin = ssd_chunked(jnp.flip(x, axis=1), jnp.flip(dt, axis=1), jnp.flip(Bm, axis=1),
                                 jnp.flip(Cm, axis=1), A, init[:, d].astype(jnp.float32))
            y = jnp.flip(y, axis=1)
        outs.append(y)
        finals.append(fin)
    return outs[0] + outs[1], jnp.stack(finals, axis=1)

def hyena_filters(L, w1, b1, w2, b2, w3, freq):
    t = jnp.linspace(0.0, 1.0, L, dtype=jnp.float32)[:, None]
    w = 2.0 * math.pi * jnp.arange(L, dtype=jnp.float32) / L
    bands = jnp.linspace(1e-4, HY_BANDS - 1, HY_BANDS, dtype=jnp.float32)
    ang = w[:, None] * bands[None]
    feat = jnp.concatenate([t, jnp.cos(ang), -jnp.sin(ang)], axis=-1)
    hdn = jnp.sin(freq[0] * (feat @ w1 + b1))
    hdn = jnp.sin(freq[1] * (hdn @ w2 + b2))
    h = (hdn @ w3).astype(jnp.float32).reshape(L, HY_ORDER, 2, HY_CH)
    deltas = jnp.linspace(HY_MIN_DECAY, HY_MAX_DECAY, HY_CH, dtype=jnp.float32)
    h = h * jnp.exp(-t * deltas)[:, None, None, :]
    fwd, bwd = h[:, :, 0], h[:, :, 1]
    return jnp.concatenate([fwd, jnp.zeros_like(fwd[:1]), jnp.flip(bwd[1:], axis=0)], axis=0)

def long_conv(u, h, bias):
    L = u.shape[1]
    uf = u.astype(jnp.float32)
    U = jnp.fft.rfft(uf, n=2 * L, axis=1)
    Hf = jnp.fft.rfft(h.astype(jnp.float32), axis=0)
    y = jnp.fft.irfft(U * Hf[None], n=2 * L, axis=1)[:, :L]
    return (y + uf * bias.astype(jnp.float32)).astype(u.dtype)

def even_mixer(h, init_state, w_in, conv_w, conv_b, A_log, dt_bias, d_skip, g_ssd,
               hy_conv_w, hy_conv_b, hy_w1, hy_b1, hy_w2, hy_b2, hy_w3, hy_freq, hy_bias, w_out):
    b, L, _ = h.shape
    proj = h @ w_in
    z, xbc, dt_raw, hy = jnp.split(proj, [SSD_INNER, SSD_INNER + SSD_XBC, SSD_INNER + SSD_XBC + SSD_HEADS], axis=-1)
    xbc = jax.nn.silu(dwconv_centred(xbc, conv_w, conv_b))
    xs, Bm, Cm = jnp.split(xbc, [SSD_INNER, SSD_INNER + SSD_GROUPS * SSD_STATE], axis=-1)
    xs = xs.reshape(b, L, SSD_HEADS, SSD_HEADDIM)
    Bm = Bm.reshape(b, L, SSD_GROUPS, SSD_STATE)
    Cm = Cm.reshape(b, L, SSD_GROUPS, SSD_STATE)
    y, final = bidirectional_ssd(xs, dt_raw, Bm, Cm, A_log, dt_bias, init_state)
    y = y + xs.astype(jnp.float32) * d_skip.astype(jnp.float32)[:, None]
    y = y.astype(h.dtype).reshape(b, L, SSD_INNER)
    y = rmsnorm(y * jax.nn.silu(z), g_ssd)
    parts = jnp.split(dwconv_centred(hy, hy_conv_w, hy_conv_b), 1 + HY_ORDER, axis=-1)
    filters = hyena_filters(L, hy_w1, hy_b1, hy_w2, hy_b2, hy_w3, hy_freq)
    u = parts[0]
    for o in range(HY_ORDER):
        u = parts[o + 1] * long_conv(u, filters[:, o], hy_bias[o])
    return jnp.concatenate([y, u], axis=-1) @ w_out, final

def odd_project(h, w_in, g_q, w_uq, g_kv):
    b, L, _ = h.shape
    proj = h @ w_in
    qkv, q_dn, kv_dn, k_rope = jnp.split(
        proj, [3 * NA_WIDTH, 3 * NA_WIDTH + MLA_Q_RANK, 3 * NA_WIDTH + MLA_Q_RANK + MLA_KV_RANK], axis=-1)
    qkv = qkv.reshape(b, L, 3, NA_HEADS, HEAD_DIM).transpose(2, 0, 3, 1, 4)
    q_mla = (rmsnorm(q_dn, g_q) @ w_uq).reshape(b, L, MLA_HEADS, MLA_QK).transpose(0, 2, 1, 3)
    ckv = rmsnorm(kv_dn, g_kv)
    return qkv[0], qkv[1], qkv[2], q_mla, ckv, k_rope

def mla_keys(ckv, k_rope, w_ukv):
    b, L, _ = ckv.shape
    kv = (ckv @ w_ukv).reshape(b, L, MLA_HEADS, MLA_NOPE + MLA_V).transpose(0, 2, 1, 3)
    k = jnp.concatenate([kv[..., :MLA_NOPE],
                         jnp.broadcast_to(k_rope[:, None].astype(kv.dtype), (b, MLA_HEADS, L, MLA_ROPE))], axis=-1)
    return k, kv[..., MLA_NOPE:]

def neighbourhood_attend(q, k, v, k_ctx, v_ctx, rel_bias):
    b, h, L, dh = q.shape
    rows = L // GRID_W
    kr = min(NA_WIN_R, rows)
    ncb = GRID_W // NA_QCB
    scale = dh ** -0.5
    r = jnp.arange(rows)
    r0 = jnp.clip(r - kr // 2, 0, rows - kr)
    qcol = jnp.arange(GRID_W).reshape(ncb, NA_QCB)
    c0 = jnp.clip(qcol - NA_WIN_C // 2, 0, GRID_W - NA_WIN_C)
    kb0 = jnp.clip(jnp.arange(ncb) * NA_QCB - NA_WIN_C // 2, 0, GRID_W - NA_KCB)
    col_idx = kb0[:, None] + jnp.arange(NA_KCB)[None]
    col_ok = (col_idx[:, None, :] >= c0[..., None]) & (col_idx[:, None, :] < c0[..., None] + NA_WIN_C)
    dr = r0[:, None] + jnp.arange(kr)[None] - r[:, None] + NA_WIN_R - 1
    dc = jnp.clip(col_idx[:, None, :] - qcol[..., None], -(NA_WIN_C - 1), NA_WIN_C - 1) + NA_WIN_C - 1
    bias = jnp.take(jnp.take(rel_bias.astype(jnp.float32), dr, axis=1), dc, axis=3)
    bias = jnp.where(col_ok[None, None, None], bias, NEG_INF).transpose(1, 0, 3, 4, 2, 5)
    k_grid = k.reshape(b, h, rows, GRID_W, dh)
    v_grid = v.reshape(b, h, rows, GRID_W, dh)
    q_rows = q.reshape(b, h, rows, ncb, NA_QCB, dh).transpose(2, 0, 1, 3, 4, 5)
    nwin = kr * NA_KCB

    def row_block(args):
        q_r, start, bias_r = args
        k_r = jnp.take(lax.dynamic_slice_in_dim(k_grid, start, kr, axis=2), col_idx, axis=3)
        v_r = jnp.take(lax.dynamic_slice_in_dim(v_grid, start, kr, axis=2), col_idx, axis=3)
        s_win = jnp.einsum('bhjqd,bhajkd->bhjqak', q_r, k_r).astype(jnp.float32) * scale + bias_r[None]
        s_ctx = jnp.einsum('bhjqd,bhcd->bhjqc', q_r, k_ctx).astype(jnp.float32) * scale
        s = jnp.concatenate([s_win.reshape(b, h, ncb, NA_QCB, nwin), s_ctx], axis=-1)
        p = jax.nn.softmax(s, axis=-1).astype(v.dtype)
        p_win = p[..., :nwin].reshape(b, h, ncb, NA_QCB, kr, NA_KCB)
        return (jnp.einsum('bhjqak,bhajkd->bhjqd', p_win, v_r)
                + jnp.einsum('bhjqc,bhcd->bhjqd', p[..., nwin:], v_ctx.astype(v.dtype)))

    out = lax.map(row_block, (q_rows, r0, bias))
    return out.transpose(1, 2, 0, 3, 4, 5).reshape(b, h, L, dh)

def odd_mixer_context(h, w_in, g_q, w_uq, g_kv, w_ukv, w_out):
    q_na, k_na, v_na, q_mla, ckv, k_rope = odd_project(h, w_in, g_q, w_uq, g_kv)
    o_na = softmax_attend(q_na, k_na, v_na, HEAD_DIM ** -0.5)
    k_m, v_m = mla_keys(ckv, k_rope, w_ukv)
    o_mla = softmax_attend(q_mla, k_m, v_m, MLA_QK ** -0.5)
    out = jnp.concatenate([merge_heads(o_na), merge_heads(o_mla)], axis=-1) @ w_out
    return out, k_na, v_na, ckv, k_rope

def odd_mixer_latent(h, k_na_c, v_na_c, ckv_c, krope_c, rel_bias, w_in, g_q, w_uq, g_kv, w_ukv, w_out):
    q_na, k_na, v_na, q_mla, ckv, k_rope = odd_project(h, w_in, g_q, w_uq, g_kv)
    o_na = neighbourhood_attend(q_na, k_na, v_na, k_na_c, v_na_c, rel_bias)
    cos, sin = axial_rope_tables(h.shape[1])
    q_mla = jnp.concatenate([q_mla[..., :MLA_NOPE], apply_axial_rope(q_mla[..., MLA_NOPE:], cos, sin)], axis=-1)
    k_lat, v_lat = mla_keys(ckv, apply_axial_rope(k_rope, cos, sin), w_ukv)
    k_ctx, v_ctx = mla_keys(ckv_c.astype(ckv.dtype), krope_c, w_ukv)
    o_mla = softmax_attend(q_mla, jnp.concatenate([k_lat, k_ctx], axis=2),
                           jnp.concatenate([v_lat, v_ctx], axis=2), MLA_QK ** -0.5)
    return jnp.concatenate([merge_heads(o_na), merge_heads(o_mla)], axis=-1) @ w_out

def hier_moe(h, w_gr, b_gr, w_er, b_er, w_gate, w_up, w_down):
    b, L, D = h.shape
    n_tok = b * L
    t = h.reshape(n_tok, D)
    g_prob = jax.nn.softmax((t @ w_gr).astype(jnp.float32) + b_gr.astype(jnp.float32), axis=-1)
    g_w, g_idx = lax.top_k(g_prob, 1)
    e_logits = ((t @ w_er).astype(jnp.float32) + b_er.astype(jnp.float32)).reshape(n_tok, MOE_GROUPS, MOE_PER_GROUP)
    e_prob = jax.nn.softmax(jnp.take_along_axis(e_logits, g_idx[:, :, None], axis=1)[:, 0], axis=-1)
    e_w, e_idx = lax.top_k(e_prob, MOE_TOPK)
    weights = g_w * e_w / jnp.sum(e_w, axis=-1, keepdims=True)
    expert = g_idx * MOE_PER_GROUP + e_idx
    combine = jnp.zeros((n_tok, MOE_EXPERTS), jnp.float32).at[jnp.arange(n_tok)[:, None], expert].add(weights)
    hid = jax.nn.silu(jnp.einsum('td,edf->tef', t, w_gate)) * jnp.einsum('td,edf->tef', t, w_up)
    out = jnp.einsum('tef,efd->td', hid * combine[..., None].astype(hid.dtype), w_down)
    return out.reshape(b, L, D).astype(h.dtype)

def setup_inputs(seed: int = 0) -> dict:
    key = jax.random.key(seed)
    keys = iter(jax.random.split(key, 64))

    def nrm(shape, scale):
        return jax.random.normal(next(keys), shape, jnp.float32) * scale

    def gain(shape):
        return 1.0 + nrm(shape, 0.01)

    dt0 = jnp.exp(jax.random.uniform(next(keys), (N_EVEN, 2, SSD_HEADS), jnp.float32,
                                     math.log(1e-3), math.log(1e-1)))
    a0 = jax.random.uniform(next(keys), (N_EVEN, 2, SSD_HEADS), jnp.float32, 1.0, 16.0)
    return {
        'x_prompt': nrm((BATCH, SEQ, D_MODEL), 1.0),
        'x_sample': nrm((DEC_BATCH, DEC_SEQ, D_MODEL), 1.0),
        'state_ssd': nrm((DEC_BATCH, N_EVEN, 2, SSD_HEADS, SSD_HEADDIM, SSD_STATE), 0.1),
        'cache_na_k': nrm((DEC_BATCH, N_ODD, NA_HEADS, PAST_LEN, HEAD_DIM), 1.0),
        'cache_na_v': nrm((DEC_BATCH, N_ODD, NA_HEADS, PAST_LEN, HEAD_DIM), 1.0),
        'cache_mla_ckv': nrm((DEC_BATCH, N_ODD, PAST_LEN, MLA_KV_RANK), 1.0),
        'cache_mla_krope': nrm((DEC_BATCH, N_ODD, PAST_LEN, MLA_ROPE), 1.0),
        'c': nrm((DEC_BATCH, D_MODEL), 1.0),
        'c_ctx': nrm((D_MODEL,), 1.0),
        'w_ada': nrm((DEPTH, D_MODEL, 6 * D_MODEL), 0.5 * D_MODEL ** -0.5),
        'b_ada': nrm((DEPTH, 6 * D_MODEL), 0.01),
        'norm_mix': gain((DEPTH, D_MODEL)),
        'norm_ffn': gain((DEPTH, D_MODEL)),
        'norm_final': gain((D_MODEL,)),
        'ev_w_in': nrm((N_EVEN, D_MODEL, EVEN_IN), D_MODEL ** -0.5),
        'ev_conv_w': nrm((N_EVEN, SSD_CONV, SSD_XBC), SSD_CONV ** -0.5),
        'ev_conv_b': nrm((N_EVEN, SSD_XBC), 0.02),
        'ssd_A_log': jnp.log(a0),
        'ssd_dt_bias': dt0 + jnp.log(-jnp.expm1(-dt0)),
        'ssd_d': gain((N_EVEN, SSD_HEADS)),
        'ssd_norm': gain((N_EVEN, SSD_INNER)),
        'hy_conv_w': nrm((N_EVEN, HY_SHORT, 3 * HY_CH), HY_SHORT ** -0.5),
        'hy_conv_b': nrm((N_EVEN, 3 * HY_CH), 0.02),
        'hy_w1': nrm((N_EVEN, HY_FEAT, HY_HID), HY_FEAT ** -0.5),
        'hy_b1': nrm((N_EVEN, HY_HID), 0.1),
        'hy_w2': nrm((N_EVEN, HY_HID, HY_HID), HY_HID ** -0.5),
        'hy_b2': nrm((N_EVEN, HY_HID), 0.1),
        'hy_w3': nrm((N_EVEN, HY_HID, HY_ORDER * 2 * HY_CH), 0.02),
        'hy_freq': 1.0 + nrm((N_EVEN, 2, HY_HID), 0.1),
        'hy_bias': nrm((N_EVEN, HY_ORDER, HY_CH), 0.5),
        'ev_w_out': nrm((N_EVEN, EVEN_OUT, D_MODEL), EVEN_OUT ** -0.5),
        'od_w_in': nrm((N_ODD, D_MODEL, ODD_IN), D_MODEL ** -0.5),
        'mla_q_norm': gain((N_ODD, MLA_Q_RANK)),
        'mla_w_uq': nrm((N_ODD, MLA_Q_RANK, MLA_HEADS * MLA_QK), MLA_Q_RANK ** -0.5),
        'mla_kv_norm': gain((N_ODD, MLA_KV_RANK)),
        'mla_w_ukv': nrm((N_ODD, MLA_KV_RANK, MLA_HEADS * (MLA_NOPE + MLA_V)), MLA_KV_RANK ** -0.5),
        'na_rel_bias': nrm((N_ODD, NA_HEADS, 2 * NA_WIN_R - 1, 2 * NA_WIN_C - 1), 0.5),
        'od_w_out': nrm((N_ODD, ODD_OUT, D_MODEL), ODD_OUT ** -0.5),
        'moe_w_gr': nrm((DEPTH, D_MODEL, MOE_GROUPS), D_MODEL ** -0.5),
        'moe_b_gr': nrm((DEPTH, MOE_GROUPS), 0.01),
        'moe_w_er': nrm((DEPTH, D_MODEL, MOE_EXPERTS), D_MODEL ** -0.5),
        'moe_b_er': nrm((DEPTH, MOE_EXPERTS), 0.01),
        'moe_w_gate': nrm((DEPTH, MOE_EXPERTS, D_MODEL, MOE_HIDDEN), D_MODEL ** -0.5),
        'moe_w_up': nrm((DEPTH, MOE_EXPERTS, D_MODEL, MOE_HIDDEN), D_MODEL ** -0.5),
        'moe_w_down': nrm((DEPTH, MOE_EXPERTS, MOE_HIDDEN, D_MODEL), MOE_HIDDEN ** -0.5),
    }

def reference(x_prompt, x_sample, state_ssd, cache_na_k, cache_na_v, cache_mla_ckv, cache_mla_krope, c, c_ctx,
              w_ada, b_ada, norm_mix, norm_ffn, norm_final, ev_w_in, ev_conv_w, ev_conv_b, ssd_A_log, ssd_dt_bias,
              ssd_d, ssd_norm, hy_conv_w, hy_conv_b, hy_w1, hy_b1, hy_w2, hy_b2, hy_w3, hy_freq, hy_bias, ev_w_out,
              od_w_in, mla_q_norm, mla_w_uq, mla_kv_norm, mla_w_ukv, na_rel_bias, od_w_out,
              moe_w_gr, moe_b_gr, moe_w_er, moe_b_er, moe_w_gate, moe_w_up, moe_w_down):
    xc, xl = x_prompt, x_sample
    new_ssd, new_na_k, new_na_v, new_ckv, new_krope = [], [], [], [], []
    for i in range(DEPTH):
        mod_c = jnp.split(jax.nn.silu(c_ctx)[None] @ w_ada[i] + b_ada[i], 6, axis=-1)
        mod_l = jnp.split(jax.nn.silu(c) @ w_ada[i] + b_ada[i], 6, axis=-1)
        hc = modulate(xc, norm_mix[i], mod_c[0], mod_c[1])
        hl = modulate(xl, norm_mix[i], mod_l[0], mod_l[1])
        if i % 2 == 0:
            e = i // 2
            ev = (ev_w_in[e], ev_conv_w[e], ev_conv_b[e], ssd_A_log[e], ssd_dt_bias[e], ssd_d[e], ssd_norm[e],
                  hy_conv_w[e], hy_conv_b[e], hy_w1[e], hy_b1[e], hy_w2[e], hy_b2[e], hy_w3[e], hy_freq[e],
                  hy_bias[e], ev_w_out[e])
            init_c = jnp.zeros((xc.shape[0], 2, SSD_HEADS, SSD_HEADDIM, SSD_STATE), jnp.float32)
            oc, fin_c = even_mixer(hc, init_c, *ev)
            ol, _ = even_mixer(hl, state_ssd[:, e], *ev)
            new_ssd.append(fin_c)
        else:
            o = i // 2
            od = (od_w_in[o], mla_q_norm[o], mla_w_uq[o], mla_kv_norm[o], mla_w_ukv[o], od_w_out[o])
            oc, k_c, v_c, ckv_c, kr_c = odd_mixer_context(hc, *od)
            ol = odd_mixer_latent(hl, cache_na_k[:, o], cache_na_v[:, o], cache_mla_ckv[:, o],
                                  cache_mla_krope[:, o], na_rel_bias[o], *od)
            new_na_k.append(k_c)
            new_na_v.append(v_c)
            new_ckv.append(ckv_c)
            new_krope.append(kr_c)
        xc = xc + mod_c[2][:, None] * oc
        xl = xl + mod_l[2][:, None] * ol
        moe = (moe_w_gr[i], moe_b_gr[i], moe_w_er[i], moe_b_er[i], moe_w_gate[i], moe_w_up[i], moe_w_down[i])
        xc = xc + mod_c[5][:, None] * hier_moe(modulate(xc, norm_ffn[i], mod_c[3], mod_c[4]), *moe)
        xl = xl + mod_l[5][:, None] * hier_moe(modulate(xl, norm_ffn[i], mod_l[3], mod_l[4]), *moe)
    y_prompt = rmsnorm(xc, norm_final)
    y_sample = rmsnorm(xl, norm_final)
    new_state_ssd = jnp.stack(new_ssd, axis=1)
    new_cache_na_k = jnp.stack(new_na_k, axis=1)
    new_cache_na_v = jnp.stack(new_na_v, axis=1)
    new_cache_mla_ckv = jnp.stack(new_ckv, axis=1)
    new_cache_mla_krope = jnp.stack(new_krope, axis=1)
    return (y_prompt, y_sample, new_state_ssd, new_cache_na_k, new_cache_na_v, new_cache_mla_ckv, new_cache_mla_krope)


_drawn_inputs = setup_inputs


def setup_inputs(seed=0):
    import zlib

    import numpy as np

    out = dict(_drawn_inputs(seed))
    spreads = {}
    factors = {'cache_na_k': 3.259,
     'cache_na_v': 2.755,
     'cache_mla_ckv': 4.746,
     'cache_mla_krope': 7.308,
     'norm_mix': 3.44,
     'norm_ffn': 5.069,
     'norm_final': 31.943,
     'ssd_d': 64.0,
     'ssd_norm': 8.0,
     'hy_conv_b': 3.955,
     'mla_q_norm': 8.0,
     'mla_kv_norm': 5.978,
     'na_rel_bias': 5.22,
     'moe_b_gr': 8.0,
     'moe_b_er': 7.527,
     'state_ssd': 8.0}
    for name, (base, spread) in spreads.items():
        noise = np.random.default_rng([zlib.crc32(name.encode()), seed]).standard_normal(out[name].shape)
        drawn = base * np.exp(spread * noise) if base else spread * noise
        out[name] = jnp.asarray(drawn.astype(out[name].dtype))
    for name, factor in factors.items():
        out[name] = (out[name] * factor).astype(out[name].dtype)
    return out
```

```python
from contextlib import ExitStack
import math

import numpy as np
import concourse.bass as bass
from concourse import mybir

F32 = mybir.dt.float32
I32 = mybir.dt.int32
ALU = mybir.AluOpType
ACT = mybir.ActivationFunctionType
AX_X = mybir.AxisListType.X

P = 128
D = 1024
KD = D // P
LP, LS = 128, 256
T = LP + LS
NT = T // P
SEGS = ((0, LP), (LP, T))
EPS = 1e-6
HEADS, HDIM, STATE, GROUPS = 16, 64, 128, 2
XBC = D + 2 * GROUPS * STATE
KX = XBC // P
TAPS, PAD = 5, 2
PADDED = PAD + LP + PAD + LS + PAD
HY_TAPS, HY_HID, HY_FEAT, HY_BANDS = 3, 64, 33, 16
COL_XBC, COL_DT, COL_HY = D, D + XBC, D + XBC + HEADS
AH, AD = 8, 64
GRID_W, WIN_R, WIN_C = 64, 8, 16
ROPE = 32
QK = AD + ROPE
QR = 256
E, PERG, NG, HID = 32, 8, 4, 256
CAP = 64
PAIRS = E // 2
ROUNDS = T // CAP
BIG = 1e30

SLOT, NSLOT = 4096, 6


ADA_AFTER = {("z", 3): (0, 4), ("z", 7): (0, 6), ("xbc", 3): (0, 8), ("xbc", 7): (0, 10), ("xbc", 11): (1, 0),
             ("hy", 0, 3): (1, 2), ("hy", 0, 7): (1, 4), ("hy", 1, 3): (1, 6), ("hy", 1, 7): (1, 8), ("hy", 2, 3): (1, 10)}


def stream_plan():
    first = [("ada", 0, b) for b in range(4)]
    for kind in [("z",)] * 2 + [("xbc",)] * 3 + [("hy", q) for q in range(3) for _ in range(2)]:
        block = kind + (sum(x[:-1] == kind for x in first),)
        first.append(block)
        l, b = ADA_AFTER.get(kind + (4 * block[-1] + 3,), (0, None))
        if b is not None:
            first += [("ada", l, b), ("ada", l, b + 1)]
    first += [("wout", b) for b in range(4)]
    second = [("od", b) for b in range(4)] + [("odout", b) for b in range(2)]
    return first, second


FIRST, SECOND = stream_plan()
LOADS = FIRST + SECOND
LOAD_AT = {n: k for k, n in enumerate(LOADS)}
assert len(FIRST) % NSLOT == 3 and len(SECOND) % NSLOT == 0 and 3 * PAIRS % NSLOT == 0


TURNS = [(i, h) for h in range(AH) for i in ("p", 0, 1)]


def bank_plan():
    j = []

    def job(name, by, block=None):
        j.append((name, by, block))

    def ada(l, b):
        for i in range(2):
            job(("adaw", l, b + i), "act")
        for i in range(2):
            job(("ada", l, b + i), "dve", ("ada", l, b + i))

    def ada_after(name):
        if name in ADA_AFTER:
            ada(*ADA_AFTER[name])

    for i in range(5):
        job(("par", i), "act")
    for k in range(KD):
        job(("xTr", k), "act")
    for b in (0, 2):
        ada(0, b)
    job(("ss", "mix0"), "act")
    for c in range(KD):
        job(("z", c), "act", ("z", c // 4) if c % 4 == 3 else None)
        ada_after(("z", c))
    job(("dt",), "dve")
    for c in range(KX):
        job(("xbc", c), "act", ("xbc", c // 4) if c % 4 == 3 else None)
        ada_after(("xbc", c))
    for t in range(NT):
        for half in range(2):
            job(("xtk", t, half), "act")
        job(("btk", t), "act")
    for d in range(2):
        for g in range(2):
            job(("sinit", d, g), "act")
    for t in range(NT):
        job(("wt", t), "act")
    for d in range(2):
        for g in range(2):
            job(("st0", d, g), "act")
    for d in range(2):
        for g in range(2):
            job(("st", d, g), "dve")
    for t in range(NT):
        job(("cb", t), "dve")
        for q in range(4):
            job(("E", t, q), "act")
            if t:
                job(("cs", t, q, 0), "act")
                job(("cs", t, q, 1), "act")
            job(("y", t, q), "dve")
    job(("ss", "ssd"), "act")
    for q in range(3):
        for c in range(KD):
            job(("hy", q, c), "act", ("hy", q, c // 4) if c % 4 == 3 else None)
            ada_after(("hy", q, c))
    job(("f", 0), "dve")
    job(("f", 1), "dve")
    for b in range(2):
        for o in range(2):
            for t in range(NT):
                job(("utk", b, o, t), "act")
            for s in range(2):
                nk = s + 1
                for x in range(2):
                    for t in range(nk):
                        job(("PQ", b, o, s, x, t), "dve")
                for k in range(nk):
                    job(("H", b, o, s, k, 0), "dve")
                    job(("H", b, o, s, k, 1), "act")
                for k in range(nk):
                    job(("U", b, o, s, k, 0), "none")
                    job(("U", b, o, s, k, 1), "dve")
                for c in range(4):
                    job(("inv", b, o, s, c), "dve")
    for m in range(KD):
        job(("wout", m), "dve", ("wout", m // 2) if m % 2 == 1 else None)

    def moe(l):
        job(("ss", "ffn%d" % l), "act")
        job(("rt", l), "dve")
        for t in range(NT):
            for h in range(2):
                job(("htk", l, t, h), "act")
        job(("pos", l), "dve")
        job(("tbl", l), "dve")
        job(("MOE", l), "none")
        for k in range(KD):
            job(("yTr", l, k), "dve")

    moe(0)
    job(("ss", "mix1"), "act")
    for c in range(8):
        job(("qk", c), "act", ("od", c // 4) if c % 4 == 3 else None)
    for t in range(NT):
        job(("v", t), "act", ("od", 2) if t == 2 else None)
    for c in range(4):
        job(("lat", c), "act", ("od", 3) if c == 3 else None)
    job(("ktok",), "act")
    job(("kctx",), "act")
    def heads(kind):
        job((kind,) + TURNS[0], "dve")
        for n, turn in enumerate(TURNS):
            if n + 1 < len(TURNS):
                job((kind,) + TURNS[n + 1], "dve")
            job((kind + "t",) + turn, "act")
            job((kind + "o",) + turn, "act")

    heads("na")
    job(("ss", "q"), "act")
    job(("ss", "kv"), "act")
    job(("mctx",), "act")
    job(("ckvtok",), "act")
    for h in range(AH):
        job(("qm", h), "act")
        job(("km", h), "act")
    for t in range(4):
        job(("vm", t), "act")
    heads("ml")
    for m in range(KD):
        job(("odout", m), "dve", ("odout", m // 4) if m % 4 == 3 else None)
    moe(1)
    job(("ss", "final"), "act")
    for t in range(NT):
        for h in range(2):
            job(("out", t, h), "act")
    return j


PLAN = bank_plan()
JOB = {n: i for i, (n, _, _) in enumerate(PLAN)}
assert len(JOB) == len(PLAN)
TAKER = [by for _, by, _ in PLAN]
RANK = [TAKER[:i].count(TAKER[i]) + 1 for i in range(len(PLAN))]
LAST_USE = {b: i for i, (_, _, b) in enumerate(PLAN) if b is not None}
assert set(LAST_USE) == set(LOADS)

ROWS = [[("c_ctx", 8), ("c", 8), ("norm_mix", 16), ("norm_ffn", 16), ("norm_final", 8), ("ssd_norm", 8),
         ("mla_q_norm", 2), ("mla_kv_norm", 1), ("ev_conv_b", 12), ("hy_conv_b", 24)],
        [("b_ada", 96)], [("hy_conv_w", 72)], [("ev_conv_w", 60)]]
PAR = {}
for i, tile in enumerate(ROWS):
    at = 0
    for name, n in tile:
        PAR[name] = i * P + at
        at += n
NROWS = [sum(n for _, n in tile) for tile in ROWS]
PAR["ssd_d"] = 4 * P
assert max(NROWS) <= P

C_ID, C_GT, C_LE, C_LT, C_GE, C_ONE = (i * P for i in range(6))
NCST = 6 * P


def host_constants():
    i = np.arange(P)
    row, col = i[:, None], i[None, :]
    cst = np.concatenate([row == col, row > col, row <= col, row < col, row >= col,
                          np.ones((P, P))], 1).astype(np.float32)

    rev = (8 * (row + col == P - 1)).astype(np.float32)

    def dft(n):
        th = math.pi / n
        a = np.arange(n, dtype=np.float64)
        f = a[:, None] * (a[None, :] + 0.5) * th
        parts = [np.cos(f), -np.sin(f), np.cos(f).T / n, -np.sin(f).T / n]
        return np.stack([x.reshape(n // P, P, n).transpose(1, 0, 2).reshape(P, -1) for x in parts], 1)

    dft_all = np.concatenate([dft(LP).reshape(P, -1), dft(LS).reshape(P, -1)], 1).astype(np.float32)

    def times(n):
        return np.linspace(0.0, 1.0, n)

    def feat(n):
        t = times(n)[:, None]
        w = 2.0 * math.pi * np.arange(n) / n
        bands = np.linspace(1e-4, HY_BANDS - 1, HY_BANDS)
        ang = w[:, None] * bands[None]
        return np.concatenate([t, np.cos(ang), -np.sin(ang)], -1).T

    feats = np.concatenate([feat(LP), feat(LS)], 1).astype(np.float32)
    deltas = np.linspace(abs(math.log(1e-2) / 1.5), abs(math.log(1e-2) / 0.3), D)
    t = np.concatenate([times(LP), times(LS)])
    decay = np.exp(-t[:, None] * deltas).astype(np.float32).reshape(NT, P, D)
    q = np.arange(LS) % GRID_W
    c0 = np.clip(q - WIN_C // 2, 0, GRID_W - WIN_C)
    ok = (q[None, :] >= c0[:, None]) & (q[None, :] < c0[:, None] + WIN_C)
    mask = np.where(ok, 0.0, -8.0 * BIG).astype(np.float32).reshape(2, P, LS)
    nf = ROPE // 4
    inv = 10000.0 ** (-np.arange(nf) / nf)
    pos = np.stack([np.arange(LS) // GRID_W, np.arange(LS) % GRID_W])
    ang = pos[:, None, :] * inv[None, :, None]
    rope = np.stack([np.stack([np.cos(ang), np.cos(ang)], 1), np.stack([-np.sin(ang), np.sin(ang)], 1)])
    rope = rope.reshape(2, ROPE, LS).transpose(1, 0, 2).astype(np.float32)
    slots = np.tile(np.arange(T), (P, 1)).astype(np.float32)
    small = np.concatenate([np.tile(np.arange(E) * CAP, (P, 1)), np.tile(np.arange(ROUNDS) * CAP, (P, 1)),
                            i[:, None] + np.arange(NT)[None] * P, np.tile(8 - np.arange(8), (P, 1)),
                            np.where(i < HY_HID, 1, -1)[:, None], i[:, None] % 32 == np.arange(2)[None]], 1).astype(np.float32)
    return {"k_cst": cst, "k_dft": dft_all, "k_feat": feats, "k_decay": decay, "k_mask": mask, "k_rope": rope,
            "k_slots": slots, "k_small": small, "k_rev": rev}


SWAP = [i ^ (ROPE // 4) for i in range(ROPE)]


def build_kernel(nc, A, K, outs, stop=None):
    with ExitStack() as ctx:
        sems = {}

        def S(name):
            if name not in sems:
                sems[name] = ctx.enter_context(nc.semaphore(name))
            return sems[name]

        def sb(name, shape, dt=F32):
            return ctx.enter_context(nc.sbuf_tensor(name, shape, dt))

        ring = sb("ring", [P, NSLOT * SLOT])
        xT = sb("xT", [P, KD, T])
        hT = sb("hT", [P, KD, T])
        cst = sb("cst", [P, NCST])
        par = sb("par", [P, 4 * P + KD])
        mod = sb("mod", [P, 2, 48, 2])
        gmod = sb("gmod", [P, 4, KD, 2])
        rstdw = sb("rstd", [P, 512])
        rstd = rstdw[:, 0:T]
        scr = sb("scr", [P, 656])
        small = sb("small", [P, E + ROUNDS + NT + PERG + 4])
        sgn, pick, eps = small[:, -4:-3], small[:, -3:-1], small[:, -1:]
        cond = par[:, 2 * P + NROWS[2]:2 * P + NROWS[2] + 2 * KD + 30]
        counti = sb("counti", [P, 1], I32)
        ar = sb("arena", [P, 19712])
        banks = [ctx.enter_context(nc.psum_tensor("bank%d" % i, [P, 512], F32)) for i in range(8)]

        rows_d = [nc.dram_tensor("rows%d" % l, (T, D), F32).ap() for l in range(2)]
        outs_d = [nc.dram_tensor("expert_rows%d" % l, (2 * T, D), F32).ap() for l in range(2)]

        ident = cst[:, C_ID:C_ID + P]
        after, upto = cst[:, C_GT:C_GT + P], cst[:, C_LE:C_LE + P]
        before, since = cst[:, C_LT:C_LT + P], cst[:, C_GE:C_GE + P]
        ones = cst[:, C_ONE:C_ONE + P]

        def area(at, *shape):
            n = int(np.prod(shape))
            assert at + n <= 19712, (at, shape)
            v = ar[:, at:at + n]
            if len(shape) == 2:
                v = v.rearrange("p (a b) -> p a b", a=shape[0])
            if len(shape) == 3:
                v = v.rearrange("p (a b c) -> p a b c", a=shape[0], b=shape[1])
            return v

        prow = area(16000, 4, P)
        d2 = area(16512, 2)
        d8 = area(16514, P)
        xrow = area(8192, NT, D)
        sq_at = {"mix0": 3072, "ssd": 6144, "ffn0": 0, "mix1": 0, "q": 15872, "kv": 16640, "ffn1": 0, "final": 0}
        szT = area(0, KD, T)
        xbcT = area(3072, KX, T)
        xtok = area(7680, NT, D)
        btok = area(10752, NT, 2 * STATE)
        cpad = area(11520, 2, PADDED)
        cacc = area(12304, 2, PADDED - 2 * PAD)
        dtw = area(13200, 8, 96)
        rf, rb = area(11520, 4, P), area(12032, 4, P)
        expE, mdec, m2 = area(12544, 4, P), area(13056, 4, P), area(13568, 4, P)
        ctf, ctb = area(14080, 4, P), area(14592, 4, P)
        cbf, cbb = area(15104, 2, P), area(15360, 2, P)
        sent = area(15616, 4, D)
        xw = area(11520, D)
        stok = area(12544, KD, P)
        stout = area(13568, 4, P)
        dts = scr[:, 0:96].rearrange("p (d t h) -> p d t h", d=2, t=NT)
        dta = scr[:, 96:192].rearrange("p (t d h) -> p t d h", d=2, t=NT)
        wexp = scr[:, 192:384].rearrange("p (t n) -> p t n", t=NT)
        wsc = scr[:, 384:480].rearrange("p (t d h) -> p t d h", d=2, t=NT)
        arow = area(14000, 2, HEADS)
        brow = area(14032, 2, HEADS)
        wdtt = area(14064, KD, HEADS)
        hyT = area(3072, KD, T)
        u0T = area(6144, KD, T)
        p1T = area(9216, KD, T)
        pq = area(12288, 2, 2, 512)
        hh = area(14336, 2, 2, 512)
        hpad = area(12288, 2, PADDED)
        hacc = area(13072, 2, PADDED - 2)
        dft = area(16384, 2560)
        hsP, hsQ = area(18944, T), area(19328, T)
        hview = hT[:, :, :].rearrange("p k t -> p (k t)")
        decay = hview[:, 0:1024].rearrange("p (a b) -> p a b", a=2)
        w3s = hview[:, 1024:1536]
        ut = hview[:, 1536:3072].rearrange("p (a b) -> p a b", a=NT)
        hyb = scr[:, 0:512]
        ytmp = rstdw
        w1t = area(14336, HY_HID)
        w2t = area(14400, P)
        featt = area(14528, T)
        fpar = area(14912, 4)
        farg = area(14916, T)
        fk = area(15300, T)
        h1 = area(15684, T)
        qkT = area(0, 8, T)
        vtok = area(3072, NT, 512)
        kcT = area(4608, 4, P)
        kctok, vctok = area(5120, 512), area(5632, 512)
        ktok = area(6144, 512)
        ncsc = area(7168, 2, T)
        npt = area(7936, 2, T)
        nbias = area(8704, 2, LS)
        nmask = area(9216, 2, LS)
        rope = area(10752, 2, LS)
        latT = area(11264, 4, T)
        wuq = area(12800, 2, AH * QK)
        wukv = area(14336, AH * 2 * AD)
        ckvT = area(15360, 4 * P)
        vm = area(15872, 4, 512)
        sqq = area(sq_at["q"], 2, T)
        rkv = area(17920, T)
        ckto = area(18304, P)
        krto = area(18432, QK)
        ckctok = area(18528, P)
        kr96 = area(18656, QK)
        nrows = area(18752, 2, 4)
        krot = area(18760, LS)
        rev = area(19016, P)
        qmT = area(0, AH, T)
        kmT = area(3072, AH, 512)
        qrot = area(8704, AH * LS)
        oT = hT
        fino = area(4096, NT, D)
        xs = area(0, 2, D)
        xsT = area(2048, 2, D)
        sg, hid, hidT = area(4096, 2, HID), area(4608, 2, HID), area(5120, 2, HID)
        ob = area(5632, 2, D)
        htok = area(7680, NT, D)
        onehot = area(10752, NT, T)
        yg = [area(at, 2, D) for at in (7680, 5632, 0)]
        yc = area(10752, NT, D)
        wr = area(14208, KD, NG + E)
        rbias = area(14500, NG + E)
        slotrow = area(14540, T)
        rmask = area(15000, NT, E)
        rtok = area(15100, 2, NT * E).rearrange("p c (t e) -> p c t e", t=NT)
        rsc = area(15400, 1600)
        rsc_g, rsc_e = rsc[:, 1000:1012], rsc[:, 1020:1023]
        efirst, thr = small[:, 0:E], small[:, E:E + ROUNDS]
        toknum, tie = small[:, E + ROUNDS:E + ROUNDS + NT], small[:, E + ROUNDS + NT:E + ROUNDS + NT + PERG]
        tbli = scr[:, 512:608].bitcast(I32)
        scati = rsc[:, 1100:1196].bitcast(I32)
        idxc = scr[:, 608:612].bitcast(I32)
        ysw = scr[:, 620:626]

        SQ_N = [("mix0", KD), ("ssd", KD), ("ffn0", KD), ("mix1", KD), ("q", 2), ("kv", 1), ("ffn1", KD), ("final", KD)]

        def sq_base(which):
            return sum(n for i, (w, n) in enumerate(SQ_N) if i < [x for x, _ in SQ_N].index(which))

        MODS = ["mix0", "ffn0", "mix1", "ffn1", "final"]
        STOP = JOB[stop] if stop is not None else len(PLAN)
        done = S("pe_done")
        taken = {"act": S("act_took"), "dve": S("dve_took")}

        def full(eng, *name):
            eng.wait_ge(done, JOB[name] + 1)

        def took(eng, *name):
            i = JOB[name]
            if TAKER[i] == "none" and name[0] == "U":
                i += 1
            if TAKER[i] != "none":
                eng.wait_ge(taken[TAKER[i]], RANK[i])

        def bank(*name):
            return banks[JOB[name] % 8]

        class Chain:

            def __init__(self, eng, name):
                self.eng, self.sem, self.n = eng, S(name), 0

            def __call__(self, ins):
                self.n += 1
                ins.then_inc(self.sem, 1)
                self.eng.wait_ge(self.sem, self.n)

        def slot(k):
            return ring[:, (k % NSLOT) * SLOT:(k % NSLOT + 1) * SLOT]

        def block_source(b):
            if b[0] == "ada":
                return A["w_ada"][b[1], :, b[2] * 512:(b[2] + 1) * 512].rearrange("(k p) n -> p k n", p=P)
            if b[0] == "z":
                return A["ev_w_in"][0, :, b[1] * 512:(b[1] + 1) * 512].rearrange("(k p) n -> p k n", p=P)
            if b[0] == "xbc":
                return A["ev_w_in"][0, :, COL_XBC + b[1] * 512:COL_XBC + (b[1] + 1) * 512].rearrange("(k p) n -> p k n", p=P)
            if b[0] == "hy":
                c0 = COL_HY + b[1] * D + b[2] * 512
                return A["ev_w_in"][0, :, c0:c0 + 512].rearrange("(k p) n -> p k n", p=P)
            if b[0] == "wout":
                return A["ev_w_out"][0, :, b[1] * 256:(b[1] + 1) * 256].rearrange("(k p) n -> p k n", p=P)
            if b[0] == "od":
                w = 512 if b[1] < 3 else 416
                return A["od_w_in"][0, :, b[1] * 512:b[1] * 512 + w].rearrange("(k p) n -> p k n", p=P)
            return A["od_w_out"][0, :, b[1] * 512:(b[1] + 1) * 512].rearrange("(k p) n -> p k n", p=P)

        def ada_rows(b):
            return slot(LOAD_AT[("ada",) + b])[:, 0:512]

        def block_view(b):
            s = slot(LOAD_AT[b])
            if b == ("od", 3):
                return s[:, 0:8 * 416].rearrange("p (k n) -> p k n", k=8)
            return s.rearrange("p (k n) -> p k n", k=16 if b[0] == "wout" else 8)

        def expert_slot(n, part):
            return 3 * ((n + 1) % 2) + part

        def pair_view(s):
            return ring[:, s * SLOT:(s + 1) * SLOT].rearrange("p (e k n) -> p e k n", e=2, n=HID)

        def down_view(s):
            return ring[:, s * SLOT:(s + 1) * SLOT].rearrange("p (e k n) -> p e k n", e=2, n=D)

        def trips(eng, l):
            eng.wait_ge(S("trips%d" % l), 1)
            return eng.value_load(counti[0:1, 0:1], min_val=0, max_val=PAIRS // 2 * (ROUNDS - 1)) + PAIRS // 2

        block = ctx.enter_context(nc.Block())

        @block.sync
        def _(sp):
            for t in range(NT):
                src = A["x_prompt"][0] if t == 0 else A["x_sample"][0, (t - 1) * P:t * P, :]
                sp.dma_start(xrow[:, t, :], src).then_inc(S("x_in"), 16)

            def static_load(k, first_after_experts):
                s = k % NSLOT
                if k >= NSLOT and not first_after_experts:
                    sp.wait_ge(done, LAST_USE[LOADS[k - NSLOT]] + 1)
                sp.dma_start(block_view(LOADS[k]), block_source(LOADS[k])).then_inc(S("full%d" % s), 16)

            def pair_loads(l, n, b, first):
                for part, name in enumerate(("moe_w_gate", "moe_w_up", "moe_w_down")):
                    s = expert_slot(b, part)
                    if first:
                        last = max(k for k in range(len(FIRST) if l == 0 else len(LOADS)) if k % NSLOT == s)
                        sp.wait_ge(done, LAST_USE[LOADS[last]] + 1)
                    else:
                        sp.wait_ge(S("gu_done%d" % l) if part < 2 else S("down_done%d" % l), n - 1)
                    pair = n % PAIRS
                    if part < 2:
                        src = A[name][l].rearrange("(q e) (p k) n -> q p e (k n)", e=2, p=P)
                    else:
                        src = A[name][l].rearrange("(q e) (p k) n -> q p e (k n)", e=2, p=P)
                    src = src[pair] if isinstance(pair, int) else src[bass.ds(pair, 1)].rearrange("q p e m -> (q p) e m")
                    dst = ring[:, s * SLOT:(s + 1) * SLOT].rearrange("p (e m) -> p e m", e=2)
                    sp.dma_start(dst, src).then_inc(S("efull%d_%d" % (l, s)), 16)

            def expert_loads(l):
                for n in range(2):
                    pair_loads(l, n, n, True)
                r = trips(sp, l)
                with sp.Fori(1, r) as i:
                    for b in range(2):
                        pair_loads(l, 2 * i + b, b, False)
                return r

            n1 = len(FIRST)
            for k in range(n1):
                if LAST_USE[LOADS[k]] < STOP or k < 3:
                    static_load(k, False)
            if STOP > JOB[("MOE", 0)]:
                r = expert_loads(0)
                for k in range(n1, len(LOADS)):
                    s = k % NSLOT
                    gone = 2 * r - (1 if s >= 3 else 0)
                    sp.wait_ge(S("down_done0") if s % 3 == 2 else S("gu_done0"), gone)
                    if k >= n1 + 3:
                        sp.wait_ge(S("yg%d" % (NT - 1)), 16)
                    static_load(k, True)
                if STOP > JOB[("MOE", 1)]:
                    expert_loads(1)

        @block.tensor
        def _(pe):
            state = {"i": 0}

            def open_bank(*name):
                i = state["i"]
                assert PLAN[i][0] == name, (PLAN[i][0], name)
                state["i"] += 1
                if i >= 8:
                    took(pe, *PLAN[i - 8][0])
                return banks[i % 8]

            def mm(out, lhsT, rhs, start, stop_):
                return nc.tensor.matmul(out, lhsT, rhs, start=start, stop=stop_, skip_group_check=True)

            def tr(out, in_):
                n = in_.shape[0]
                return nc.tensor.transpose(out, in_, ident[0:n, 0:n])

            def arrived(b):
                k = LOAD_AT[b]
                pe.wait_ge(S("full%d" % (k % NSLOT)), 16 * (k // NSLOT + 1))

            def project(name, w, col, rhs, width=T, m=P, k0=KD):
                ps = open_bank(*name)
                for k in range(k0):
                    last = mm(ps[0:m, 0:width], w[:, k, col:col + m], rhs[:, k, 0:width], k == 0, k == k0 - 1)
                last.then_inc(done, 1)

            def ada(l, b0):
                for b in (b0, b0 + 1):
                    ps = open_bank("adaw", l, b)
                    arrived(("ada", l, b))
                    w = block_view(("ada", l, b))
                    for k in range(KD):
                        g = k % 4
                        last = nc.tensor.matmul(ps[32 * g:32 * g + 32, :], cond[:, 2 * k:2 * k + 32],
                                                w[:, k, :], start=k < 4, stop=k >= 4, tile_position=(0, 32 * g),
                                                skip_group_check=True)
                    last.then_inc(done, 1)
                for b in (b0, b0 + 1):
                    ps = open_bank("ada", l, b)
                    took(pe, "adaw", l, b)
                    for m in range(4):
                        last = mm(ps[:, 2 * m:2 * m + 2], ada_rows((l, b))[:, m * P:(m + 1) * P], pick, True, True)
                    last.then_inc(done, 1)

            def ada_after(*name):
                if name in ADA_AFTER:
                    ada(*ADA_AFTER[name])

            def sum_squares(which, src, n):
                ps = open_bank("ss", which)
                for k in range(n):
                    pe.wait_ge(S("sq"), sq_base(which) + k + 1)
                    last = mm(ps[:, 0:T], ones, src[:, k, :], k == 0, k == n - 1)
                last.then_inc(done, 1)

            def mixer_input(i):
                pe.wait_ge(S("hT"), KD * (i + 1))

            pe.wait_ge(S("cst_in"), 16)
            pe.wait_ge(S("rows_in"), 16 * sum(len(t) for t in ROWS))
            for i in range(4):
                ps = open_bank("par", i)
                tr(ps[:, 0:NROWS[i]], prow[0:NROWS[i], i, :]).then_inc(done, 1)
            ps = open_bank("par", 4)
            pe.wait_ge(S("d8"), 1)
            tr(ps[:, 0:KD], d8[0:KD, :]).then_inc(done, 1)
            pe.wait_ge(S("x_in"), 16 * NT)
            for k in range(KD):
                ps = open_bank("xTr", k)
                for t in range(NT):
                    last = tr(ps[:, t * P:(t + 1) * P], xrow[:, t, k * P:(k + 1) * P])
                last.then_inc(done, 1)
            pe.wait_ge(S("silc"), 1)
            pe.wait_ge(S("small_in"), 16)
            for b in (0, 2):
                ada(0, b)
            sum_squares("mix0", area(sq_at["mix0"], KD, T), KD)
            mixer_input(0)
            for c in range(KD):
                if c % 4 == 0:
                    arrived(("z", c // 4))
                project(("z", c), block_view(("z", c // 4)), c % 4 * P, hT)
                ada_after("z", c)
            ps = open_bank("dt")
            pe.wait_ge(S("dtin"), 16 * 3)
            for t in range(NT):
                for k in range(KD):
                    last = mm(ps[:, t * HEADS:(t + 1) * HEADS], hT[:, k, t * P:(t + 1) * P], wdtt[:, k, :], k == 0, k == KD - 1)
            last.then_inc(done, 1)
            for c in range(KX):
                if c % 4 == 0:
                    arrived(("xbc", c // 4))
                project(("xbc", c), block_view(("xbc", c // 4)), c % 4 * P, hT)
                ada_after("xbc", c)
            pe.wait_ge(S("xbc"), KX)
            for t in range(NT):
                for half in range(2):
                    ps = open_bank("xtk", t, half)
                    for c in range(4):
                        last = tr(ps[:, c * P:(c + 1) * P], xbcT[:, half * 4 + c, t * P:(t + 1) * P])
                    last.then_inc(done, 1)
                ps = open_bank("btk", t)
                for g in range(2):
                    last = tr(ps[:, g * P:(g + 1) * P], xbcT[:, KD + g, t * P:(t + 1) * P])
                last.then_inc(done, 1)
            for d in range(2):
                pe.wait_ge(S("sinit_in"), 16 * (d + 1))
                for g in range(2):
                    ps = open_bank("sinit", d, g)
                    for c in range(4):
                        last = tr(ps[:, c * P:(c + 1) * P], stok[:, g * 4 + c, :])
                    last.then_inc(done, 1)
            pe.wait_ge(S("dta"), 1)
            for t in range(NT):
                ps = open_bank("wt", t)
                mm(ps[:, 0:HEADS], after, dta[:, t, 0, :], True, True)
                mm(ps[:, HEADS:2 * HEADS], before, dta[:, t, 1, :], True, True)
                mm(ps[:, 2 * HEADS:4 * HEADS], ones, dta[:, t, :, :].rearrange("p d h -> p (d h)"), True, True).then_inc(done, 1)
            for d in range(2):
                pe.wait_ge(S("xw"), d + 1)
                took(pe, "btk", 0)
                for g in range(2):
                    ps = open_bank("st0", d, g)
                    for c in range(4):
                        last = mm(ps[:, c * P:(c + 1) * P], xw[:, (g * 4 + c) * P:(g * 4 + c + 1) * P], btok[:, 0, g * P:(g + 1) * P], True, True)
                    last.then_inc(done, 1)
            for d in range(2):
                pe.wait_ge(S("xw"), d + 3)
                took(pe, "btk", d + 1)
                for g in range(2):
                    ps = open_bank("st", d, g)
                    mm(ps[:, :], btok[:, d + 1, g * P:(g + 1) * P], xw[:, g * 512:(g + 1) * 512], True, True).then_inc(done, 1)
            step = 0
            for t in range(NT):
                tt = slice(t * P, (t + 1) * P)
                ps = open_bank("cb", t)
                for g in range(2):
                    last = mm(ps[:, g * P:(g + 1) * P], xbcT[:, KD + g, tt], xbcT[:, KD + 2 + g, tt], True, True)
                last.then_inc(done, 1)
                for q in range(4):
                    ps = open_bank("E", t, q)
                    pe.wait_ge(S("rfb"), 2 * (step + 1))
                    mm(ps[:, :], after, rf.rearrange("p h l -> p (h l)"), True, False)
                    mm(ps[:, :], before, rb.rearrange("p h l -> p (h l)"), False, True).then_inc(done, 1)
                    if t:
                        ps = open_bank("cs", t, q, 0)
                        mm(ps[:, :], ones, rf.rearrange("p h l -> p (h l)"), True, True).then_inc(done, 1)
                        ps = open_bank("cs", t, q, 1)
                        mm(ps[:, :], ones, rb.rearrange("p h l -> p (h l)"), True, True).then_inc(done, 1)
                    ps = open_bank("y", t, q)
                    pe.wait_ge(S("mm"), step + 1)
                    if t:
                        pe.wait_ge(S("ctd"), 2 * (4 * (t - 1) + q + 1))
                        took(pe, "st", 1, 1)
                        took(pe, "sinit", 1, 1)
                    for j in range(4):
                        h = 4 * q + j
                        o = ps[(j % 2) * HDIM:(j % 2 + 1) * HDIM, (j // 2) * P:(j // 2 + 1) * P]
                        hp = slice(h * HDIM, (h + 1) * HDIM)
                        last = mm(o, xtok[:, t, hp], mdec[:, j, :], True, t == 0)
                        if t:
                            mm(o, sent[:, t - 1, hp], ctf[:, j, :], False, False)
                            last = mm(o, sent[:, t + 1, hp], ctb[:, j, :], False, True)
                    last.then_inc(done, 1)
                    step += 1
            sum_squares("ssd", area(sq_at["ssd"], KD, T), KD)

            for q in range(3):
                for c in range(KD):
                    if c % 4 == 0:
                        arrived(("hy", q, c // 4))
                    project(("hy", q, c), block_view(("hy", q, c // 4)), c % 4 * P, hT)
                    ada_after("hy", q, c)
            pe.wait_ge(S("hyc_in"), 16 * 11)
            ps = open_bank("f", 0)
            mm(ps[0:HY_HID, 0:T], w1t[0:HY_FEAT, :], featt[0:HY_FEAT, :], True, True).then_inc(done, 1)
            ps = open_bank("f", 1)
            pe.wait_ge(S("fsin"), 1)
            mm(ps[:, 0:T], w2t[0:HY_HID, :], h1[0:HY_HID, :], True, True).then_inc(done, 1)
            pe.wait_ge(S("hs"), 1)
            pe.wait_ge(S("hconv"), 3 * KD)
            for b in range(2):
                for o in range(2):
                    src = u0T if o == 0 else p1T
                    if o == 1:
                        took(pe, "inv", b, 0, 1, 3)
                    for t in range(NT):
                        ps = open_bank("utk", b, o, t)
                        for c in range(4):
                            last = tr(ps[:, c * P:(c + 1) * P], src[:, b * 4 + c, t * P:(t + 1) * P])
                        last.then_inc(done, 1)
                    for s in range(2):
                        nk = s + 1
                        n = nk * P
                        dv = dft[:, 4 * P * s:4 * P * s + 4 * nk * n].rearrange("p (x k n) -> p x k n", x=4, k=nk)
                        pe.wait_ge(S("w3_in"), 32 * (2 * b + o + 1))
                        for x, hs in enumerate((hsP, hsQ)):
                            for t in range(nk):
                                ps = open_bank("PQ", b, o, s, x, t)
                                mm(ps[:, :], hs[:, (s + t) * P:(s + t + 1) * P], w3s, True, True).then_inc(done, 1)
                        for x in range(2):
                            took(pe, "PQ", b, o, s, x, nk - 1)
                        for k in range(nk):
                            for x in range(2):
                                ps = open_bank("H", b, o, s, k, x)
                                for t in range(nk):
                                    last = mm(ps[:, :], dv[:, x, t, k * P:(k + 1) * P], pq[:, x, t, :], t == 0, t == nk - 1)
                                last.then_inc(done, 1)
                        for t in range(nk):
                            took(pe, "utk", b, o, s + t)
                        for k in range(nk):
                            for x in range(2):
                                ps = open_bank("U", b, o, s, k, x)
                                for t in range(nk):
                                    last = mm(ps[:, :], dv[:, x, t, k * P:(k + 1) * P], ut[:, s + t, :], t == 0, t == nk - 1)
                                last.then_inc(done, 1)
                        pe.wait_ge(S("spec"), 3 * (2 * b + o) + (3 if s else 1))
                        for c in range(4):
                            ps = open_bank("inv", b, o, s, c)
                            for x in range(2):
                                for k in range(nk):
                                    last = mm(ps[:, 0:n], pq[:, x, k, c * P:(c + 1) * P], dv[:, 2 + x, k, :],
                                              x == 0 and k == 0, x == 1 and k == nk - 1)
                            last.then_inc(done, 1)
            took(pe, "inv", 1, 1, 1, 3)
            pe.wait_ge(S("yn"), KD)
            for m in range(KD):
                if m % 2 == 0:
                    arrived(("wout", m // 2))
                w = block_view(("wout", m // 2))
                ps = open_bank("wout", m)
                for k in range(2 * KD):
                    rhs = szT[:, k, :] if k < KD else hyT[:, k - KD, :]
                    last = mm(ps[:, 0:T], w[:, k, m % 2 * P:(m % 2 + 1) * P], rhs, k == 0, k == 2 * KD - 1)
                last.then_inc(done, 1)

            def moe(l):
                sum_squares("ffn%d" % l, area(sq_at["ffn%d" % l], KD, T), KD)
                mixer_input(1 + 2 * l)
                ps = open_bank("rt", l)
                pe.wait_ge(S("router_in%d" % l), 16 * 5)
                for t in range(NT):
                    for k in range(KD):
                        last = mm(ps[:, t * 40:t * 40 + NG + E], hT[:, k, t * P:(t + 1) * P], wr[:, k, :], k == 0, k == KD - 1)
                last.then_inc(done, 1)
                for t in range(NT):
                    for h in range(2):
                        ps = open_bank("htk", l, t, h)
                        for c in range(4):
                            last = tr(ps[:, c * P:(c + 1) * P], hT[:, h * 4 + c, t * P:(t + 1) * P])
                        last.then_inc(done, 1)
                ps = open_bank("pos", l)
                pe.wait_ge(S("chosen"), l + 1)
                for t in range(NT):
                    for u in range(t):
                        mm(ps[:, t * E:(t + 1) * E], ones, rmask[:, u, :], u == 0, False)
                    mm(ps[:, t * E:(t + 1) * E], before, rmask[:, t, :], t == 0, True)
                for t in range(NT):
                    last = mm(ps[:, NT * E:(NT + 1) * E], ones, rmask[:, t, :], t == 0, t == NT - 1)
                last.then_inc(done, 1)
                ps = open_bank("tbl", l)
                for c in range(2):
                    pe.wait_ge(S("onehot"), 2 * l + c + 1)
                    for r in range(ROUNDS):
                        for par_ in range(2):
                            for t in range(NT):
                                o = ps[par_ * CAP:(par_ + 1) * CAP, c * 96 + r * PAIRS:c * 96 + (r + 1) * PAIRS]
                                rhs = rtok[:, c, t, :].rearrange("p (q e) -> p e q", e=2)[:, par_, :]
                                last = mm(o, onehot[:, t, r * CAP:(r + 1) * CAP], rhs, t == 0, t == NT - 1)
                    if c == 0:
                        last.then_inc(S("tbl0"), 1)
                last.then_inc(done, 1)
                assert PLAN[state["i"]][0] == ("MOE", l)
                if STOP <= JOB[("MOE", l)]:
                    raise StopIteration
                for j in range(state["i"] - 8, state["i"]):
                    took(pe, *PLAN[j][0])
                state["i"] += 1
                r = trips(pe, l)
                s = {x: S("%s%d" % (x, l)) for x in
                     ("x_ps", "x_act", "x_dve", "gu_done", "hid", "ht_done", "ht_act", "down_done", "d_act", "d_dve")}

                def turn(n, b):
                    pe.wait_ge(S("gather%d_%d" % (l, b)), 16 * ((n - b) // 2 + 1) if isinstance(n, int) else 8 * (n - b) + 16)
                    if not (isinstance(n, int) and n == 0):
                        pe.wait_ge(s["x_act"], n)
                        pe.wait_ge(s["x_dve"], n)
                    v = xs[:, b, :].rearrange("p (m k) -> p k m", k=KD)
                    for k in range(KD):
                        last = tr(banks[k // 4][:, (k % 4) * P:(k % 4 + 1) * P], v[:, k, :])
                    last.then_inc(s["x_ps"], 1)

                def gate_up(n, b):
                    fills = 16 * ((n - b) // 2 + 1) if isinstance(n, int) else 8 * (n - b) + 16
                    for part in range(2):
                        pe.wait_ge(S("efull%d_%d" % (l, expert_slot(b, part))), fills)
                    pe.wait_ge(s["x_act"], n + 1)
                    pe.wait_ge(s["x_dve"], n + 1)
                    if not (isinstance(n, int) and n < 2):
                        pe.wait_ge(s["hid"], n - 1)
                    x = xsT[:, b, :].rearrange("p (k m) -> p k m", k=KD)
                    s0 = expert_slot(b, 0)
                    w = ring[:, s0 * SLOT:(s0 + 2) * SLOT].rearrange("p (x e k n) -> p e k x n", x=2, e=2, n=HID)
                    for k in range(KD):
                        for e in range(2):
                            o = banks[2 + b][e * CAP:(e + 1) * CAP, :].rearrange("p (x n) -> p x n", x=2)
                            last = mm(o, x[:, k, e * CAP:(e + 1) * CAP], w[:, e, k, :, :], k == 0, k == KD - 1)
                    last.then_inc(s["gu_done"], 1)

                def turn_hidden(n, b):
                    pe.wait_ge(s["hid"], n + 1)
                    v = hid[:, b, :].rearrange("p (m k) -> p k m", k=2)
                    for k in range(2):
                        last = tr(banks[4][:, k * P:(k + 1) * P], v[:, k, :])
                    last.then_inc(s["ht_done"], 1)

                def down(n, b):
                    fills = 16 * ((n - b) // 2 + 1) if isinstance(n, int) else 8 * (n - b) + 16
                    pe.wait_ge(S("efull%d_%d" % (l, expert_slot(b, 2))), fills)
                    pe.wait_ge(s["ht_act"], n + 1)
                    if not (isinstance(n, int) and n == 0):
                        pe.wait_ge(s["d_act"], n)
                        pe.wait_ge(s["d_dve"], n)
                    w = down_view(expert_slot(b, 2))
                    x = hidT[:, b, :].rearrange("p (k m) -> p k m", k=2)
                    for half in range(2):
                        for k in range(2):
                            for e in range(2):
                                last = mm(banks[5 + half][e * CAP:(e + 1) * CAP, :], x[:, k, e * CAP:(e + 1) * CAP],
                                          w[:, e, k, half * 512:(half + 1) * 512], k == 0, k == 1)
                    last.then_inc(s["down_done"], 1)

                turn(0, 0)
                gate_up(0, 0)
                turn(1, 1)
                turn_hidden(0, 0)
                with pe.Fori(0, r - 1) as i:
                    for b in range(2):
                        n = 2 * i + 1 + b
                        gate_up(n, 1 - b)
                        down(n - 1, b)
                        turn(n + 1, b)
                        turn_hidden(n, 1 - b)
                n = 2 * r - 1
                gate_up(n, 1)
                down(n - 1, 0)
                turn_hidden(n, 1)
                down(n, 1)
                for x in ("x_act", "x_dve", "ht_act", "d_act", "d_dve", "hid"):
                    pe.wait_ge(s[x], 2 * r)
                pe.sem_inc(done, 1)
                for k in range(KD):
                    ps = open_bank("yTr", l, k)
                    pe.wait_ge(S("yc"), NT * (l + 1))
                    for t in range(NT):
                        last = tr(ps[:, t * P:(t + 1) * P], yc[:, t, k * P:(k + 1) * P])
                    last.then_inc(done, 1)

            try:
                moe(0)
                if STOP <= JOB[("ss", "mix1")]:
                    raise StopIteration
                sum_squares("mix1", area(sq_at["mix1"], KD, T), KD)
                mixer_input(2)
                for c in range(8):
                    if c % 4 == 0:
                        arrived(("od", c // 4))
                    project(("qk", c), block_view(("od", c // 4)), c % 4 * P, hT)
                arrived(("od", 2))
                for t in range(NT):
                    ps = open_bank("v", t)
                    w = block_view(("od", 2))
                    for k in range(KD):
                        last = mm(ps[:, :], hT[:, k, t * P:(t + 1) * P], w[:, k, :], k == 0, k == KD - 1)
                    last.then_inc(done, 1)
                arrived(("od", 3))
                for c in range(3):
                    project(("lat", c), block_view(("od", 3)), c * P, hT)
                project(("lat", 3), block_view(("od", 3)), QR + P - AD, hT, m=QK)
                ps = open_bank("ktok")
                took(pe, "lat", 3)
                for c in range(4):
                    last = tr(ps[:, c * P:(c + 1) * P], qkT[:, 4 + c, 0:P])
                last.then_inc(done, 1)
                ps = open_bank("kctx")
                pe.wait_ge(S("nactx_in"), 16 * 5)
                for c in range(4):
                    last = tr(ps[:, c * P:(c + 1) * P], kctok[:, c * P:(c + 1) * P])
                last.then_inc(done, 1)
                took(pe, "kctx")
                def heads(kind, scores, values, first):
                    scores(*TURNS[0])
                    for n, (i, h) in enumerate(TURNS):
                        if n + 1 < len(TURNS):
                            scores(*TURNS[n + 1])
                        hp = slice((h % 2) * AD, (h % 2 + 1) * AD)
                        nk = 1 if i == "p" else 3
                        b = n % 2
                        ps = open_bank(kind + "t", i, h)
                        pe.wait_ge(S("prob"), first + n + 1)
                        for j in range(nk):
                            last = tr(ps[:, j * P:(j + 1) * P], ncsc[:, b, j * P:(j + 1) * P])
                        last.then_inc(done, 1)
                        ps = open_bank(kind + "o", i, h)
                        took(pe, kind + "t", i, h)
                        for j in range(nk):
                            last = mm(ps[hp, 0:P], values(i, h, j), npt[:, b, j * P:(j + 1) * P], j == 0, j == nk - 1)
                        last.then_inc(done, 1)

                def na_values(i, h, j):
                    if j == 2:
                        return vctok[:, h * AD:(h + 1) * AD]
                    return vtok[:, j if i == "p" else 1 + j, h * AD:(h + 1) * AD]

                def na_scores(i, h):
                        hp = slice((h % 2) * AD, (h % 2 + 1) * AD)
                        ps = open_bank("na", i, h)
                        q0 = 0 if i == "p" else LP + i * P
                        q = qkT[hp, h // 2, q0:q0 + P]
                        nk = 1 if i == "p" else 3
                        if i == "p":
                            last = mm(ps[:, 0:P], q, qkT[hp, 4 + h // 2, 0:P], True, True)
                        else:
                            mm(ps[:, 0:LS], q, qkT[hp, 4 + h // 2, LP:T], True, False)
                            pe.wait_ge(S("nbias%d" % i), 32 * (h + 1))
                            mm(ps[:, 0:LS], rev, nbias[:, i, :], False, True)
                            last = mm(ps[:, LS:T], q, kcT[hp, h // 2, :], True, True)
                        last.then_inc(done, 1)
                heads("na", na_scores, na_values, 0)
                sum_squares("q", sqq, 2)
                ps = open_bank("ss", "kv")
                pe.wait_ge(S("sq"), sq_base("kv") + 1)
                mm(ps[:, 0:T], ones, area(sq_at["kv"], T), True, True).then_inc(done, 1)
                ps = open_bank("mctx")
                pe.wait_ge(S("mctx_in"), 16 * 2)
                pe.wait_ge(S("kr0"), 1)
                tr(ps[:, 0:P], ckctok)
                tr(ps[0:QK, P:2 * P], kr96).then_inc(done, 1)
                ps = open_bank("ckvtok")
                pe.wait_ge(S("ckvn"), 1)
                tr(ps[:, 0:P], ckvT[:, 0:P])
                tr(ps[:, P:P + QK], latT[0:QK, 3, 0:P]).then_inc(done, 1)
                took(pe, "mctx")
                pe.wait_ge(S("qn"), 2)
                pe.wait_ge(S("wmla_in"), 16 * 2)
                for h in range(AH):
                    ps = open_bank("qm", h)
                    for k in range(2):
                        last = mm(ps[0:QK, 0:T], wuq[:, k, h * QK:(h + 1) * QK], latT[:, k, :], k == 0, k == 1)
                    last.then_inc(done, 1)
                    ps = open_bank("km", h)
                    mm(ps[0:AD, :], wukv[:, h * 2 * AD:h * 2 * AD + AD], ckvT, True, True).then_inc(done, 1)
                for t in range(4):
                    ps = open_bank("vm", t)
                    rhs = wukv.rearrange("p (h c) -> p h c", h=AH)[:, :, AD:2 * AD]
                    mm(ps[:, :].rearrange("p (h c) -> p h c", h=AH), ckvT[:, t * P:(t + 1) * P], rhs, True, True).then_inc(done, 1)
                pe.wait_ge(S("roped"), 2)
                took(pe, "km", AH - 1)
                took(pe, "qm", AH - 1)
                took(pe, "vm", 3)

                def ml_scores(i, h):
                    ps = open_bank("ml", i, h)
                    q0 = 0 if i == "p" else LP + i * P
                    nk = 1 if i == "p" else 3
                    keys = kmT[0:QK, h, 0:P] if i == "p" else kmT[0:QK, h, P:4 * P]
                    mm(ps[:, 0:nk * P], qmT[0:QK, h, q0:q0 + P], keys, True, True).then_inc(done, 1)

                def ml_values(i, h, j):
                    return vm[:, j if i == "p" else 1 + j, h * AD:(h + 1) * AD]

                heads("ml", ml_scores, ml_values, len(TURNS))
                took(pe, "mlo", 1, AH - 1)
                for m in range(KD):
                    if m % 4 == 0:
                        arrived(("odout", m // 4))
                    project(("odout", m), block_view(("odout", m // 4)), m % 4 * P, oT)
                moe(1)
                sum_squares("final", area(sq_at["final"], KD, T), KD)
                pe.wait_ge(S("fin"), KD)
                for t in range(NT):
                    for h in range(2):
                        ps = open_bank("out", t, h)
                        for c in range(4):
                            last = tr(ps[:, c * P:(c + 1) * P], hT[:, h * 4 + c, t * P:(t + 1) * P])
                        last.then_inc(done, 1)
            except StopIteration:
                pass

        @block.scalar
        def _(act):
            A_ = nc.scalar.activation

            act.dma_start(cst[:, :], K["k_cst"]).then_inc(S("cst_in"), 16)
            for i, tile in enumerate(ROWS):
                at = 0
                for name, n in tile:
                    src = A[name]
                    if len(src.shape) == 1:
                        src = src.rearrange("(r p) -> r p", p=P)
                    elif len(src.shape) == 2:
                        src = src.rearrange("a (r p) -> (a r) p", p=P)
                    else:
                        src = src.rearrange("a b (r p) -> (a b r) p", p=P)
                    act.dma_start(prow[at:at + n, i, :], src).then_inc(S("rows_in"), 16)
                    at += n

            def seg_add(out, in_, bias):
                for v, (a, b) in enumerate(SEGS):
                    last = A_(out[:, a:b], in_[:, a:b], ACT.Identity, bias=bias[:, v:v + 1])
                return last

            def root(which, width):
                full(act, "ss", which)
                A_(rstd, bank("ss", which)[:, 0:T], ACT.Sqrt, bias=eps[:, 0:1], scale=1.0 / width).then_inc(taken["act"], 1)

            def squares(which, src, n):
                dst = area(sq_at[which], n, T)
                for k in range(n):
                    A_(dst[:, k, :], src[:, k, :], ACT.Square).then_inc(S("sq"), 1)

            def shift(i, layer, chunk0):
                src = area(sq_at[MODS[i]], KD, T)
                for k in range(KD):
                    act.wait_ge(S("nrm"), KD * i + k + 1)
                    seg_add(hT[:, k, :], src[:, k, :], mod[:, layer, chunk0 + k, :]).then_inc(S("hT"), 1)

            def ada(l, b0):
                for b in (b0, b0 + 1):
                    full(act, "adaw", l, b)
                    A_(ada_rows((l, b)), bank("adaw", l, b)[:, :], ACT.Copy).then_inc(taken["act"], 1)

            def ada_after(*name):
                if name in ADA_AFTER:
                    ada(*ADA_AFTER[name])

            for i in range(4):
                full(act, "par", i)
                A_(par[:, i * P:i * P + NROWS[i]], bank("par", i)[:, 0:NROWS[i]], ACT.Copy).then_inc(taken["act"], 1)
            full(act, "par", 4)
            A_(par[:, PAR["ssd_d"]:PAR["ssd_d"] + KD], bank("par", 4)[:, 0:KD], ACT.Copy).then_inc(taken["act"], 1)
            took(act, "par", 4)
            act.wait_ge(S("const"), 1)
            A_(cond[:, 0:2 * KD].rearrange("p (k v) -> p v k", v=2), par[:, 0:2 * KD].rearrange("p (v k) -> p v k", v=2),
               ACT.Silu).then_inc(S("silc"), 1)
            for k in range(KD):
                full(act, "xTr", k)
                A_(xT[:, k, :], bank("xTr", k)[:, 0:T], ACT.Copy).then_inc(taken["act"], 1)
            took(act, "xTr", KD - 1)
            squares("mix0", xT, KD)
            for b in (0, 2):
                ada(0, b)
            root("mix0", D)
            took(act, "ada", 0, 3)
            shift(0, 0, 0)
            for c in range(KD):
                full(act, "z", c)
                A_(szT[:, c, :], bank("z", c)[:, 0:T], ACT.Silu).then_inc(taken["act"], 1)
                ada_after("z", c)
            act.wait_ge(S("dt_abs"), 1)
            A_(dtw[:, 1, :], dtw[:, 1, :], ACT.Exp).then_inc(S("dt_exp"), 1)
            act.wait_ge(S("dt_one"), 1)
            A_(dtw[:, 3, :], dtw[:, 2, :], ACT.Ln).then_inc(S("dt_ln"), 1)
            act.wait_ge(S("dtin"), 16 * 3)
            A_(arow, arow, ACT.Exp).then_inc(S("dt_ln"), 1)
            for c in range(KX + 1):
                if c < KX:
                    if c >= 2:
                        act.wait_ge(S("conv"), c - 1)
                    full(act, "xbc", c)
                    ps = bank("xbc", c)
                    A_(cpad[:, c % 2, PAD:PAD + LP], ps[:, 0:LP], ACT.Copy)
                    A_(cpad[:, c % 2, 2 * PAD + LP:2 * PAD + T], ps[:, LP:T], ACT.Copy).then_inc(taken["act"], 1)
                    ada_after("xbc", c)
                if c:
                    act.wait_ge(S("conv"), c)
                    A_(xbcT[:, c - 1, 0:LP], cacc[:, (c - 1) % 2, 0:LP], ACT.Silu)
                    A_(xbcT[:, c - 1, LP:T], cacc[:, (c - 1) % 2, LP + PAD:T + PAD], ACT.Silu).then_inc(S("xbc"), 1)
            for t in range(NT):
                for half in range(2):
                    full(act, "xtk", t, half)
                    A_(xtok[:, t, half * 512:(half + 1) * 512], bank("xtk", t, half)[:, :], ACT.Copy).then_inc(taken["act"], 1)
                full(act, "btk", t)
                A_(btok[:, t, :], bank("btk", t)[:, 0:2 * STATE], ACT.Copy).then_inc(taken["act"], 1)
            for d in range(2):
                for g in range(2):
                    full(act, "sinit", d, g)
                    A_(sent[:, 3 * d, g * 512:(g + 1) * 512], bank("sinit", d, g)[:, :], ACT.Copy).then_inc(taken["act"], 1)
            for t in range(NT):
                full(act, "wt", t)
                A_(wexp[:, t, :], bank("wt", t)[:, 0:64], ACT.Exp).then_inc(taken["act"], 1)
            for d in range(2):
                for g in range(2):
                    full(act, "st0", d, g)
                    n = 2 * d + g
                    if n:
                        act.wait_ge(S("state_out"), 16 * n)
                    A_(stout, bank("st0", d, g)[:, :].rearrange("p (c n) -> p c n", c=4), ACT.Copy).then_inc(taken["act"], 1)
                    took(act, "st0", d, g)
                    act.dma_start(outs[2][0, 0, d, g * 8:(g + 1) * 8].rearrange("(c h) q n -> (h q) c n", h=2), stout)\
                       .then_inc(S("state_out"), 16)
            act.wait_ge(S("state_out"), 64)
            took(act, "st", 1, 1)
            step = 0
            for t in range(NT):
                for q in range(4):
                    full(act, "E", t, q)
                    if step:
                        act.wait_ge(S("mm"), step)
                    A_(expE.rearrange("p h l -> p (h l)"), bank("E", t, q)[:, :], ACT.Exp).then_inc(taken["act"], 1)
                    if t:
                        if step > 4:
                            full(act, "y", *divmod(step - 1, 4))
                        for d, ct in enumerate((ctf, ctb)):
                            full(act, "cs", t, q, d)
                            A_(ct.rearrange("p h l -> p (h l)"), bank("cs", t, q, d)[:, :], ACT.Exp).then_inc(taken["act"], 1)
                    step += 1
            act.wait_ge(S("yz"), 12)
            for k in range(KD):
                A_(area(sq_at["ssd"], KD, T)[:, k, :], szT[:, k, :], ACT.Square).then_inc(S("sq"), 1)
            root("ssd", D)
            for c in range(3 * KD):
                if c == 0:
                    act.wait_ge(S("hpad0"), 1)
                if c >= 2:
                    act.wait_ge(S("hconv"), c - 1)
                full(act, "hy", c // KD, c % KD)
                ps = bank("hy", c // KD, c % KD)
                A_(hpad[:, c % 2, 1:1 + LP], ps[:, 0:LP], ACT.Copy)
                A_(hpad[:, c % 2, 2 + LP:2 + T], ps[:, LP:T], ACT.Copy).then_inc(taken["act"], 1)
                ada_after("hy", c // KD, c % KD)
            for i in range(2):
                act.wait_ge(S("farg"), i + 1)
                dst = h1[0:HY_HID, :] if i == 0 else hsP
                src = farg[0:HY_HID, :] if i == 0 else farg
                A_(dst, src, ACT.Sin).then_inc(S("fsin"), 1)
            for b in range(2):
                for o in range(2):
                    for t in range(NT):
                        full(act, "utk", b, o, t)
                        if (b, o) != (0, 0):
                            pb, po = (b, 0) if o else (0, 1)
                            full(act, "U", pb, po, 1, 1, 1)
                        A_(ut[:, t, :], bank("utk", b, o, t)[:, :], ACT.Copy).then_inc(taken["act"], 1)
                    for s in range(2):
                        for k in range(s + 1):
                            full(act, "H", b, o, s, k, 1)
                            if (b, o, s) != (0, 0, 0):
                                act.wait_ge(S("spec"), 3 * (2 * b + o) + s)
                            A_(hh[:, 1, k, :], bank("H", b, o, s, k, 1)[:, :], ACT.Copy).then_inc(taken["act"], 1)

            def moe(l):
                took(act, "wout" if l == 0 else "odout", KD - 1)
                squares("ffn%d" % l, xT, KD)
                root("ffn%d" % l, D)
                took(act, "ada", l, 11)
                shift(1 + 2 * l, l, 24)
                for t in range(NT):
                    for h in range(2):
                        full(act, "htk", l, t, h)
                        A_(htok[:, t, h * 512:(h + 1) * 512], bank("htk", l, t, h)[:, :], ACT.Copy).then_inc(taken["act"], 1)
                    took(act, "htk", l, t, 1)
                    act.dma_start(rows_d[l][t * P:(t + 1) * P, :], htok[:, t, :]).then_inc(S("rows_out"), 16)
                act.wait_ge(S("gl"), l + 1)
                A_(rsc_g, rsc_g, ACT.Exp).then_inc(S("ge"), 1)
                act.wait_ge(S("el"), l + 1)
                A_(rsc_e, rsc_e, ACT.Exp).then_inc(S("ee"), 1)
                if STOP <= JOB[("MOE", l)]:
                    return
                r = trips(act, l)
                s = {x: S("%s%d" % (x, l)) for x in
                     ("x_ps", "x_act", "x_dve", "gu_done", "silu", "hid", "ht_done", "ht_act", "down_done", "d_act", "d_dve")}

                def take_rows(n, b):
                    act.wait_ge(s["x_ps"], n + 1)
                    A_(xsT[:, b, 0:512], banks[0][:, :], ACT.Copy).then_inc(s["x_act"], 1)

                def take_gate(n, b):
                    act.wait_ge(s["gu_done"], n + 1)
                    if not (isinstance(n, int) and n < 2):
                        act.wait_ge(s["hid"], n - 1)
                    A_(sg[:, b, :], banks[2 + b][:, 0:HID], ACT.Silu).then_inc(s["silu"], 1)

                def take_hidden(n, b):
                    act.wait_ge(s["ht_done"], n + 1)
                    if not (isinstance(n, int) and n < 2):
                        act.wait_ge(s["down_done"], n - 1)
                    A_(hidT[:, b, :], banks[4][:, 0:HID], ACT.Copy).then_inc(s["ht_act"], 1)

                def take_down(n, b, stored):
                    act.wait_ge(s["down_done"], n + 1)
                    act.wait_ge(S("stored%d_%d" % (l, b)), stored)
                    A_(ob[:, b, 0:512], banks[5][:, :], ACT.Copy).then_inc(s["d_act"], 1)

                take_rows(0, 0)
                take_gate(0, 0)
                take_rows(1, 1)
                take_hidden(0, 0)
                with act.Fori(0, r - 1) as i:
                    for b in range(2):
                        n = 2 * i + 1 + b
                        take_gate(n, 1 - b)
                        take_down(n - 1, b, 16 * i)
                        take_rows(n + 1, b)
                        take_hidden(n, 1 - b)
                n = 2 * r - 1
                take_gate(n, 1)
                take_down(n - 1, 0, 16 * (r - 1))
                take_hidden(n, 1)
                take_down(n, 1, 16 * (r - 1))

            if STOP > JOB[("ss", "ffn0")]:
                moe(0)
            if STOP > JOB[("ss", "mix1")]:
                took(act, "yTr", 0, KD - 1)
                squares("mix1", xT, KD)
                root("mix1", D)
                took(act, "ada", 1, 11)
                shift(2, 1, 0)
                for c in range(8):
                    full(act, "qk", c)
                    A_(qkT[:, c, :], bank("qk", c)[:, 0:T], ACT.Copy).then_inc(taken["act"], 1)
                for t in range(NT):
                    full(act, "v", t)
                    A_(vtok[:, t, :], bank("v", t)[:, :], ACT.Copy).then_inc(taken["act"], 1)
                for c in range(4):
                    m = QK if c == 3 else P
                    full(act, "lat", c)
                    A_(latT[0:m, c, :], bank("lat", c)[0:m, 0:T], ACT.Copy).then_inc(taken["act"], 1)
                full(act, "ktok")
                A_(ktok, bank("ktok")[:, :], ACT.Copy).then_inc(taken["act"], 1)
                full(act, "kctx")
                A_(kcT[:, :, :], bank("kctx")[:, :].rearrange("p (c n) -> p c n", c=4), ACT.Copy).then_inc(taken["act"], 1)
                took(act, "kctx")
                act.dma_start(outs[3][0, 0].rearrange("h t c -> t h c"), ktok.rearrange("p (h c) -> p h c", h=AH)).then_inc(S("cache_out"), 16)
                act.dma_start(outs[4][0, 0].rearrange("h t c -> t h c"), vtok[:, 0, :].rearrange("p (h c) -> p h c", h=AH)).then_inc(S("cache_out"), 16)

                def heads(kind, scale, chunk0, first):
                    def exps(n):
                        b = n % 2
                        nk = 1 if TURNS[n][0] == "p" else 3
                        act.wait_ge(S("negm"), first + n + 1)
                        A_(ncsc[:, b, 0:nk * P], ncsc[:, b, 0:nk * P], ACT.Exp, bias=nrows[:, b, 0:1], scale=scale,
                           accum_out=nrows[:, b, 1:2]).then_inc(S("expd"), 1)

                    exps(0)
                    for n, (i, h) in enumerate(TURNS):
                        if n + 1 < len(TURNS):
                            exps(n + 1)
                        b = n % 2
                        nk = 1 if i == "p" else 3
                        full(act, kind + "t", i, h)
                        if n >= 2:
                            full(act, kind + "o", *TURNS[n - 2])
                        A_(npt[:, b, 0:nk * P], bank(kind + "t", i, h)[:, 0:nk * P], ACT.Copy).then_inc(taken["act"], 1)
                        full(act, kind + "o", i, h)
                        hp = slice((h % 2) * AD, (h % 2 + 1) * AD)
                        q0 = 0 if i == "p" else LP + i * P
                        A_(oT[hp, chunk0 + h // 2, q0:q0 + P], bank(kind + "o", i, h)[hp, 0:P], ACT.Copy).then_inc(taken["act"], 1)

                heads("na", AD ** -0.5, 0, 0)
                act.wait_ge(S("cache_out"), 32)
                squares("q", latT, 2)
                A_(area(sq_at["kv"], T), latT[:, 2, :], ACT.Square).then_inc(S("sq"), 1)
                root("q", QR)
                full(act, "ss", "kv")
                A_(rkv, bank("ss", "kv")[:, 0:T], ACT.Sqrt, bias=eps[:, 0:1], scale=1.0 / P).then_inc(taken["act"], 1)
                full(act, "mctx")
                A_(ckvT[:, T:T + P], bank("mctx")[:, 0:P], ACT.Copy)
                for h in range(AH):
                    last = A_(kmT[AD:QK, h, T:T + P], bank("mctx")[AD:QK, P:2 * P], ACT.Copy)
                last.then_inc(taken["act"], 1)
                full(act, "ckvtok")
                A_(ckto, bank("ckvtok")[:, 0:P], ACT.Copy)
                A_(krto, bank("ckvtok")[:, P:P + QK], ACT.Copy).then_inc(taken["act"], 1)
                took(act, "ckvtok")
                act.dma_start(outs[5][0, 0], ckto).then_inc(S("cache_out"), 16)
                act.dma_start(outs[6][0, 0], krto[:, AD:QK]).then_inc(S("cache_out"), 16)
                for h in range(AH):
                    full(act, "qm", h)
                    A_(qmT[0:QK, h, :], bank("qm", h)[0:QK, 0:T], ACT.Copy).then_inc(taken["act"], 1)
                    full(act, "km", h)
                    A_(kmT[0:AD, h, :], bank("km", h)[0:AD, :], ACT.Copy).then_inc(taken["act"], 1)
                for t in range(4):
                    full(act, "vm", t)
                    A_(vm[:, t, :], bank("vm", t)[:, :], ACT.Copy).then_inc(taken["act"], 1)
                heads("ml", QK ** -0.5, 4, len(TURNS))
                moe(1)
                if STOP > JOB[("ss", "final")]:
                    took(act, "yTr", 1, KD - 1)
                    squares("final", xT, KD)
                    root("final", D)
                    for t in range(NT):
                        for h in range(2):
                            full(act, "out", t, h)
                            A_(fino[:, t, h * 512:(h + 1) * 512], bank("out", t, h)[:, :], ACT.Copy).then_inc(taken["act"], 1)
                        took(act, "out", t, 1)
                        dst = outs[0][0] if t == 0 else outs[1][0, (t - 1) * P:t * P, :]
                        act.dma_start(dst, fino[:, t, :]).then_inc(S("y_out"), 16)
                    act.wait_ge(S("y_out"), 16 * NT)
                    act.wait_ge(S("cache_out"), 64)

        @block.vector
        def _(dve):
            TT, TS, STT = nc.vector.tensor_tensor, nc.vector.tensor_scalar, nc.vector.scalar_tensor_tensor
            COPY, RED = nc.vector.tensor_copy, nc.vector.tensor_reduce
            link = Chain(dve, "dve_chain")
            mult, add, sub = ALU.mult, ALU.add, ALU.subtract

            def col(name, i):
                return par[:, PAR[name] + i:PAR[name] + i + 1]

            def take(ins):
                ins.then_inc(taken["dve"], 1)

            def over(ap, n, last=True):
                if last:
                    return ap.unsqueeze(len(ap.shape)).to_broadcast(list(ap.shape) + [n])
                return ap.unsqueeze(1).to_broadcast([ap.shape[0], n] + list(ap.shape[1:]))

            def ada(l, b0):
                for b in (b0, b0 + 1):
                    full(dve, "ada", l, b)
                    bias = par[:, PAR["b_ada"] + l * 48 + 4 * b:PAR["b_ada"] + l * 48 + 4 * b + 4]
                    take(TT(mod[:, l, 4 * b:4 * b + 4, :], bank("ada", l, b)[:, 0:8].rearrange("p (m v) -> p m v", v=2),
                            over(bias, 2), add))

            def ada_after(*name):
                if name in ADA_AFTER:
                    ada(*ADA_AFTER[name])

            def gain(i, l, name, chunk0, last_block):
                took(dve, "ada", l, last_block)
                g = par[:, PAR[name] + l * KD:PAR[name] + (l + 1) * KD]
                link(STT(out=gmod[:, i, :, :], in0=mod[:, l, chunk0:chunk0 + KD, :], scalar=1.0, in1=over(g, 2),
                         op0=add, op1=mult))

            def norm(i):
                which = MODS[i]
                took(dve, "ss", which)
                link(nc.vector.reciprocal(rstd, rstd))
                dst = area(sq_at[which], KD, T)
                for k in range(KD):
                    for v, (a, b) in enumerate(SEGS):
                        last = STT(out=dst[:, k, a:b], in0=xT[:, k, a:b], scalar=gmod[:, i, k, v:v + 1], in1=rstd[:, a:b],
                                   op0=mult, op1=mult)
                    last.then_inc(S("nrm"), 1)

            def add_gated(name, l, chunk0):
                for m in range(KD):
                    full(dve, *name, m)
                    for v, (a, b) in enumerate(SEGS):
                        last = STT(out=xT[:, m, a:b], in0=bank(*name, m)[:, a:b], scalar=mod[:, l, chunk0 + m, v:v + 1],
                                   in1=xT[:, m, a:b], op0=mult, op1=add)
                    take(last)

            nc.vector.memset(eps[:, :], EPS)
            nc.vector.memset(cond[:, 2 * KD:], 0.0)
            nc.vector.memset(cpad, 0.0).then_inc(S("const"), 1)
            dve.wait_ge(S("d2_in"), 16)
            COPY(d8[0:KD, :].rearrange("c (h r) -> c h r", h=2), over(d2[0:KD, :], HDIM)).then_inc(S("d8"), 1)
            took(dve, "par", 3)
            dve.wait_ge(S("small_in"), 16)
            for b in (0, 2):
                ada(0, b)
            gain(0, 0, "norm_mix", 8, 3)
            norm(0)
            for c in range(KD):
                ada_after("z", c)
            full(dve, "dt")
            dve.wait_ge(S("dtin"), 16 * 3)
            dps = bank("dt")[:, 0:NT * HEADS].rearrange("p (t h) -> p t h", t=NT)
            for d in range(2):
                last = TT(dtw[:, 0, d * 48:(d + 1) * 48].rearrange("p (t h) -> p t h", t=NT), dps, over(brow[:, d, :], NT, False), add)
            take(last)
            took(dve, "dt")
            STT(out=dtw[:, 1, :], in0=dtw[:, 0, :], scalar=-1.0, in1=dtw[:, 0, :], op0=mult, op1=ALU.min).then_inc(S("dt_abs"), 1)
            dve.wait_ge(S("dt_exp"), 1)
            TS(dtw[:, 2, :], dtw[:, 1, :], 1.0, None, add).then_inc(S("dt_one"), 1)
            dve.wait_ge(S("dt_one"), 1)
            link(TS(dtw[:, 4, :], dtw[:, 2, :], -1.0, None, add))
            link(TT(dtw[:, 5, :], dtw[:, 1, :], dtw[:, 4, :], sub))
            dve.wait_ge(S("dt_ln"), 2)
            link(TT(dtw[:, 5, :], dtw[:, 5, :], dtw[:, 3, :], add))
            link(STT(out=dts.rearrange("p d t h -> p (d t h)"), in0=dtw[:, 0, :], scalar=0.0, in1=dtw[:, 5, :], op0=ALU.max, op1=add))
            for d in range(2):
                last = STT(out=dta[:, :, d, :], in0=dts[:, d, :, :], scalar=-1.0, in1=over(arow[:, d, :], NT, False), op0=mult, op1=mult)
            last.then_inc(S("dta"), 1)
            n = T + PAD
            for c in range(KX):
                took(dve, "xbc", c)
                if c >= 2:
                    dve.wait_ge(S("xbc"), c - 1)
                src, acc = cpad[:, c % 2, :], cacc[:, c % 2, 0:n]
                link(TS(acc, src[:, 0:n], col("ev_conv_w", c), col("ev_conv_b", c), mult, add))
                for k in range(1, TAPS):
                    last = STT(out=acc, in0=src[:, k:k + n], scalar=col("ev_conv_w", k * KX + c), in1=acc, op0=mult, op1=add)
                    if k < TAPS - 1:
                        link(last)
                last.then_inc(S("conv"), 1)
                ada_after("xbc", c)
            for t in range(NT):
                took(dve, "wt", t)
                for d in range(2):
                    last = TT(wsc[:, t, d, :], wexp[:, t, d * HEADS:(d + 1) * HEADS], dts[:, d, t, :], mult)
                link(last)
            for i, (t, d) in enumerate(((0, 0), (0, 1), (1, 0), (2, 1))):
                if i:
                    full(dve, *(("st0", i - 1, 1) if i < 3 else ("st", 0, 1)))
                TT(xw.rearrange("p (h c) -> p h c", h=HEADS), xtok[:, t, :].rearrange("p (h c) -> p h c", h=HEADS),
                   over(wsc[:, t, d, :], HDIM), mult).then_inc(S("xw"), 1)
                if i < 2:
                    continue
                d = i - 2
                src, dst, t = ((0, 1, 1), (3, 2, 2))[d]
                took(dve, "sinit", d, 1)
                for g in range(2):
                    gs = slice(g * 512, (g + 1) * 512)
                    tot = wexp[:, t, 32 + d * HEADS + g * 8:32 + d * HEADS + g * 8 + 8]
                    link(TT(sent[:, dst, gs].rearrange("p (h c) -> p h c", h=8), sent[:, src, gs].rearrange("p (h c) -> p h c", h=8),
                            over(tot, HDIM), mult))
                for g in range(2):
                    gs = slice(g * 512, (g + 1) * 512)
                    full(dve, "st", d, g)
                    take(TT(sent[:, dst, gs], sent[:, dst, gs], bank("st", d, g)[:, :], add))
            took(dve, "st", 1, 1)
            dve.wait_ge(S("state_out"), 64)
            step = 0
            for t in range(NT):
                tt = slice(t * P, (t + 1) * P)
                full(dve, "cb", t)
                cps = bank("cb", t)[:, 0:2 * P].rearrange("p (g l) -> p g l", g=2)
                TT(cbf, cps, over(upto, 2, False), mult)
                take(TT(cbb, cps, over(since, 2, False), mult))
                took(dve, "cb", t)
                for q in range(4):
                    hs = slice(4 * q, 4 * q + 4)
                    TT(mdec, over(cbf[:, q // 2, :], 4, False), over(dts[:, 0, t, hs], P), mult)
                    link(TT(m2, over(cbb[:, q // 2, :], 4, False), over(dts[:, 1, t, hs], P), mult))
                    link(TT(mdec, mdec, m2, add))
                    took(dve, "E", t, q)
                    TT(mdec, mdec, expE, mult).then_inc(S("mm"), 1)
                    if t:
                        for d, ct in enumerate((ctf, ctb)):
                            took(dve, "cs", t, q, d)
                            TT(ct, ct, over(xbcT[:, KD + 2 + q // 2, tt], 4, False), mult).then_inc(S("ctd"), 1)
                    full(dve, "y", t, q)
                    for j in range(2):
                        last = STT(out=m2[:, j, :], in0=xbcT[:, 2 * q + j, tt], scalar=par[:, PAR["ssd_d"] + 2 * q + j:PAR["ssd_d"] + 2 * q + j + 1],
                                   in1=bank("y", t, q)[:, j * P:(j + 1) * P], op0=mult, op1=add)
                    take(last)
                    took(dve, "y", t, q)
                    TT(szT[:, 2 * q:2 * q + 2, tt], szT[:, 2 * q:2 * q + 2, tt], m2[:, 0:2, :], mult).then_inc(S("yz"), 1)
                    step += 1
                    dve.wait_ge(S("yz"), step)
            took(dve, "ss", "ssd")
            link(nc.vector.reciprocal(rstd, rstd))
            for k in range(KD):
                STT(out=szT[:, k, :], in0=szT[:, k, :], scalar=col("ssd_norm", k), in1=rstd, op0=mult, op1=mult).then_inc(S("yn"), 1)
            nc.vector.memset(hpad, 0.0).then_inc(S("hpad0"), 1)
            n = T + 1
            for c in range(3 * KD):
                q, k = divmod(c, KD)
                took(dve, "hy", q, k)
                src, acc = hpad[:, c % 2, :], hacc[:, c % 2, 0:n]
                dst = (u0T, p1T, hyT)[q][:, k, :]
                link(TS(acc, src[:, 0:n], col("hy_conv_w", c), col("hy_conv_b", c), mult, add))
                link(STT(out=acc, in0=src[:, 1:1 + n], scalar=col("hy_conv_w", 3 * KD + c), in1=acc, op0=mult, op1=add))
                for v, (a, b) in enumerate(SEGS):
                    last = STT(out=dst[:, a:b], in0=src[:, 2 + a + v:2 + b + v], scalar=col("hy_conv_w", 6 * KD + c),
                               in1=acc[:, a + v:b + v], op0=mult, op1=add)
                last.then_inc(S("hconv"), 1)
                ada_after("hy", q, k)
            two_pi_hi = float(np.float32(6.28125))
            two_pi_lo = 2.0 * math.pi - two_pi_hi
            magic = 12582912.0
            for i in range(2):
                m = HY_HID if i == 0 else P
                a, k = farg[0:m, :], fk[0:m, :]
                full(dve, "f", i)
                if i:
                    dve.wait_ge(S("fsin"), 1)
                dve.wait_ge(S("hyc_in"), 16 * 11)
                take(TS(a, bank("f", i)[0:m, 0:T], fpar[0:m, 2 * i:2 * i + 1], fpar[0:m, 2 * i + 1:2 * i + 2], add, mult))
                took(dve, "f", i)
                link(TS(k, a, 1.0 / (2.0 * math.pi), magic, mult, add))
                link(TS(k, k, -magic, None, add))
                link(STT(out=a, in0=k, scalar=-two_pi_hi, in1=a, op0=mult, op1=add))
                link(STT(out=a, in0=k, scalar=-two_pi_lo, in1=a, op0=mult, op1=add))
                TS(a, a, 3.1415925, -3.1415925, ALU.min, ALU.max).then_inc(S("farg"), 1)
            dve.wait_ge(S("fsin"), 2)
            nc.vector.memset(hsP[HY_HID:P, 0:1], 0.0)
            link(nc.vector.memset(hsP[HY_HID:P, LP:LP + 1], 0.0))
            TS(hsQ, hsP, sgn[:, 0:1], None, mult).then_inc(S("hs"), 1)
            loads = 0
            for b in range(2):
                for o in range(2):
                    for s in range(2):
                        nk = s + 1
                        n = nk * P
                        loads += 1
                        dve.wait_ge(S("dec_in"), 16 * loads)
                        for x in range(2):
                            for t in range(nk):
                                full(dve, "PQ", b, o, s, x, t)
                                if x == 0 and t == 0 and loads > 1:
                                    ps_, pb, po = (0, b, o) if s else (1, b - (o == 0), 1 - o)
                                    full(dve, "inv", pb, po, ps_, 3)
                                take(TT(pq[:, x, t, :], bank("PQ", b, o, s, x, t)[:, :], decay[:, t, :], mult))
                        dve.wait_ge(S("hyb_in"), 16 * (2 * b + o + 1))
                        for k in range(nk):
                            full(dve, "H", b, o, s, k, 0)
                            take(TT(hh[:, 0, k, :], bank("H", b, o, s, k, 0)[:, :], hyb, add))
                        for k in range(nk):
                            took(dve, "H", b, o, s, k, 0)
                            took(dve, "H", b, o, s, k, 1)
                            full(dve, "U", b, o, s, nk - 1, 1)
                            ure, uim = bank("U", b, o, s, k, 0)[:, :], bank("U", b, o, s, k, 1)[:, :]
                            TT(pq[:, 0, k, :], ure, hh[:, 0, k, :], mult)
                            link(TT(ytmp[:, :], uim, hh[:, 1, k, :], mult))
                            TT(pq[:, 0, k, :], pq[:, 0, k, :], ytmp[:, :], sub)
                            link(TT(pq[:, 1, k, :], ure, hh[:, 1, k, :], mult))
                            take(TT(ytmp[:, :], uim, hh[:, 0, k, :], mult))
                            took(dve, "U", b, o, s, k, 1)
                            TT(pq[:, 1, k, :], pq[:, 1, k, :], ytmp[:, :], add).then_inc(S("spec"), 1)
                            dve.wait_ge(S("spec"), 3 * (2 * b + o) + s + k + 1)
                        a0, a1 = SEGS[s]
                        for c in range(4):
                            full(dve, "inv", b, o, s, c)
                            dst = (p1T if o == 0 else hyT)[:, b * 4 + c, a0:a1]
                            take(TT(dst, dst, bank("inv", b, o, s, c)[:, 0:n], mult))
            add_gated(("wout",), 0, 16)

            def first_of(out, values, top, n):
                v = rsc[:, 1200:1200 + NT * n].rearrange("p (t n) -> p t n", t=NT)
                m = rsc[:, 1300:1300 + NT]
                link(TT(v, values, over(top, n), ALU.is_ge))
                link(TT(v, v, over(tie[:, 0:n], NT, False), mult))
                link(RED(m, v, AX_X, ALU.max))
                link(TT(out, v, over(m, n), ALU.is_equal))

            def moe(l):
                gain(1 + 2 * l, l, "norm_ffn", 32, 11)
                norm(1 + 2 * l)
                full(dve, "rt", l)
                lg = rsc[:, 0:108].rearrange("p (t n) -> p t n", t=NT)
                gl, el = lg[:, :, 0:NG], lg[:, :, NG:NG + E]
                go = rsc[:, 120:132].rearrange("p (t g) -> p t g", t=NT)
                gm_, gs_, m1, m2_, w_ = (rsc[:, 140 + 4 * i:140 + 4 * i + NT] for i in range(5))
                dve.wait_ge(S("router_in%d" % l), 16 * 5)
                rps = bank("rt", l)[:, 0:120].rearrange("p (t n) -> p t n", t=NT)[:, :, 0:NG + E]
                take(TT(lg, rps, over(rbias, NT, False), add))
                took(dve, "rt", l)
                link(RED(gm_, gl, AX_X, ALU.max))
                TT(rsc_g.rearrange("p (t g) -> p t g", t=NT), gl, over(gm_, NG), sub).then_inc(S("gl"), 1)
                first_of(go, gl, gm_, NG)
                pr = rsc[:, 200:296].rearrange("p (t g j) -> p t g j", t=NT, g=NG)
                for t in range(NT):
                    last = TT(pr[:, t], el[:, t, :].rearrange("p (g j) -> p g j", g=NG), over(go[:, t, :], PERG), mult)
                link(last)
                es = rsc[:, 300:324].rearrange("p (t j) -> p t j", t=NT)
                o1 = rsc[:, 330:354].rearrange("p (t j) -> p t j", t=NT)
                o2 = rsc[:, 360:384].rearrange("p (t j) -> p t j", t=NT)
                e2 = rsc[:, 390:414].rearrange("p (t j) -> p t j", t=NT)
                link(RED(es, pr.rearrange("p t g j -> p t j g"), AX_X, add))
                link(RED(m1, es, AX_X, ALU.max))
                first_of(o1, es, m1, PERG)
                link(STT(out=e2, in0=o1, scalar=-BIG, in1=es, op0=mult, op1=add))
                link(RED(m2_, e2, AX_X, ALU.max))
                TT(rsc_e, m2_, m1, sub).then_inc(S("el"), 1)
                first_of(o2, e2, m2_, PERG)
                ohs = rsc[:, 420:612].rearrange("p (c t e) -> p c t e", c=2, t=NT)
                for c, o in enumerate((o1, o2)):
                    for t in range(NT):
                        last = TT(ohs[:, c, t, :].rearrange("p (g j) -> p g j", g=NG), over(go[:, t, :], PERG),
                                  over(o[:, t, :], NG, False), mult)
                link(last)
                TT(rmask, ohs[:, 0], ohs[:, 1], add).then_inc(S("chosen"), 1)
                for c in range(2):
                    last = STT(out=rtok[:, c], in0=over(toknum, E), scalar=float(1 + T * c), in1=ohs[:, c], op0=add, op1=mult)
                link(last)
                dve.wait_ge(S("ge"), l + 1)
                link(RED(gs_, rsc_g.rearrange("p (t g) -> p t g", t=NT), AX_X, add))
                dve.wait_ge(S("ee"), l + 1)
                link(TS(w_, rsc_e, 1.0, None, add))
                link(TT(w_, w_, gs_, mult))
                link(nc.vector.reciprocal(ysw[:, 0:NT], w_))
                link(TT(ysw[:, NT:2 * NT], ysw[:, 0:NT], rsc_e, mult))
                full(dve, "pos", l)
                pps = bank("pos", l)[:, 0:NT * E].rearrange("p (t e) -> p t e", t=NT)
                pp = rsc[:, 620:812].rearrange("p (c t e) -> p c t e", c=2, t=NT)
                posn = rsc[:, 820:826]
                cm, cmp_ = rsc[:, 860:861], rsc[:, 862:868]
                link(RED(cm, bank("pos", l)[:, NT * E:(NT + 1) * E], AX_X, ALU.max))
                for c in range(2):
                    last = TT(pp[:, c], pps, ohs[:, c], mult)
                take(last)
                took(dve, "pos", l)
                link(TS(cmp_, thr, cm, float(PAIRS // 2), ALU.is_lt, mult))
                link(RED(cm, cmp_[:, 1:ROUNDS], AX_X, add))
                COPY(counti[:, :], cm).then_inc(S("trips%d" % l), 1)
                link(RED(posn.rearrange("p (c t) -> p c t", c=2), pp, AX_X, add))
                for c in range(2):
                    if c:
                        dve.wait_ge(S("tbl0"), l + 1)
                    for t in range(NT):
                        last = TS(onehot[:, t, :], slotrow, posn[:, c * NT + t:c * NT + t + 1], None, ALU.is_equal)
                    last.then_inc(S("onehot"), 1)
                full(dve, "tbl", l)
                tb = rsc[:, 900:996]
                link(COPY(tb, bank("tbl", l)[:, 0:96]))
                take(TT(tb, tb, bank("tbl", l)[:, 96:192], add))
                took(dve, "tbl", l)
                empty, sf = rsc[:, 1200:1296], rsc[:, 1300:1396]
                link(TS(empty, tb, 0.0, 4096.0, ALU.is_equal, mult))
                link(STT(out=sf, in0=tb, scalar=-1.0, in1=empty, op0=add, op1=add))
                COPY(scati, sf)
                link(TS(empty, tb, float(T + 1), -float(T), ALU.is_ge, mult))
                link(TT(sf, sf, empty, add))
                COPY(tbli, sf).then_inc(S("table"), 1)
                if STOP <= JOB[("MOE", l)]:
                    return
                r = trips(dve, l)
                s = {x: S("%s%d" % (x, l)) for x in
                     ("x_ps", "x_act", "x_dve", "gu_done", "silu", "hid", "ht_done", "ht_act", "down_done", "d_act", "d_dve")}

                def take_rows(n, b):
                    dve.wait_ge(s["x_ps"], n + 1)
                    COPY(xsT[:, b, 512:1024], banks[1][:, :]).then_inc(s["x_dve"], 1)

                def take_up(n, b):
                    dve.wait_ge(s["silu"], n + 1)
                    if not (isinstance(n, int) and n < 2):
                        dve.wait_ge(s["ht_done"], n - 1)
                    TT(hid[:, b, :], sg[:, b, :], banks[2 + b][:, HID:2 * HID], mult).then_inc(s["hid"], 1)

                def take_down(n, b, stored):
                    dve.wait_ge(s["down_done"], n + 1)
                    dve.wait_ge(S("stored%d_%d" % (l, b)), stored)
                    COPY(ob[:, b, 512:1024], banks[6][:, :]).then_inc(s["d_dve"], 1)

                take_rows(0, 0)
                take_up(0, 0)
                take_rows(1, 1)
                with dve.Fori(0, r - 1) as i:
                    for b in range(2):
                        n = 2 * i + 1 + b
                        take_up(n, 1 - b)
                        take_down(n - 1, b, 16 * i)
                        take_rows(n + 1, b)
                n = 2 * r - 1
                take_up(n, 1)
                take_down(n - 1, 0, 16 * (r - 1))
                take_down(n, 1, 16 * (r - 1))
                for t in range(NT):
                    dve.wait_ge(S("yg%d" % t), 16 * (l + 1))
                    link(TS(yc[:, t, :], yg[t][:, 0, :], ysw[:, t:t + 1], None, mult))
                    STT(out=yc[:, t, :], in0=yg[t][:, 1, :], scalar=ysw[:, NT + t:NT + t + 1], in1=yc[:, t, :], op0=mult, op1=add)\
                        .then_inc(S("yc"), 1)
                add_gated(("yTr", l), l, 40)

            def heads(kind, scale, first):
                def scores(n):
                    i, h = TURNS[n]
                    b = n % 2
                    nk = 1 if i == "p" else 3
                    full(dve, kind, i, h)
                    if n >= 2:
                        full(dve, kind + "t", *TURNS[n - 2])
                    ps = bank(kind, i, h)
                    if kind == "na" and i != "p":
                        TT(ncsc[:, b, 0:LS], ps[:, 0:LS], nmask[:, i, :], add)
                        take(COPY(ncsc[:, b, LS:T], ps[:, LS:T]))
                    else:
                        take(COPY(ncsc[:, b, 0:nk * P], ps[:, 0:nk * P]))
                    took(dve, kind, i, h)
                    link(RED(nrows[:, b, 2:3], ncsc[:, b, 0:nk * P], AX_X, ALU.max))
                    TS(nrows[:, b, 0:1], nrows[:, b, 2:3], -scale, None, mult).then_inc(S("negm"), 1)

                def normalise(n):
                    b = n % 2
                    nk = 1 if TURNS[n][0] == "p" else 3
                    dve.wait_ge(S("expd"), first + n + 1)
                    link(nc.vector.reciprocal(nrows[:, b, 3:4], nrows[:, b, 1:2]))
                    TS(ncsc[:, b, 0:nk * P], ncsc[:, b, 0:nk * P], nrows[:, b, 3:4], None, mult).then_inc(S("prob"), 1)

                scores(0)
                for n in range(len(TURNS)):
                    if n + 1 < len(TURNS):
                        scores(n + 1)
                    normalise(n)

            if STOP > JOB[("ss", "ffn0")]:
                moe(0)
            if STOP > JOB[("ss", "mix1")]:
                gain(2, 1, "norm_mix", 8, 11)
                norm(2)
                dve.wait_ge(S("nactx_in"), 16 * 5)
                heads("na", AD ** -0.5, 0)
                took(dve, "lat", 3)
                took(dve, "nao", 1, AH - 1)
                cos, sin = rope[AD:QK, 0, :], rope[AD:QK, 1, :]
                kr = latT[AD:QK, 3, LP:T]
                link(nc.vector.stream_shuffle(krot[AD:QK, :], kr, SWAP))
                TT(krot[AD:QK, :], krot[AD:QK, :], sin, mult)
                link(TT(kr, kr, cos, mult))
                link(TT(kr, kr, krot[AD:QK, :], add))
                full(dve, "nao", 1, AH - 1)
                dve.wait_ge(S("cache_out"), 32)
                COPY(kmT[AD:QK, :, 0:T], over(latT[AD:QK, 3, :], AH, False)).then_inc(S("roped"), 1)
                took(dve, "ss", "q")
                link(nc.vector.reciprocal(rstd, rstd))
                for k in range(2):
                    STT(out=latT[:, k, :], in0=latT[:, k, :], scalar=col("mla_q_norm", k), in1=rstd, op0=mult, op1=mult).then_inc(S("qn"), 1)
                took(dve, "ss", "kv")
                link(nc.vector.reciprocal(rkv, rkv))
                STT(out=ckvT[:, 0:T], in0=latT[:, 2, :], scalar=col("mla_kv_norm", 0), in1=rkv, op0=mult, op1=mult).then_inc(S("ckvn"), 1)
                took(dve, "qm", AH - 1)
                qr = qmT[AD:QK, :, LP:T]
                qrv = qrot[AD:QK, :].rearrange("p (h n) -> p h n", h=AH)
                for h in range(AH):
                    last = nc.vector.stream_shuffle(qrv[:, h, :], qr[:, h, :], SWAP)
                link(last)
                TT(qrv, qrv, over(sin, AH, False), mult)
                link(TT(qr, qr, over(cos, AH, False), mult))
                TT(qr, qr, qrv, add).then_inc(S("roped"), 1)
                heads("ml", QK ** -0.5, len(TURNS))
                add_gated(("odout",), 1, 16)
                moe(1)
                if STOP > JOB[("ss", "final")]:
                    took(dve, "ss", "final")
                    link(nc.vector.reciprocal(rstd, rstd))
                    for k in range(KD):
                        STT(out=hT[:, k, :], in0=xT[:, k, :], scalar=col("norm_final", k), in1=rstd, op0=mult, op1=mult).then_inc(S("fin"), 1)

        @block.gpsimd
        def _(pool):
            dma = pool.dma_start
            with nc.allow_non_contiguous_dma(reason="a few small parameters"):
                dma(d2[0:KD, :], A["ssd_d"][0].rearrange("(c h) -> c h", h=2)).then_inc(S("d2_in"), 16)
            dma(wdtt, A["ev_w_in"][0, :, COL_DT:COL_DT + HEADS].rearrange("(k p) n -> p k n", p=P)).then_inc(S("dtin"), 16)
            dma(brow, A["ssd_dt_bias"][0].partition_broadcast(P)).then_inc(S("dtin"), 16)
            dma(arow, A["ssd_A_log"][0].partition_broadcast(P)).then_inc(S("dtin"), 16)
            dma(small[:, 0:-1], K["k_small"]).then_inc(S("small_in"), 16)
            for d in range(2):
                pool.wait_ge(S("xbc"), KX)
                pool.wait_ge(S("dta"), 1)
                if d:
                    full(pool, "sinit", 0, 1)
                dma(stok, A["state_ssd"][0, 0, d].rearrange("(c h) q n -> (h q) c n", h=2)).then_inc(S("sinit_in"), 16)
            full(pool, "st", 1, 1)
            step = 0
            for t in range(NT):
                for q in range(4):
                    if step:
                        pt, pq_ = divmod(step - 1, 4)
                        full(pool, *(("cs", pt, pq_, 1) if pt else ("E", pt, pq_)))
                    for d, (dst, m) in enumerate(((rf, upto), (rb, since))):
                        nc.gpsimd.tensor_tensor(dst, m.unsqueeze(1).to_broadcast([P, 4, P]),
                                                dta[:, t, d, 4 * q:4 * q + 4].unsqueeze(2).to_broadcast([P, 4, P]), ALU.mult)\
                            .then_inc(S("rfb"), 1)
                    step += 1
            full(pool, "y", 2, 3)
            with nc.allow_non_contiguous_dma(reason="a few small parameters"):
                dma(dft, K["k_dft"]).then_inc(S("hyc_in"), 16)
                dma(w1t[0:HY_FEAT, :], A["hy_w1"][0]).then_inc(S("hyc_in"), 16)
                dma(featt[0:HY_FEAT, :], K["k_feat"]).then_inc(S("hyc_in"), 16)
                for j in range(2):
                    dma(w2t[0:HY_HID, j * HY_HID:(j + 1) * HY_HID], A["hy_w2"][0]).then_inc(S("hyc_in"), 16)
                for src, c, n in ((A["hy_b1"][0], 0, 1), (A["hy_freq"][0, 0], 1, 1), (A["hy_b2"][0], 2, 2), (A["hy_freq"][0, 1], 3, 2)):
                    for j in range(n):
                        dma(fpar[j * HY_HID:(j + 1) * HY_HID, c:c + 1], src.rearrange("(p o) -> p o", o=1)).then_inc(S("hyc_in"), 16)
            full(pool, "hy", 2, KD - 1)
            last_load = None
            for b in range(2):
                for o in range(2):
                    if last_load is not None:
                        full(pool, "PQ", *last_load, 1, 1, 1)
                        took(pool, "H", *last_load, 1, 1, 0)
                    cs = slice(b * 512, (b + 1) * 512)
                    w3 = A["hy_w3"][0].rearrange("a (o d n) -> a o d n", o=2, d=2)
                    for j in range(2):
                        dma(w3s[j * HY_HID:(j + 1) * HY_HID, :], w3[:, o, j, cs]).then_inc(S("w3_in"), 16)
                    dma(hyb, A["hy_bias"][0, o, cs].partition_broadcast(P)).then_inc(S("hyb_in"), 16)
                    for s in range(2):
                        if s:
                            took(pool, "PQ", b, o, 0, 1, 0)
                        elif last_load is not None:
                            took(pool, "PQ", *last_load, 1, 1, 1)
                        src = K["k_decay"][0:1, :, cs] if s == 0 else K["k_decay"][1:3, :, cs]
                        dma(decay[:, 0:s + 1, :], src.rearrange("t p n -> p t n")).then_inc(S("dec_in"), 16)
                    last_load = (b, o)

            def moe(l):
                took(pool, *(("inv", 1, 1, 1, 3) if l == 0 else ("mlo", 1, AH - 1)))
                full(pool, "inv", 1, 1, 1, 3)
                sem = S("router_in%d" % l)
                dma(wr[:, :, 0:NG], A["moe_w_gr"][l].rearrange("(k p) n -> p k n", p=P)).then_inc(sem, 16)
                dma(wr[:, :, NG:NG + E], A["moe_w_er"][l].rearrange("(k p) n -> p k n", p=P)).then_inc(sem, 16)
                dma(rbias[:, 0:NG], A["moe_b_gr"][l].partition_broadcast(P)).then_inc(sem, 16)
                dma(rbias[:, NG:NG + E], A["moe_b_er"][l].partition_broadcast(P)).then_inc(sem, 16)
                dma(slotrow, K["k_slots"]).then_inc(sem, 16)
                if STOP <= JOB[("MOE", l)]:
                    return

                pool.wait_ge(S("table"), l + 1)
                nc.gpsimd.memset(xs, 0.0).then_inc(S("xs0"), 1)
                pool.wait_ge(S("xs0"), l + 1)

                def gather(n, b):
                    if not (isinstance(n, int) and n < 2):
                        pool.wait_ge(S("x_ps%d" % l), n - 1)
                    pool.wait_ge(S("table"), l + 1)
                    at = tbli[:, n:n + 1] if isinstance(n, int) else tbli[:, bass.ds(n, 1)]
                    need = pool.to_reg(n + 1)
                    nc.gpsimd.tensor_copy(idxc[:, b:b + 1], at).then_inc(S("idx%d" % l), 1)
                    pool.wait_ge(S("rows_out"), 16 * NT * (l + 1))
                    pool.wait_ge(S("idx%d" % l), need)
                    nc.gpsimd.indirect_dma_start(xs[:, b, :], None, rows_d[l], bass.IndirectOffsetOnAxis(ap=idxc[:, b:b + 1], axis=0),
                                                 bounds_check=T - 1, oob_is_err=False)\
                        .then_inc(S("gather%d_%d" % (l, b)), 16)

                def scatter(n, b):
                    for who in ("d_act", "d_dve"):
                        pool.wait_ge(S("%s%d" % (who, l)), n + 1)
                    pool.wait_ge(S("table"), l + 1)
                    need = pool.to_reg(n + 1)
                    nc.gpsimd.tensor_copy(idxc[:, 2 + b:3 + b], scati[:, bass.ds(n, 1)]).then_inc(S("sidx%d" % l), 1)
                    pool.wait_ge(S("rows_out"), 16 * NT * (l + 1))
                    pool.wait_ge(S("sidx%d" % l), need)
                    nc.gpsimd.indirect_dma_start(outs_d[l], bass.IndirectOffsetOnAxis(ap=idxc[:, 2 + b:3 + b], axis=0), ob[:, b, :], None,
                                                 bounds_check=2 * T - 1, oob_is_err=False)\
                        .then_inc(S("stored%d_%d" % (l, b)), 16)

                for n in range(4):
                    gather(n, n % 2)
                r = trips(pool, l)
                with pool.Fori(0, r - 2) as i:
                    for b in range(2):
                        scatter(2 * i + b, b)
                        gather(2 * i + b + 4, b)
                for n in range(4):
                    scatter(2 * r - 4 + n, n % 2)
                need = pool.to_reg(16 * r)
                pool.wait_ge(S("table"), l + 1)
                for b in range(2):
                    pool.wait_ge(S("stored%d_%d" % (l, b)), need)
                src = outs_d[l].rearrange("(c t p) n -> t p c n", c=2, p=P)
                for t in range(NT):
                    dma(yg[t], src[t]).then_inc(S("yg%d" % t), 16)

            if STOP > JOB[("ss", "ffn0")]:
                moe(0)
            if STOP > JOB[("ss", "mix1")]:
                full(pool, "yTr", 0, KD - 1)
                dma(kctok.rearrange("p (h c) -> p h c", h=AH), A["cache_na_k"][0, 0].rearrange("h t c -> t h c")).then_inc(S("nactx_in"), 16)
                dma(vctok.rearrange("p (h c) -> p h c", h=AH), A["cache_na_v"][0, 0].rearrange("h t c -> t h c")).then_inc(S("nactx_in"), 16)
                dma(nmask, K["k_mask"].rearrange("i p n -> p i n")).then_inc(S("nactx_in"), 16)
                dma(rope[AD:QK, :, :], K["k_rope"]).then_inc(S("nactx_in"), 16)
                dma(rev, K["k_rev"]).then_inc(S("nactx_in"), 16)

                def bias_load(i, h):
                    tab = A["na_rel_bias"]
                    for pr_ in range(2):
                        base = h * 465 + (6 - 2 * i + pr_) * 31 - (GRID_W - WIN_C)
                        src = bass.AP(tab.tensor, base, [[1, GRID_W], [31, LS // GRID_W], [1, GRID_W]])
                        dst = nbias[pr_ * GRID_W:(pr_ + 1) * GRID_W, i, :].rearrange("p (a c) -> p a c", a=LS // GRID_W)
                        dma(dst, src).then_inc(S("nbias%d" % i), 16)

                bias_load(0, 0)
                bias_load(1, 0)
                nc.gpsimd.memset(kr96[:, 0:AD], 0.0).then_inc(S("kr0"), 1)
                dma(ckctok, A["cache_mla_ckv"][0, 0]).then_inc(S("mctx_in"), 16)
                dma(kr96[:, AD:QK], A["cache_mla_krope"][0, 0]).then_inc(S("mctx_in"), 16)
                dma(wuq, A["mla_w_uq"][0].rearrange("(k p) n -> p k n", p=P)).then_inc(S("wmla_in"), 16)
                dma(wukv, A["mla_w_ukv"][0]).then_inc(S("wmla_in"), 16)
                for h in range(1, AH):
                    for i in range(2):
                        full(pool, "na", i, h - 1)
                        bias_load(i, h)
                moe(1)


_INS = ['x_prompt', 'x_sample', 'state_ssd', 'cache_na_k', 'cache_na_v', 'cache_mla_ckv', 'cache_mla_krope', 'c', 'c_ctx',
        'w_ada', 'b_ada', 'norm_mix', 'norm_ffn', 'norm_final', 'ev_w_in', 'ev_conv_w', 'ev_conv_b', 'ssd_A_log',
        'ssd_dt_bias', 'ssd_d', 'ssd_norm', 'hy_conv_w', 'hy_conv_b', 'hy_w1', 'hy_b1', 'hy_w2', 'hy_b2', 'hy_w3',
        'hy_freq', 'hy_bias', 'ev_w_out', 'od_w_in', 'mla_q_norm', 'mla_w_uq', 'mla_kv_norm', 'mla_w_ukv',
        'na_rel_bias', 'od_w_out', 'moe_w_gr', 'moe_b_gr', 'moe_w_er', 'moe_b_er', 'moe_w_gate', 'moe_w_up', 'moe_w_down']
_OUTS = [(1, LP, D), (1, LS, D), (1, 1, 2, HEADS, HDIM, STATE), (1, 1, AH, LP, AD), (1, 1, AH, LP, AD),
         (1, 1, LP, P), (1, 1, LP, ROPE)]


def kernel(**inputs):
    import numpy as _np
    import concourse.bacc as _bacc
    from concourse import mybir as _mybir
    from concourse.bass_utils import run_bass_kernel_spmd as _run

    nc = _bacc.Bacc("TRN2", target_bir_lowering=False, num_devices=1)
    arrays, given, consts, outs = {}, {}, {}, []
    for name in _INS:
        a = _np.ascontiguousarray(inputs[name])
        arrays[f"in_{name}_dram"] = a
        given[name] = nc.dram_tensor(f"in_{name}_dram", a.shape, _mybir.dt.from_np(a.dtype), kind="ExternalInput").ap()
    for name, a in host_constants().items():
        a = _np.ascontiguousarray(a)
        arrays[f"in_{name}_dram"] = a
        consts[name] = nc.dram_tensor(f"in_{name}_dram", a.shape, _mybir.dt.from_np(a.dtype), kind="ExternalInput").ap()
    for i, shape in enumerate(_OUTS):
        outs.append(nc.dram_tensor(f"out_{i}_dram", shape, _mybir.dt.float32, kind="ExternalOutput").ap())
    build_kernel(nc, given, consts, outs)
    r = _run(nc, [arrays], core_ids=[0])
    return tuple(r.results[0][f"out_{i}_dram"] for i in range(len(_OUTS)))
```

```python
from contextlib import ExitStack
import math

import numpy as np
import concourse.bass as bass
from concourse import mybir

F32 = mybir.dt.float32
I32 = mybir.dt.int32
BF16 = mybir.dt.bfloat16
ALU = mybir.AluOpType
ACT = mybir.ActivationFunctionType
AX_X = mybir.AxisListType.X

P = 128
D = 1024
KD = D // P
LP, LS = 128, 256
T = LP + LS
NT = T // P
SEGS = ((0, LP), (LP, T))
EPS = 1e-6
HEADS, HDIM, STATE, GROUPS = 16, 64, 128, 2
XBC = D + 2 * GROUPS * STATE
KX = XBC // P
TAPS, PAD = 5, 2
PADDED = PAD + LP + PAD + LS + PAD
HY_TAPS, HY_HID, HY_FEAT, HY_BANDS = 3, 64, 33, 16
COL_XBC, COL_DT, COL_HY = D, D + XBC, D + XBC + HEADS
AH, AD = 8, 64
GRID_W, WIN_R, WIN_C = 64, 8, 16
ROPE = 32
QK = AD + ROPE
QR = 256
E, PERG, NG, HID = 32, 8, 4, 256
CAP = 64
PAIRS = E // 2
ROUNDS = T // CAP
BIG = 1e30

SLOT, NSLOT = 4096, 6


ADA_AFTER = {("z", 3): (0, 4), ("z", 7): (0, 6), ("xbc", 3): (0, 8), ("xbc", 7): (0, 10), ("xbc", 11): (1, 0),
             ("hy", 0, 3): (1, 2), ("hy", 0, 7): (1, 4), ("hy", 1, 3): (1, 6), ("hy", 1, 7): (1, 8), ("hy", 2, 3): (1, 10)}


def stream_plan():
    first = [("ada", 0, b) for b in range(4)]
    for kind in [("z",)] * 2 + [("xbc",)] * 3 + [("hy", q) for q in range(3) for _ in range(2)]:
        block = kind + (sum(x[:-1] == kind for x in first),)
        first.append(block)
        l, b = ADA_AFTER.get(kind + (4 * block[-1] + 3,), (0, None))
        if b is not None:
            first += [("ada", l, b), ("ada", l, b + 1)]
    first += [("wout", b) for b in range(4)]
    second = [("od", b) for b in range(4)] + [("odout", b) for b in range(2)]
    return first, second


FIRST, SECOND = stream_plan()
LOADS = FIRST + SECOND
LOAD_AT = {n: k for k, n in enumerate(LOADS)}
HY_SLOTS = [k % NSLOT for k in (len(FIRST) - 6, len(FIRST) - 5)]
assert len(FIRST) % NSLOT == 3 and len(SECOND) % NSLOT == 0 and 3 * PAIRS % NSLOT == 0


TURNS = [(i, h) for h in range(AH) for i in ("p", 0, 1)]


QUADS = [(t, q) for t in range(NT) for q in range(4)]


def bank_plan():
    j = []

    def job(name, by, block=None):
        j.append((name, by, block))

    def ada(l, b):
        for i in range(2):
            job(("adaw", l, b + i), "act")
        for i in range(2):
            job(("ada", l, b + i), "dve", ("ada", l, b + i))

    def ada_after(name):
        if name in ADA_AFTER:
            ada(*ADA_AFTER[name])

    for i in range(5):
        job(("par", i), "act")
    for k in range(KD):
        job(("xTr", k), "act")
    for b in (0, 2):
        ada(0, b)
    job(("ss", "mix0"), "act")
    for c in range(KD):
        job(("z", c), "act", ("z", c // 4) if c % 4 == 3 else None)
        ada_after(("z", c))
    job(("dt",), "dve")
    for c in range(KX):
        job(("xbc", c), "act", ("xbc", c // 4) if c % 4 == 3 else None)
        ada_after(("xbc", c))
    for t in range(NT):
        for half in range(2):
            job(("xtk", t, half), "act")
        job(("btk", t), "act")
    for d in range(2):
        for g in range(2):
            job(("sinit", d, g), "act")
    for t in range(NT):
        job(("wt", t), "act")
    for d in range(2):
        for g in range(2):
            job(("st0", d, g), "act")
    for d in range(2):
        for g in range(2):
            job(("st", d, g), "dve")
    job(("cb", 0), "dve")
    for step in range(-1, len(QUADS)):
        if step + 1 < len(QUADS):
            t, q = QUADS[step + 1]
            job(("E", t, q), "act")
            if t:
                job(("cs", t, q, 0), "act")
                job(("cs", t, q, 1), "act")
        if step >= 0:
            t, q = QUADS[step]
            if q == 3 and t + 1 < NT:
                job(("cb", t + 1), "dve")
            job(("y", t, q), "dve")
    job(("ss", "ssd"), "act")
    for q in range(3):
        for c in range(KD):
            job(("hy", q, c), "act", ("hy", q, c // 4) if c % 4 == 3 else None)
            ada_after(("hy", q, c))
    job(("f", 0), "dve")
    job(("f", 1), "dve")
    for b in range(2):
        for o in range(2):
            for t in range(NT):
                job(("utk", b, o, t), "act")
            for s in range(2):
                for x in range(2):
                    for t in range(s + 1):
                        job(("PQ", b, o, s, x, t), "dve")
            for s in range(2):
                for k in range(s + 1):
                    job(("H", b, o, s, k, 0), "dve")
                    job(("H", b, o, s, k, 1), "act")
            for s in range(2):
                for k in range(s + 1):
                    job(("U", b, o, s, k, 0), "none")
                    job(("U", b, o, s, k, 1), "dve")
            for s in range(2):
                for c in range(4):
                    job(("inv", b, o, s, c), "dve")
    for m in range(KD):
        job(("wout", m), "dve", ("wout", m // 2) if m % 2 == 1 else None)

    def moe(l):
        job(("ss", "ffn%d" % l), "act")
        job(("rt", l), "dve")
        for t in range(NT):
            for h in range(2):
                job(("htk", l, t, h), "act")
        job(("pos", l), "dve")
        job(("tbl", l), "dve")
        job(("MOE", l), "none")
        for k in range(KD):
            job(("yTr", l, k), "dve")

    moe(0)
    job(("ss", "mix1"), "act")
    for c in range(8):
        job(("qk", c), "act", ("od", c // 4) if c % 4 == 3 else None)
    for t in range(NT):
        job(("v", t), "act", ("od", 2) if t == 2 else None)
    for c in range(4):
        job(("lat", c), "act", ("od", 3) if c == 3 else None)
    job(("ktok",), "act")
    job(("kctx",), "act")
    def heads(kind):
        for n in range(-2, len(TURNS) + 1):
            if n + 2 < len(TURNS):
                job((kind,) + TURNS[n + 2], "dve")
            if 0 <= n < len(TURNS):
                job((kind + "t",) + TURNS[n], "act")
            if n >= 1:
                job((kind + "o",) + TURNS[n - 1], "act")

    heads("na")
    job(("ss", "q"), "act")
    job(("ss", "kv"), "act")
    job(("mctx",), "act")
    job(("ckvtok",), "act")
    for h in range(AH):
        job(("qm", h), "act")
        job(("km", h), "act")
    for t in range(4):
        job(("vm", t), "act")
    heads("ml")
    for m in range(KD):
        job(("odout", m), "dve", ("odout", m // 4) if m % 4 == 3 else None)
    moe(1)
    job(("ss", "final"), "act")
    for t in range(NT):
        for h in range(2):
            job(("out", t, h), "act")
    return j


PLAN = bank_plan()
JOB = {n: i for i, (n, _, _) in enumerate(PLAN)}
assert len(JOB) == len(PLAN)
TAKER = [by for _, by, _ in PLAN]
RANK = [TAKER[:i].count(TAKER[i]) + 1 for i in range(len(PLAN))]
LAST_USE = {b: i for i, (_, _, b) in enumerate(PLAN) if b is not None}
assert set(LAST_USE) == set(LOADS)

HY_LOADS = 8

ROWS = [[("c_ctx", 8), ("c", 8), ("norm_mix", 16), ("norm_ffn", 16), ("norm_final", 8), ("ssd_norm", 8),
         ("mla_q_norm", 2), ("mla_kv_norm", 1), ("ev_conv_b", 12), ("hy_conv_b", 24)],
        [("b_ada", 96)], [("hy_conv_w", 72)], [("ev_conv_w", 60)]]
PAR = {}
for i, tile in enumerate(ROWS):
    at = 0
    for name, n in tile:
        PAR[name] = i * P + at
        at += n
NROWS = [sum(n for _, n in tile) for tile in ROWS]
PAR["ssd_d"] = 4 * P
assert max(NROWS) <= P

C_ID, C_GT, C_LE, C_LT, C_GE, C_ONE = (i * P for i in range(6))
NCST = 6 * P


def host_constants():
    i = np.arange(P)
    row, col = i[:, None], i[None, :]
    cst = np.concatenate([row == col, row > col, row <= col, row < col, row >= col,
                          np.ones((P, P))], 1).astype(np.float32)

    rev = (8 * (row + col == P - 1)).astype(np.float32)

    def dft(n):
        th = math.pi / n
        a = np.arange(n, dtype=np.float64)
        f = a[:, None] * (a[None, :] + 0.5) * th
        parts = [np.cos(f), -np.sin(f), np.cos(f).T / n, -np.sin(f).T / n]
        return np.stack([x.reshape(n // P, P, n).transpose(1, 0, 2).reshape(P, -1) for x in parts], 1)

    dft_all = np.concatenate([dft(LP).reshape(P, -1), dft(LS).reshape(P, -1)], 1).astype(np.float32)

    def times(n):
        return np.linspace(0.0, 1.0, n)

    def feat(n):
        t = times(n)[:, None]
        w = 2.0 * math.pi * np.arange(n) / n
        bands = np.linspace(1e-4, HY_BANDS - 1, HY_BANDS)
        ang = w[:, None] * bands[None]
        return np.concatenate([t, np.cos(ang), -np.sin(ang)], -1).T

    feats = np.concatenate([feat(LP), feat(LS)], 1).astype(np.float32)
    deltas = np.linspace(abs(math.log(1e-2) / 1.5), abs(math.log(1e-2) / 0.3), D)
    t = np.concatenate([times(LP), times(LS)])
    decay = np.exp(-t[:, None] * deltas).astype(np.float32).reshape(NT, P, D)
    q = np.arange(LS) % GRID_W
    c0 = np.clip(q - WIN_C // 2, 0, GRID_W - WIN_C)
    ok = (q[None, :] >= c0[:, None]) & (q[None, :] < c0[:, None] + WIN_C)
    mask = np.where(ok, 0.0, -8.0 * BIG).astype(np.float32).reshape(2, P, LS)
    nf = ROPE // 4
    inv = 10000.0 ** (-np.arange(nf) / nf)
    pos = np.stack([np.arange(LS) // GRID_W, np.arange(LS) % GRID_W])
    ang = pos[:, None, :] * inv[None, :, None]
    rope = np.stack([np.stack([np.cos(ang), np.cos(ang)], 1), np.stack([-np.sin(ang), np.sin(ang)], 1)])
    rope = rope.reshape(2, ROPE, LS).transpose(1, 0, 2).astype(np.float32)
    slots = np.tile(np.arange(T), (P, 1)).astype(np.float32)
    small = np.concatenate([np.tile(np.arange(E) * CAP, (P, 1)), np.tile(np.arange(ROUNDS) * CAP, (P, 1)),
                            i[:, None] + 1, np.tile(np.arange(NT) * P, (P, 1)), np.tile(8 - np.arange(8), (P, 1)),
                            np.where(i < HY_HID, 1, -1)[:, None], i[:, None] % 32 == np.arange(2)[None]], 1).astype(np.float32)
    return {"k_cst": cst, "k_dft": dft_all, "k_feat": feats, "k_decay": decay, "k_mask": mask, "k_rope": rope,
            "k_slots": slots, "k_small": small, "k_rev": rev}


SWAP = [i ^ (ROPE // 4) for i in range(ROPE)]


def build_kernel(nc, A, K, outs):
    with ExitStack() as ctx:
        sems = {}

        def S(name):
            if name not in sems:
                sems[name] = ctx.enter_context(nc.semaphore(name))
            return sems[name]

        def sb(name, shape, dt=F32):
            return ctx.enter_context(nc.sbuf_tensor(name, shape, dt))

        ring = sb("ring", [P, NSLOT * SLOT])
        xT = sb("xT", [P, KD, T])
        hT = sb("hT", [P, KD, T])
        cst = sb("cst", [P, NCST])
        par = sb("par", [P, 4 * P + KD])
        mod = sb("mod", [P, 2, 48, 2])
        gmod = sb("gmod", [P, 4, KD, 2])
        rstdw = sb("rstd", [P, 512])
        rstd = rstdw[:, 0:T]
        scr = sb("scr", [P, 656])
        small = sb("small", [P, E + ROUNDS + 1 + NT + PERG + 4])
        sgn, pick, eps = small[:, -4:-3], small[:, -3:-1], small[:, -1:]
        cond = par[:, 2 * P + NROWS[2]:2 * P + NROWS[2] + 2 * KD + 30]
        counti = sb("counti", [P, 1], I32)
        ar = sb("arena", [P, 19712])
        banks = [ctx.enter_context(nc.psum_tensor("bank%d" % i, [P, 512], F32)) for i in range(8)]

        rows_d = [nc.dram_tensor("rows%d" % l, (T, D), F32).ap() for l in range(2)]
        outs_d = [nc.dram_tensor("expert_rows%d" % l, (2 * T, D), F32).ap() for l in range(2)]

        ident = cst[:, C_ID:C_ID + P]
        after, upto = cst[:, C_GT:C_GT + P], cst[:, C_LE:C_LE + P]
        before, since = cst[:, C_LT:C_LT + P], cst[:, C_GE:C_GE + P]
        ones = cst[:, C_ONE:C_ONE + P]

        def area(at, *shape):
            n = int(np.prod(shape))
            assert at + n <= 19712, (at, shape)
            v = ar[:, at:at + n]
            if len(shape) == 2:
                v = v.rearrange("p (a b) -> p a b", a=shape[0])
            if len(shape) == 3:
                v = v.rearrange("p (a b c) -> p a b c", a=shape[0], b=shape[1])
            return v

        prow = area(16000, 4, P)
        d2 = area(16512, 2)
        d8 = area(16514, P)
        xrow = area(8192, NT, D)
        sq_at = {"mix0": 3072, "ssd": 6144, "ffn0": 6144, "mix1": 0, "q": 15872, "kv": 16640, "ffn1": 0, "final": 0}
        szT = area(0, KD, T)
        xbcT = area(3072, KX, T)
        xtok = area(7680, NT, D)
        btok = area(10752, NT, 2 * STATE)
        cpad = area(11520, 2, PADDED)
        cacc = area(12304, 2, PADDED - 2 * PAD)
        dtw = area(13200, 8, 96)
        rf, rb = area(11520, 4, P), area(12032, 4, P)
        expE, m2 = area(12544, 4, P), area(13568, 4, P)
        mdecs = (area(13056, 4, P), rstdw[:, :].rearrange("p (h l) -> p h l", h=4))
        ctf, ctb = area(14080, 4, P), area(14592, 4, P)
        cbf, cbb = area(15104, 2, P), area(15360, 2, P)
        sent = area(15616, 4, D)
        xw = area(11520, D)
        stok = [area(16640, KD, P), area(17664, KD, P)]
        stout = area(13568, 4, P)
        dts = scr[:, 0:96].rearrange("p (d t h) -> p d t h", d=2, t=NT)
        dta = scr[:, 96:192].rearrange("p (t d h) -> p t d h", d=2, t=NT)
        wexp = scr[:, 192:384].rearrange("p (t n) -> p t n", t=NT)
        wsc = scr[:, 384:480].rearrange("p (t d h) -> p t d h", d=2, t=NT)
        arow = area(14000, 2, HEADS)
        brow = area(14032, 2, HEADS)
        wdtt = area(14064, KD, HEADS)
        hyT = area(3072, KD, T)
        u0T = area(6144, KD, T)
        p1T = area(9216, KD, T)
        hview = hT[:, :, :].rearrange("p k t -> p (k t)")
        ut = hview[:, 1536:3072].rearrange("p (a b) -> p a b", a=NT)
        pq = (hview[:, 0:1024].rearrange("p (x k n) -> p x k n", x=2, k=1), area(12288, 2, 2, 512))
        hh = ((hview[:, 1024:1536].unsqueeze(1), scr[:, 0:512].unsqueeze(1)), (area(14336, 2, 512), area(15360, 2, 512)))
        hpad = area(12288, 2, PADDED)
        hacc = area(13072, 2, PADDED - 2)
        dft = area(16384, 2560)
        hsP, hsQ = area(18944, T), area(19328, T)
        hyl = [ring[:, s * SLOT:(s + 1) * SLOT] for s in HY_SLOTS]
        w3s = hyl[0][:, 0:2048].rearrange("p (b o n) -> p b o n", b=2, o=2)
        decay = (hyl[0][:, 2048:3584].rearrange("p (t n) -> p t n", t=NT), hyl[1][:, 2048:3584].rearrange("p (t n) -> p t n", t=NT))
        hyb = hyl[1][:, 0:2048].rearrange("p (b o n) -> p b o n", b=2, o=2)
        ytmp = rstdw
        w1t = area(14336, HY_HID)
        w2t = area(14400, P)
        featt = area(14528, T)
        fpar = area(14912, 4)
        farg = area(14916, T)
        fk = area(15300, T)
        h1 = area(15684, T)
        qkT = area(0, 8, T)
        vtok = area(3072, NT, 512)
        kcT = area(4608, 4, P)
        kctok, vctok = area(5120, 512), area(5632, 512)
        ktok = area(6144, 512)
        ncsc = [area(at, T) for at in (7168, 7552, 9728)]
        npt = area(7936, 2, T)
        nbias = area(8704, 2, LS)
        nmask = area(9216, 2, LS)
        rope = area(10752, 2, LS)
        latT = area(11264, 4, T)
        wuq = area(12800, 2, AH * QK)
        wukv = area(14336, AH * 2 * AD)
        ckvT = area(15360, 4 * P)
        vm = area(15872, 4, 512)
        sqq = area(sq_at["q"], 2, T)
        rkv = area(17920, T)
        ckto = area(18304, P)
        krto = area(18432, QK)
        ckctok = area(18528, P)
        kr96 = area(18656, QK)
        nrows = area(18752, 3, 4)
        krot = area(18768, LS)
        rev = area(19024, P)
        qmT = area(0, AH, T)
        kmT = area(3072, AH, 512)
        qrot = area(8704, AH * LS)
        oT = hT
        fino = area(4096, NT, D)
        xs = area(0, 2, D)
        xsT = area(2048, 2, D)
        sg, hid, hidT = area(4096, 2, HID), area(4608, 2, HID), area(5120, 2, HID)
        ob = area(5632, 2, D)
        htok = area(7680, NT, D)
        onehot = area(10752, NT, T // 2).bitcast(BF16)
        yg = [area(at, 2, D) for at in (7680, 5632, 0)]
        yc = area(10752, NT, D)
        wr = area(14208, KD, NG + E)
        rbias = area(14500, NG + E)
        slotrow = area(14540, T)
        rmask = area(15000, NT, E)
        rtok = area(15100, 2, NT * E).bitcast(BF16).rearrange("p c (t e x) -> p c t e x", t=NT, x=2)
        rsc = area(15400, 1600)
        rsc_g, rsc_e = rsc[:, 1000:1012], rsc[:, 1020:1023]
        efirst, thr = small[:, 0:E], small[:, E:E + ROUNDS]
        tokin, tilestart = small[:, E + ROUNDS:E + ROUNDS + 1], small[:, E + ROUNDS + 1:E + ROUNDS + 1 + NT]
        tie = small[:, E + ROUNDS + 1 + NT:E + ROUNDS + 1 + NT + PERG]
        tbli = scr[:, 512:608].bitcast(I32)
        scati = rsc[:, 1100:1196].bitcast(I32)
        idxc = scr[:, 608:612].bitcast(I32)
        ysw = scr[:, 620:626]

        SQ_N = [("mix0", KD), ("ssd", KD), ("ffn0", KD), ("mix1", KD), ("q", 2), ("kv", 1), ("ffn1", KD), ("final", KD)]

        def sq_base(which):
            return sum(n for i, (w, n) in enumerate(SQ_N) if i < [x for x, _ in SQ_N].index(which))

        MODS = ["mix0", "ffn0", "mix1", "ffn1", "final"]
        done = S("pe_done")
        taken = {"act": S("act_took"), "dve": S("dve_took")}

        def full(eng, *name):
            eng.wait_ge(done, JOB[name] + 1)

        def took(eng, *name):
            i = JOB[name]
            if TAKER[i] == "none" and name[0] == "U":
                i += 1
            if TAKER[i] != "none":
                eng.wait_ge(taken[TAKER[i]], RANK[i])

        def bank(*name):
            return banks[JOB[name] % 8]

        class Chain:

            def __init__(self, eng, name):
                self.eng, self.sem, self.n = eng, S(name), 0

            def __call__(self, ins):
                self.n += 1
                ins.then_inc(self.sem, 1)
                self.eng.wait_ge(self.sem, self.n)

        def slot(k):
            return ring[:, (k % NSLOT) * SLOT:(k % NSLOT + 1) * SLOT]

        def block_source(b):
            if b[0] == "ada":
                return A["w_ada"][b[1], :, b[2] * 512:(b[2] + 1) * 512].rearrange("(k p) n -> p k n", p=P)
            if b[0] == "z":
                return A["ev_w_in"][0, :, b[1] * 512:(b[1] + 1) * 512].rearrange("(k p) n -> p k n", p=P)
            if b[0] == "xbc":
                return A["ev_w_in"][0, :, COL_XBC + b[1] * 512:COL_XBC + (b[1] + 1) * 512].rearrange("(k p) n -> p k n", p=P)
            if b[0] == "hy":
                c0 = COL_HY + b[1] * D + b[2] * 512
                return A["ev_w_in"][0, :, c0:c0 + 512].rearrange("(k p) n -> p k n", p=P)
            if b[0] == "wout":
                return A["ev_w_out"][0, :, b[1] * 256:(b[1] + 1) * 256].rearrange("(k p) n -> p k n", p=P)
            if b[0] == "od":
                w = 512 if b[1] < 3 else 416
                return A["od_w_in"][0, :, b[1] * 512:b[1] * 512 + w].rearrange("(k p) n -> p k n", p=P)
            return A["od_w_out"][0, :, b[1] * 512:(b[1] + 1) * 512].rearrange("(k p) n -> p k n", p=P)

        def ada_rows(b):
            return slot(LOAD_AT[("ada",) + b])[:, 0:512]

        def block_view(b):
            s = slot(LOAD_AT[b])
            if b == ("od", 3):
                return s[:, 0:8 * 416].rearrange("p (k n) -> p k n", k=8)
            return s.rearrange("p (k n) -> p k n", k=16 if b[0] == "wout" else 8)

        def expert_slot(n, part):
            return 3 * ((n + 1) % 2) + part

        def down_view(s):
            return ring[:, s * SLOT:(s + 1) * SLOT].rearrange("p (e k n) -> p e k n", e=2, n=D)

        def trips(eng, l):
            eng.wait_ge(S("trips%d" % l), 1)
            return eng.value_load(counti[0:1, 0:1], min_val=0, max_val=PAIRS // 2 * (ROUNDS - 1)) + PAIRS // 2

        block = ctx.enter_context(nc.Block())

        @block.sync
        def _(sp):
            for t in range(NT):
                src = A["x_prompt"][0] if t == 0 else A["x_sample"][0, (t - 1) * P:t * P, :]
                sp.dma_start(xrow[:, t, :], src).then_inc(S("x_in"), 16)

            def static_load(k, first_after_experts):
                s = k % NSLOT
                if k >= NSLOT and not first_after_experts:
                    sp.wait_ge(done, LAST_USE[LOADS[k - NSLOT]] + 1)
                sp.dma_start(block_view(LOADS[k]), block_source(LOADS[k])).then_inc(S("full%d" % s), 16)

            def pair_loads(l, n, b, first):
                for part, name in enumerate(("moe_w_gate", "moe_w_up", "moe_w_down")):
                    s = expert_slot(b, part)
                    if first:
                        last = max(k for k in range(len(FIRST) if l == 0 else len(LOADS)) if k % NSLOT == s)
                        if l == 0 and s in HY_SLOTS:
                            sp.wait_ge(done, JOB[("inv", 1, 1, 1, 3)] + 1)
                        else:
                            sp.wait_ge(done, LAST_USE[LOADS[last]] + 1)
                    else:
                        sp.wait_ge(S("gu_done%d" % l) if part < 2 else S("down_done%d" % l), n - 1)
                    pair = n % PAIRS
                    src = A[name][l].rearrange("(q e) (p k) n -> q p e (k n)", e=2, p=P)
                    src = src[pair] if isinstance(pair, int) else src[bass.ds(pair, 1)].rearrange("q p e m -> (q p) e m")
                    dst = ring[:, s * SLOT:(s + 1) * SLOT].rearrange("p (e m) -> p e m", e=2)
                    sp.dma_start(dst, src).then_inc(S("efull%d_%d" % (l, s)), 16)

            def expert_loads(l):
                for n in range(2):
                    pair_loads(l, n, n, True)
                r = trips(sp, l)
                with sp.Fori(1, r) as i:
                    for b in range(2):
                        pair_loads(l, 2 * i + b, b, False)
                return r

            n1 = len(FIRST)
            for k in range(n1):
                if k == 1:
                    sp.wait_ge(S("rows_in"), 16 * sum(len(t) for t in ROWS))
                    sp.wait_ge(S("small_in"), 16)
                static_load(k, False)
            r = expert_loads(0)
            for k in range(n1, len(LOADS)):
                s = k % NSLOT
                gone = 2 * r - (1 if s >= 3 else 0)
                sp.wait_ge(S("down_done0") if s % 3 == 2 else S("gu_done0"), gone)
                if k >= n1 + 3:
                    sp.wait_ge(S("yg%d" % (NT - 1)), 16)
                static_load(k, True)
            expert_loads(1)

        @block.tensor
        def _(pe):
            state = {"i": 0}

            def open_bank(*name):
                i = state["i"]
                assert PLAN[i][0] == name, (PLAN[i][0], name)
                state["i"] += 1
                if i >= 8:
                    took(pe, *PLAN[i - 8][0])
                return banks[i % 8]

            def mm(out, lhsT, rhs, start, stop_):
                return nc.tensor.matmul(out, lhsT, rhs, start=start, stop=stop_, skip_group_check=True)

            def tr(out, in_):
                n = in_.shape[0]
                return nc.tensor.transpose(out, in_, ident[0:n, 0:n])

            def arrived(b):
                k = LOAD_AT[b]
                pe.wait_ge(S("full%d" % (k % NSLOT)), 16 * (k // NSLOT + 1))

            def project(name, w, col, rhs, width=T, m=P, k0=KD):
                ps = open_bank(*name)
                for k in range(k0):
                    last = mm(ps[0:m, 0:width], w[:, k, col:col + m], rhs[:, k, 0:width], k == 0, k == k0 - 1)
                last.then_inc(done, 1)

            def ada(l, b0):
                for b in (b0, b0 + 1):
                    ps = open_bank("adaw", l, b)
                    arrived(("ada", l, b))
                    w = block_view(("ada", l, b))
                    for k in range(KD):
                        g = k % 4
                        last = nc.tensor.matmul(ps[32 * g:32 * g + 32, :], cond[:, 2 * k:2 * k + 32],
                                                w[:, k, :], start=k < 4, stop=k >= 4, tile_position=(0, 32 * g),
                                                skip_group_check=True)
                    last.then_inc(done, 1)
                for b in (b0, b0 + 1):
                    ps = open_bank("ada", l, b)
                    took(pe, "adaw", l, b)
                    for m in range(4):
                        last = mm(ps[:, 2 * m:2 * m + 2], ada_rows((l, b))[:, m * P:(m + 1) * P], pick, True, True)
                    last.then_inc(done, 1)

            def ada_after(*name):
                if name in ADA_AFTER:
                    ada(*ADA_AFTER[name])

            def sum_squares(which, src, n):
                ps = open_bank("ss", which)
                for k in range(n):
                    pe.wait_ge(S("sq"), sq_base(which) + k + 1)
                    last = mm(ps[:, 0:T], ones, src[:, k, :], k == 0, k == n - 1)
                last.then_inc(done, 1)

            def sum_added_squares(which, src, n):
                ps = open_bank("ss", which)
                pe.wait_ge(S("sqsum"), n)
                mm(ps[:, 0:T], ones, src[:, 0, :], True, True).then_inc(done, 1)

            def mixer_input(i):
                pe.wait_ge(S("hT"), KD * (i + 1))

            pe.wait_ge(S("cst_in"), 16)
            pe.wait_ge(S("rows_in"), 16 * sum(len(t) for t in ROWS))
            for i in range(4):
                ps = open_bank("par", i)
                tr(ps[:, 0:NROWS[i]], prow[0:NROWS[i], i, :]).then_inc(done, 1)
            ps = open_bank("par", 4)
            pe.wait_ge(S("d8"), 1)
            tr(ps[:, 0:KD], d8[0:KD, :]).then_inc(done, 1)
            pe.wait_ge(S("x_in"), 16 * NT)
            for k in range(KD):
                ps = open_bank("xTr", k)
                for t in range(NT):
                    last = tr(ps[:, t * P:(t + 1) * P], xrow[:, t, k * P:(k + 1) * P])
                last.then_inc(done, 1)
            pe.wait_ge(S("silc"), 1)
            pe.wait_ge(S("small_in"), 16)
            for b in (0, 2):
                ada(0, b)
            sum_squares("mix0", area(sq_at["mix0"], KD, T), KD)
            mixer_input(0)
            for c in range(KD):
                if c % 4 == 0:
                    arrived(("z", c // 4))
                project(("z", c), block_view(("z", c // 4)), c % 4 * P, hT)
                ada_after("z", c)
            ps = open_bank("dt")
            pe.wait_ge(S("dtin"), 16 * 3)
            for t in range(NT):
                for k in range(KD):
                    last = mm(ps[:, t * HEADS:(t + 1) * HEADS], hT[:, k, t * P:(t + 1) * P], wdtt[:, k, :], k == 0, k == KD - 1)
            last.then_inc(done, 1)
            for c in range(KX):
                if c % 4 == 0:
                    arrived(("xbc", c // 4))
                project(("xbc", c), block_view(("xbc", c // 4)), c % 4 * P, hT)
                ada_after("xbc", c)
            pe.wait_ge(S("xbc"), KX)
            for t in range(NT):
                for half in range(2):
                    ps = open_bank("xtk", t, half)
                    for c in range(4):
                        last = tr(ps[:, c * P:(c + 1) * P], xbcT[:, half * 4 + c, t * P:(t + 1) * P])
                    last.then_inc(done, 1)
                ps = open_bank("btk", t)
                for g in range(2):
                    last = tr(ps[:, g * P:(g + 1) * P], xbcT[:, KD + g, t * P:(t + 1) * P])
                last.then_inc(done, 1)
            for d in range(2):
                pe.wait_ge(S("sinit_in%d" % d), 16)
                for g in range(2):
                    ps = open_bank("sinit", d, g)
                    for c in range(4):
                        last = tr(ps[:, c * P:(c + 1) * P], stok[d][:, g * 4 + c, :])
                    last.then_inc(done, 1)
            pe.wait_ge(S("dta"), 1)
            for t in range(NT):
                ps = open_bank("wt", t)
                mm(ps[:, 0:HEADS], after, dta[:, t, 0, :], True, True)
                mm(ps[:, HEADS:2 * HEADS], before, dta[:, t, 1, :], True, True)
                mm(ps[:, 2 * HEADS:4 * HEADS], ones, dta[:, t, :, :].rearrange("p d h -> p (d h)"), True, True).then_inc(done, 1)
            for d in range(2):
                pe.wait_ge(S("xw"), d + 1)
                took(pe, "btk", 0)
                for g in range(2):
                    ps = open_bank("st0", d, g)
                    for c in range(4):
                        last = mm(ps[:, c * P:(c + 1) * P], xw[:, (g * 4 + c) * P:(g * 4 + c + 1) * P], btok[:, 0, g * P:(g + 1) * P], True, True)
                    last.then_inc(done, 1)
            for d in range(2):
                pe.wait_ge(S("xw"), d + 3)
                took(pe, "btk", d + 1)
                for g in range(2):
                    ps = open_bank("st", d, g)
                    mm(ps[:, :], btok[:, d + 1, g * P:(g + 1) * P], xw[:, g * 512:(g + 1) * 512], True, True).then_inc(done, 1)
            def chunk_scores(t):
                tt = slice(t * P, (t + 1) * P)
                ps = open_bank("cb", t)
                for g in range(2):
                    last = mm(ps[:, g * P:(g + 1) * P], xbcT[:, KD + g, tt], xbcT[:, KD + 2 + g, tt], True, True)
                last.then_inc(done, 1)

            def decays(step, t, q):
                ps = open_bank("E", t, q)
                pe.wait_ge(S("rfb"), 2 * (step + 1))
                mm(ps[:, :], after, rf.rearrange("p h l -> p (h l)"), True, False)
                mm(ps[:, :], before, rb.rearrange("p h l -> p (h l)"), False, True).then_inc(done, 1)
                if t:
                    ps = open_bank("cs", t, q, 0)
                    mm(ps[:, :], ones, rf.rearrange("p h l -> p (h l)"), True, True).then_inc(done, 1)
                    ps = open_bank("cs", t, q, 1)
                    mm(ps[:, :], ones, rb.rearrange("p h l -> p (h l)"), True, True).then_inc(done, 1)

            def outputs(step, t, q):
                ps = open_bank("y", t, q)
                pe.wait_ge(S("mm"), step + 1)
                if t:
                    pe.wait_ge(S("ctd"), 2 * (4 * (t - 1) + q + 1))
                    took(pe, "st", 1, 1)
                    took(pe, "sinit", 1, 1)
                for j in range(4):
                    h = 4 * q + j
                    o = ps[(j % 2) * HDIM:(j % 2 + 1) * HDIM, (j // 2) * P:(j // 2 + 1) * P]
                    hp = slice(h * HDIM, (h + 1) * HDIM)
                    last = mm(o, xtok[:, t, hp], mdecs[step % 2][:, j, :], True, t == 0)
                    if t:
                        mm(o, sent[:, t - 1, hp], ctf[:, j, :], False, False)
                        last = mm(o, sent[:, t + 1, hp], ctb[:, j, :], False, True)
                last.then_inc(done, 1)

            chunk_scores(0)
            for step in range(-1, len(QUADS)):
                if step + 1 < len(QUADS):
                    decays(step + 1, *QUADS[step + 1])
                if step >= 0:
                    t, q = QUADS[step]
                    if q == 3 and t + 1 < NT:
                        chunk_scores(t + 1)
                    outputs(step, t, q)
            sum_squares("ssd", area(sq_at["ssd"], KD, T), KD)

            for q in range(3):
                for c in range(KD):
                    if c % 4 == 0:
                        arrived(("hy", q, c // 4))
                    project(("hy", q, c), block_view(("hy", q, c // 4)), c % 4 * P, hT)
                    ada_after("hy", q, c)
            pe.wait_ge(S("hyc_in"), 16 * 11)
            ps = open_bank("f", 0)
            mm(ps[0:HY_HID, 0:T], w1t[0:HY_FEAT, :], featt[0:HY_FEAT, :], True, True).then_inc(done, 1)
            ps = open_bank("f", 1)
            pe.wait_ge(S("fsin"), 1)
            mm(ps[:, 0:T], w2t[0:HY_HID, :], h1[0:HY_HID, :], True, True).then_inc(done, 1)
            pe.wait_ge(S("hs"), 1)
            pe.wait_ge(S("hconv"), 3 * KD)
            for b in range(2):
                for o in range(2):
                    src = u0T if o == 0 else p1T
                    if o == 1:
                        took(pe, "inv", b, 0, 1, 3)
                    for t in range(NT):
                        ps = open_bank("utk", b, o, t)
                        for c in range(4):
                            last = tr(ps[:, c * P:(c + 1) * P], src[:, b * 4 + c, t * P:(t + 1) * P])
                        last.then_inc(done, 1)
                    dv = [dft[:, 4 * P * s:4 * P * s + 4 * (s + 1) * (s + 1) * P]
                          .rearrange("p (x k n) -> p x k n", x=4, k=s + 1) for s in range(2)]
                    pe.wait_ge(S("hypar_in"), 16 * HY_LOADS)
                    for s in range(2):
                        for x, hs in enumerate((hsP, hsQ)):
                            for t in range(s + 1):
                                ps = open_bank("PQ", b, o, s, x, t)
                                mm(ps[:, :], hs[:, (s + t) * P:(s + t + 1) * P], w3s[:, b, o, :], True, True).then_inc(done, 1)
                    for s in range(2):
                        for x in range(2):
                            took(pe, "PQ", b, o, s, x, s)
                        for k in range(s + 1):
                            for x in range(2):
                                ps = open_bank("H", b, o, s, k, x)
                                for t in range(s + 1):
                                    last = mm(ps[:, :], dv[s][:, x, t, k * P:(k + 1) * P], pq[s][:, x, t, :], t == 0, t == s)
                                last.then_inc(done, 1)
                    for s in range(2):
                        for t in range(s + 1):
                            took(pe, "utk", b, o, s + t)
                        for k in range(s + 1):
                            for x in range(2):
                                ps = open_bank("U", b, o, s, k, x)
                                for t in range(s + 1):
                                    last = mm(ps[:, :], dv[s][:, x, t, k * P:(k + 1) * P], ut[:, s + t, :], t == 0, t == s)
                                last.then_inc(done, 1)
                    for s in range(2):
                        pe.wait_ge(S("spec"), 3 * (2 * b + o) + (3 if s else 1))
                        for c in range(4):
                            ps = open_bank("inv", b, o, s, c)
                            for x in range(2):
                                for k in range(s + 1):
                                    last = mm(ps[:, 0:(s + 1) * P], pq[s][:, x, k, c * P:(c + 1) * P], dv[s][:, 2 + x, k, :],
                                              x == 0 and k == 0, x == 1 and k == s)
                            last.then_inc(done, 1)
            took(pe, "inv", 1, 1, 1, 3)
            pe.wait_ge(S("yn"), KD)
            for m in range(KD):
                if m % 2 == 0:
                    arrived(("wout", m // 2))
                w = block_view(("wout", m // 2))
                ps = open_bank("wout", m)
                for k in range(2 * KD):
                    rhs = szT[:, k, :] if k < KD else hyT[:, k - KD, :]
                    last = mm(ps[:, 0:T], w[:, k, m % 2 * P:(m % 2 + 1) * P], rhs, k == 0, k == 2 * KD - 1)
                last.then_inc(done, 1)

            def moe(l):
                sum_added_squares("ffn%d" % l, area(sq_at["ffn%d" % l], KD, T), (l + 1) * (KD - 1))
                mixer_input(1 + 2 * l)
                ps = open_bank("rt", l)
                pe.wait_ge(S("router_in%d" % l), 16 * 5)
                for t in range(NT):
                    for k in range(KD):
                        last = mm(ps[:, t * 40:t * 40 + NG + E], hT[:, k, t * P:(t + 1) * P], wr[:, k, :], k == 0, k == KD - 1)
                last.then_inc(done, 1)
                for t in range(NT):
                    for h in range(2):
                        ps = open_bank("htk", l, t, h)
                        for c in range(4):
                            last = tr(ps[:, c * P:(c + 1) * P], hT[:, h * 4 + c, t * P:(t + 1) * P])
                        last.then_inc(done, 1)
                ps = open_bank("pos", l)
                pe.wait_ge(S("chosen"), l + 1)
                for t in range(NT):
                    for u in range(t):
                        mm(ps[:, t * E:(t + 1) * E], ones, rmask[:, u, :], u == 0, False)
                    mm(ps[:, t * E:(t + 1) * E], before, rmask[:, t, :], t == 0, True)
                for t in range(NT):
                    last = mm(ps[:, NT * E:(NT + 1) * E], ones, rmask[:, t, :], t == 0, t == NT - 1)
                last.then_inc(done, 1)
                ps = open_bank("tbl", l)
                for c in range(2):
                    pe.wait_ge(S("onehot"), 2 * l + c + 1)
                    for r in range(ROUNDS):
                        for par_ in range(2):
                            for t in range(NT):
                                at = 2 * PAIRS * (c * ROUNDS + r)
                                o = ps[par_ * CAP:(par_ + 1) * CAP, at:at + 2 * PAIRS]
                                rhs = rtok[:, c, t, :, :].rearrange("p (q e) x -> p e q x", e=2)[:, par_, :, :]
                                last = mm(o, onehot[:, t, r * CAP:(r + 1) * CAP], rhs, t == 0, t == NT - 1)
                    if c == 0:
                        last.then_inc(S("tbl0"), 1)
                last.then_inc(done, 1)
                assert PLAN[state["i"]][0] == ("MOE", l)
                for j in range(state["i"] - 8, state["i"]):
                    took(pe, *PLAN[j][0])
                state["i"] += 1
                r = trips(pe, l)
                s = {x: S("%s%d" % (x, l)) for x in
                     ("x_ps", "x_act", "x_dve", "gu_done", "hid", "ht_done", "ht_act", "down_done", "d_act", "d_dve")}

                def turn(n, b):
                    pe.wait_ge(S("gather%d_%d" % (l, b)), 16 * ((n - b) // 2 + 1) if isinstance(n, int) else 8 * (n - b) + 16)
                    if not (isinstance(n, int) and n == 0):
                        pe.wait_ge(s["x_act"], n)
                        pe.wait_ge(s["x_dve"], n)
                    v = xs[:, b, :].rearrange("p (m k) -> p k m", k=KD)
                    for k in range(KD):
                        last = tr(banks[k // 4][:, (k % 4) * P:(k % 4 + 1) * P], v[:, k, :])
                    last.then_inc(s["x_ps"], 1)

                def gate_up(n, b):
                    fills = 16 * ((n - b) // 2 + 1) if isinstance(n, int) else 8 * (n - b) + 16
                    for part in range(2):
                        pe.wait_ge(S("efull%d_%d" % (l, expert_slot(b, part))), fills)
                    pe.wait_ge(s["x_act"], n + 1)
                    pe.wait_ge(s["x_dve"], n + 1)
                    if not (isinstance(n, int) and n < 2):
                        pe.wait_ge(s["hid"], n - 1)
                    x = xsT[:, b, :].rearrange("p (k m) -> p k m", k=KD)
                    s0 = expert_slot(b, 0)
                    w = ring[:, s0 * SLOT:(s0 + 2) * SLOT].rearrange("p (x e k n) -> p e k x n", x=2, e=2, n=HID)
                    for k in range(KD):
                        for e in range(2):
                            o = banks[2 + b][e * CAP:(e + 1) * CAP, :].rearrange("p (x n) -> p x n", x=2)
                            last = mm(o, x[:, k, e * CAP:(e + 1) * CAP], w[:, e, k, :, :], k == 0, k == KD - 1)
                    last.then_inc(s["gu_done"], 1)

                def turn_hidden(n, b):
                    pe.wait_ge(s["hid"], n + 1)
                    v = hid[:, b, :].rearrange("p (m k) -> p k m", k=2)
                    for k in range(2):
                        last = tr(banks[4][:, k * P:(k + 1) * P], v[:, k, :])
                    last.then_inc(s["ht_done"], 1)

                def down(n, b):
                    fills = 16 * ((n - b) // 2 + 1) if isinstance(n, int) else 8 * (n - b) + 16
                    pe.wait_ge(S("efull%d_%d" % (l, expert_slot(b, 2))), fills)
                    pe.wait_ge(s["ht_act"], n + 1)
                    if not (isinstance(n, int) and n == 0):
                        pe.wait_ge(s["d_act"], n)
                        pe.wait_ge(s["d_dve"], n)
                    w = down_view(expert_slot(b, 2))
                    x = hidT[:, b, :].rearrange("p (k m) -> p k m", k=2)
                    for half in range(2):
                        for k in range(2):
                            for e in range(2):
                                last = mm(banks[5 + half][e * CAP:(e + 1) * CAP, :], x[:, k, e * CAP:(e + 1) * CAP],
                                          w[:, e, k, half * 512:(half + 1) * 512], k == 0, k == 1)
                    last.then_inc(s["down_done"], 1)

                turn(0, 0)
                gate_up(0, 0)
                turn(1, 1)
                turn_hidden(0, 0)
                with pe.Fori(0, r - 1) as i:
                    for b in range(2):
                        n = 2 * i + 1 + b
                        gate_up(n, 1 - b)
                        down(n - 1, b)
                        turn(n + 1, b)
                        turn_hidden(n, 1 - b)
                n = 2 * r - 1
                gate_up(n, 1)
                down(n - 1, 0)
                turn_hidden(n, 1)
                down(n, 1)
                for x in ("x_act", "x_dve", "ht_act", "d_act", "d_dve", "hid"):
                    pe.wait_ge(s[x], 2 * r)
                pe.sem_inc(done, 1)
                for k in range(KD):
                    ps = open_bank("yTr", l, k)
                    pe.wait_ge(S("yc"), NT * (l + 1))
                    for t in range(NT):
                        last = tr(ps[:, t * P:(t + 1) * P], yc[:, t, k * P:(k + 1) * P])
                    last.then_inc(done, 1)

            moe(0)
            sum_squares("mix1", area(sq_at["mix1"], KD, T), KD)
            mixer_input(2)
            for c in range(8):
                if c % 4 == 0:
                    arrived(("od", c // 4))
                project(("qk", c), block_view(("od", c // 4)), c % 4 * P, hT)
            arrived(("od", 2))
            for t in range(NT):
                ps = open_bank("v", t)
                w = block_view(("od", 2))
                for k in range(KD):
                    last = mm(ps[:, :], hT[:, k, t * P:(t + 1) * P], w[:, k, :], k == 0, k == KD - 1)
                last.then_inc(done, 1)
            arrived(("od", 3))
            for c in range(3):
                project(("lat", c), block_view(("od", 3)), c * P, hT)
            project(("lat", 3), block_view(("od", 3)), QR + P - AD, hT, m=QK)
            ps = open_bank("ktok")
            took(pe, "lat", 3)
            for c in range(4):
                last = tr(ps[:, c * P:(c + 1) * P], qkT[:, 4 + c, 0:P])
            last.then_inc(done, 1)
            ps = open_bank("kctx")
            pe.wait_ge(S("nactx_in"), 16 * 5)
            for c in range(4):
                last = tr(ps[:, c * P:(c + 1) * P], kctok[:, c * P:(c + 1) * P])
            last.then_inc(done, 1)
            took(pe, "kctx")
            def heads(kind, scores, values, first):
                def turned(n, i, h):
                    ps = open_bank(kind + "t", i, h)
                    pe.wait_ge(S("prob"), first + n + 1)
                    for j in range(1 if i == "p" else 3):
                        last = tr(ps[:, j * P:(j + 1) * P], ncsc[n % 3][:, j * P:(j + 1) * P])
                    last.then_inc(done, 1)

                def mixed(n, i, h):
                    hp = slice((h % 2) * AD, (h % 2 + 1) * AD)
                    nk = 1 if i == "p" else 3
                    b = n % 2
                    ps = open_bank(kind + "o", i, h)
                    took(pe, kind + "t", i, h)
                    for j in range(nk):
                        last = mm(ps[hp, 0:P], values(i, h, j), npt[:, b, j * P:(j + 1) * P], j == 0, j == nk - 1)
                    last.then_inc(done, 1)

                for n in range(-2, len(TURNS) + 1):
                    if n + 2 < len(TURNS):
                        scores(*TURNS[n + 2])
                    if 0 <= n < len(TURNS):
                        turned(n, *TURNS[n])
                    if n >= 1:
                        mixed(n - 1, *TURNS[n - 1])

            def na_values(i, h, j):
                if j == 2:
                    return vctok[:, h * AD:(h + 1) * AD]
                return vtok[:, j if i == "p" else 1 + j, h * AD:(h + 1) * AD]

            def na_scores(i, h):
                hp = slice((h % 2) * AD, (h % 2 + 1) * AD)
                ps = open_bank("na", i, h)
                q0 = 0 if i == "p" else LP + i * P
                q = qkT[hp, h // 2, q0:q0 + P]
                if i == "p":
                    last = mm(ps[:, 0:P], q, qkT[hp, 4 + h // 2, 0:P], True, True)
                else:
                    mm(ps[:, 0:LS], q, qkT[hp, 4 + h // 2, LP:T], True, False)
                    pe.wait_ge(S("nbias%d" % i), 32 * (h + 1))
                    mm(ps[:, 0:LS], rev, nbias[:, i, :], False, True)
                    last = mm(ps[:, LS:T], q, kcT[hp, h // 2, :], True, True)
                last.then_inc(done, 1)
            heads("na", na_scores, na_values, 0)
            sum_squares("q", sqq, 2)
            ps = open_bank("ss", "kv")
            pe.wait_ge(S("sq"), sq_base("kv") + 1)
            mm(ps[:, 0:T], ones, area(sq_at["kv"], T), True, True).then_inc(done, 1)
            ps = open_bank("mctx")
            pe.wait_ge(S("mctx_in"), 16 * 2)
            pe.wait_ge(S("kr0"), 1)
            tr(ps[:, 0:P], ckctok)
            tr(ps[0:QK, P:2 * P], kr96).then_inc(done, 1)
            ps = open_bank("ckvtok")
            pe.wait_ge(S("ckvn"), 1)
            tr(ps[:, 0:P], ckvT[:, 0:P])
            tr(ps[:, P:P + QK], latT[0:QK, 3, 0:P]).then_inc(done, 1)
            took(pe, "mctx")
            pe.wait_ge(S("qn"), 2)
            pe.wait_ge(S("wmla_in"), 16 * 2)
            for h in range(AH):
                ps = open_bank("qm", h)
                for k in range(2):
                    last = mm(ps[0:QK, 0:T], wuq[:, k, h * QK:(h + 1) * QK], latT[:, k, :], k == 0, k == 1)
                last.then_inc(done, 1)
                ps = open_bank("km", h)
                mm(ps[0:AD, :], wukv[:, h * 2 * AD:h * 2 * AD + AD], ckvT, True, True).then_inc(done, 1)
            for t in range(4):
                ps = open_bank("vm", t)
                rhs = wukv.rearrange("p (h c) -> p h c", h=AH)[:, :, AD:2 * AD]
                mm(ps[:, :].rearrange("p (h c) -> p h c", h=AH), ckvT[:, t * P:(t + 1) * P], rhs, True, True).then_inc(done, 1)
            pe.wait_ge(S("roped"), 2)
            took(pe, "km", AH - 1)
            took(pe, "qm", AH - 1)
            took(pe, "vm", 3)

            def ml_scores(i, h):
                ps = open_bank("ml", i, h)
                q0 = 0 if i == "p" else LP + i * P
                nk = 1 if i == "p" else 3
                keys = kmT[0:QK, h, 0:P] if i == "p" else kmT[0:QK, h, P:4 * P]
                mm(ps[:, 0:nk * P], qmT[0:QK, h, q0:q0 + P], keys, True, True).then_inc(done, 1)

            def ml_values(i, h, j):
                return vm[:, j if i == "p" else 1 + j, h * AD:(h + 1) * AD]

            heads("ml", ml_scores, ml_values, len(TURNS))
            took(pe, "mlo", 1, AH - 1)
            for m in range(KD):
                if m % 4 == 0:
                    arrived(("odout", m // 4))
                project(("odout", m), block_view(("odout", m // 4)), m % 4 * P, oT)
            moe(1)
            sum_squares("final", area(sq_at["final"], KD, T), KD)
            pe.wait_ge(S("fin"), KD)
            for t in range(NT):
                for h in range(2):
                    ps = open_bank("out", t, h)
                    for c in range(4):
                        last = tr(ps[:, c * P:(c + 1) * P], hT[:, h * 4 + c, t * P:(t + 1) * P])
                    last.then_inc(done, 1)

        @block.scalar
        def _(act):
            A_ = nc.scalar.activation

            act.dma_start(cst[:, :], K["k_cst"]).then_inc(S("cst_in"), 16)
            for i, tile in enumerate(ROWS):
                at = 0
                for name, n in tile:
                    src = A[name]
                    if len(src.shape) == 1:
                        src = src.rearrange("(r p) -> r p", p=P)
                    elif len(src.shape) == 2:
                        src = src.rearrange("a (r p) -> (a r) p", p=P)
                    else:
                        src = src.rearrange("a b (r p) -> (a b r) p", p=P)
                    act.dma_start(prow[at:at + n, i, :], src).then_inc(S("rows_in"), 16)
                    at += n

            def seg_add(out, in_, bias):
                for v, (a, b) in enumerate(SEGS):
                    last = A_(out[:, a:b], in_[:, a:b], ACT.Identity, bias=bias[:, v:v + 1])
                return last

            def root(which, width):
                full(act, "ss", which)
                A_(rstd, bank("ss", which)[:, 0:T], ACT.Sqrt, bias=eps[:, 0:1], scale=1.0 / width).then_inc(taken["act"], 1)

            def squares(which, src, n, *product):
                dst = area(sq_at[which], n, T)
                for k in range(n):
                    if product:
                        took(act, *product, k)
                    A_(dst[:, k, :], src[:, k, :], ACT.Square).then_inc(S("sq"), 1)

            def shift(i, layer, chunk0):
                src = area(sq_at[MODS[i]], KD, T)
                for k in range(KD):
                    act.wait_ge(S("nrm"), KD * i + k + 1)
                    seg_add(hT[:, k, :], src[:, k, :], mod[:, layer, chunk0 + k, :]).then_inc(S("hT"), 1)

            def ada(l, b0):
                for b in (b0, b0 + 1):
                    full(act, "adaw", l, b)
                    A_(ada_rows((l, b)), bank("adaw", l, b)[:, :], ACT.Copy).then_inc(taken["act"], 1)

            def ada_after(*name):
                if name in ADA_AFTER:
                    ada(*ADA_AFTER[name])

            for i in range(4):
                full(act, "par", i)
                A_(par[:, i * P:i * P + NROWS[i]], bank("par", i)[:, 0:NROWS[i]], ACT.Copy).then_inc(taken["act"], 1)
            full(act, "par", 4)
            A_(par[:, PAR["ssd_d"]:PAR["ssd_d"] + KD], bank("par", 4)[:, 0:KD], ACT.Copy).then_inc(taken["act"], 1)
            took(act, "par", 4)
            act.wait_ge(S("const"), 1)
            A_(cond[:, 0:2 * KD].rearrange("p (k v) -> p v k", v=2), par[:, 0:2 * KD].rearrange("p (v k) -> p v k", v=2),
               ACT.Silu).then_inc(S("silc"), 1)
            for k in range(KD):
                full(act, "xTr", k)
                A_(xT[:, k, :], bank("xTr", k)[:, 0:T], ACT.Copy).then_inc(taken["act"], 1)
            took(act, "xTr", KD - 1)
            squares("mix0", xT, KD)
            for b in (0, 2):
                ada(0, b)
            root("mix0", D)
            took(act, "ada", 0, 3)
            shift(0, 0, 0)
            for c in range(KD):
                full(act, "z", c)
                A_(szT[:, c, :], bank("z", c)[:, 0:T], ACT.Silu).then_inc(taken["act"], 1)
                ada_after("z", c)
            act.wait_ge(S("dt_abs"), 1)
            A_(dtw[:, 1, :], dtw[:, 1, :], ACT.Exp).then_inc(S("dt_exp"), 1)
            act.wait_ge(S("dt_one"), 1)
            A_(dtw[:, 3, :], dtw[:, 2, :], ACT.Ln).then_inc(S("dt_ln"), 1)
            act.wait_ge(S("dtin"), 16 * 3)
            A_(arow, arow, ACT.Exp).then_inc(S("dt_ln"), 1)
            for c in range(KX + 1):
                if c < KX:
                    if c >= 2:
                        act.wait_ge(S("conv"), c - 1)
                    full(act, "xbc", c)
                    ps = bank("xbc", c)
                    A_(cpad[:, c % 2, PAD:PAD + LP], ps[:, 0:LP], ACT.Copy)
                    A_(cpad[:, c % 2, 2 * PAD + LP:2 * PAD + T], ps[:, LP:T], ACT.Copy).then_inc(taken["act"], 1)
                    ada_after("xbc", c)
                if c:
                    act.wait_ge(S("conv"), c)
                    A_(xbcT[:, c - 1, 0:LP], cacc[:, (c - 1) % 2, 0:LP], ACT.Silu)
                    A_(xbcT[:, c - 1, LP:T], cacc[:, (c - 1) % 2, LP + PAD:T + PAD], ACT.Silu).then_inc(S("xbc"), 1)
            for t in range(NT):
                for half in range(2):
                    full(act, "xtk", t, half)
                    A_(xtok[:, t, half * 512:(half + 1) * 512], bank("xtk", t, half)[:, :], ACT.Copy).then_inc(taken["act"], 1)
                full(act, "btk", t)
                A_(btok[:, t, :], bank("btk", t)[:, 0:2 * STATE], ACT.Copy).then_inc(taken["act"], 1)
            for d in range(2):
                for g in range(2):
                    full(act, "sinit", d, g)
                    A_(sent[:, 3 * d, g * 512:(g + 1) * 512], bank("sinit", d, g)[:, :], ACT.Copy).then_inc(taken["act"], 1)
            for t in range(NT):
                full(act, "wt", t)
                A_(wexp[:, t, :], bank("wt", t)[:, 0:64], ACT.Exp).then_inc(taken["act"], 1)
            for d in range(2):
                for g in range(2):
                    full(act, "st0", d, g)
                    n = 2 * d + g
                    if n:
                        act.wait_ge(S("state_out"), 16 * n)
                    A_(stout, bank("st0", d, g)[:, :].rearrange("p (c n) -> p c n", c=4), ACT.Copy).then_inc(taken["act"], 1)
                    took(act, "st0", d, g)
                    act.dma_start(outs[2][0, 0, d, g * 8:(g + 1) * 8].rearrange("(c h) q n -> (h q) c n", h=2), stout)\
                       .then_inc(S("state_out"), 16)
            act.wait_ge(S("state_out"), 64)
            took(act, "st", 1, 1)
            step = 0
            for t in range(NT):
                for q in range(4):
                    full(act, "E", t, q)
                    if step:
                        act.wait_ge(S("mm"), step)
                    A_(expE.rearrange("p h l -> p (h l)"), bank("E", t, q)[:, :], ACT.Exp).then_inc(taken["act"], 1)
                    if t:
                        if step > 4:
                            full(act, "y", *divmod(step - 1, 4))
                        for d, ct in enumerate((ctf, ctb)):
                            full(act, "cs", t, q, d)
                            A_(ct.rearrange("p h l -> p (h l)"), bank("cs", t, q, d)[:, :], ACT.Exp).then_inc(taken["act"], 1)
                    step += 1
            act.wait_ge(S("yz"), 12)
            for k in range(KD):
                A_(area(sq_at["ssd"], KD, T)[:, k, :], szT[:, k, :], ACT.Square).then_inc(S("sq"), 1)
            root("ssd", D)
            for c in range(3 * KD):
                if c == 0:
                    act.wait_ge(S("hpad0"), 1)
                if c >= 2:
                    act.wait_ge(S("hconv"), c - 1)
                full(act, "hy", c // KD, c % KD)
                ps = bank("hy", c // KD, c % KD)
                A_(hpad[:, c % 2, 1:1 + LP], ps[:, 0:LP], ACT.Copy)
                A_(hpad[:, c % 2, 2 + LP:2 + T], ps[:, LP:T], ACT.Copy).then_inc(taken["act"], 1)
                ada_after("hy", c // KD, c % KD)
            for i in range(2):
                act.wait_ge(S("farg"), i + 1)
                dst = h1[0:HY_HID, :] if i == 0 else hsP
                src = farg[0:HY_HID, :] if i == 0 else farg
                A_(dst, src, ACT.Sin).then_inc(S("fsin"), 1)
            for b in range(2):
                for o in range(2):
                    for t in range(NT):
                        full(act, "utk", b, o, t)
                        if (b, o) != (0, 0):
                            pb, po = (b, 0) if o else (0, 1)
                            full(act, "U", pb, po, 1, 1, 1)
                        A_(ut[:, t, :], bank("utk", b, o, t)[:, :], ACT.Copy).then_inc(taken["act"], 1)
                    for s in range(2):
                        for k in range(s + 1):
                            full(act, "H", b, o, s, k, 1)
                            if (b, o) != (0, 0):
                                act.wait_ge(S("spec"), 3 * (2 * b + o))
                            A_(hh[s][1][:, k, :], bank("H", b, o, s, k, 1)[:, :], ACT.Copy).then_inc(taken["act"], 1)

            def moe(l):
                squares("ffn%d" % l, xT, KD, "wout" if l == 0 else "odout")
                root("ffn%d" % l, D)
                took(act, "ada", l, 11)
                shift(1 + 2 * l, l, 24)
                for t in range(NT):
                    for h in range(2):
                        full(act, "htk", l, t, h)
                        A_(htok[:, t, h * 512:(h + 1) * 512], bank("htk", l, t, h)[:, :], ACT.Copy).then_inc(taken["act"], 1)
                    took(act, "htk", l, t, 1)
                    act.dma_start(rows_d[l][t * P:(t + 1) * P, :], htok[:, t, :]).then_inc(S("rows_out"), 16)
                act.wait_ge(S("gl"), l + 1)
                A_(rsc_g, rsc_g, ACT.Exp).then_inc(S("ge"), 1)
                act.wait_ge(S("el"), l + 1)
                A_(rsc_e, rsc_e, ACT.Exp).then_inc(S("ee"), 1)
                r = trips(act, l)
                s = {x: S("%s%d" % (x, l)) for x in
                     ("x_ps", "x_act", "x_dve", "gu_done", "silu", "hid", "ht_done", "ht_act", "down_done", "d_act", "d_dve")}

                def take_rows(n, b):
                    act.wait_ge(s["x_ps"], n + 1)
                    A_(xsT[:, b, 0:512], banks[0][:, :], ACT.Copy).then_inc(s["x_act"], 1)

                def take_gate(n, b):
                    act.wait_ge(s["gu_done"], n + 1)
                    if not (isinstance(n, int) and n < 2):
                        act.wait_ge(s["hid"], n - 1)
                    A_(sg[:, b, :], banks[2 + b][:, 0:HID], ACT.Silu).then_inc(s["silu"], 1)

                def take_hidden(n, b):
                    act.wait_ge(s["ht_done"], n + 1)
                    if not (isinstance(n, int) and n < 2):
                        act.wait_ge(s["down_done"], n - 1)
                    A_(hidT[:, b, :], banks[4][:, 0:HID], ACT.Copy).then_inc(s["ht_act"], 1)

                def take_down(n, b, stored):
                    act.wait_ge(s["down_done"], n + 1)
                    act.wait_ge(S("stored%d_%d" % (l, b)), stored)
                    A_(ob[:, b, 0:512], banks[5][:, :], ACT.Copy).then_inc(s["d_act"], 1)

                take_rows(0, 0)
                take_gate(0, 0)
                take_rows(1, 1)
                take_hidden(0, 0)
                with act.Fori(0, r - 1) as i:
                    for b in range(2):
                        n = 2 * i + 1 + b
                        take_gate(n, 1 - b)
                        take_down(n - 1, b, 16 * i)
                        take_rows(n + 1, b)
                        take_hidden(n, 1 - b)
                n = 2 * r - 1
                take_gate(n, 1)
                take_down(n - 1, 0, 16 * (r - 1))
                take_hidden(n, 1)
                take_down(n, 1, 16 * (r - 1))

            moe(0)
            squares("mix1", xT, KD, "yTr", 0)
            root("mix1", D)
            took(act, "ada", 1, 11)
            shift(2, 1, 0)
            for c in range(8):
                full(act, "qk", c)
                A_(qkT[:, c, :], bank("qk", c)[:, 0:T], ACT.Copy).then_inc(taken["act"], 1)
            for t in range(NT):
                full(act, "v", t)
                A_(vtok[:, t, :], bank("v", t)[:, :], ACT.Copy).then_inc(taken["act"], 1)
            for c in range(4):
                m = QK if c == 3 else P
                full(act, "lat", c)
                A_(latT[0:m, c, :], bank("lat", c)[0:m, 0:T], ACT.Copy).then_inc(taken["act"], 1)
            full(act, "ktok")
            A_(ktok, bank("ktok")[:, :], ACT.Copy).then_inc(taken["act"], 1)
            full(act, "kctx")
            A_(kcT[:, :, :], bank("kctx")[:, :].rearrange("p (c n) -> p c n", c=4), ACT.Copy).then_inc(taken["act"], 1)
            took(act, "kctx")
            act.dma_start(outs[3][0, 0].rearrange("h t c -> t h c"), ktok.rearrange("p (h c) -> p h c", h=AH)).then_inc(S("cache_out"), 16)
            act.dma_start(outs[4][0, 0].rearrange("h t c -> t h c"), vtok[:, 0, :].rearrange("p (h c) -> p h c", h=AH)).then_inc(S("cache_out"), 16)

            def heads(kind, scale, chunk0, first):
                def exps(n):
                    b = n % 3
                    sc = ncsc[b][:, 0:(1 if TURNS[n][0] == "p" else 3) * P]
                    act.wait_ge(S("negm"), first + n + 1)
                    A_(sc, sc, ACT.Exp, bias=nrows[:, b, 0:1], scale=scale, accum_out=nrows[:, b, 1:2]).then_inc(S("expd"), 1)

                def take_turned(n, i, h):
                    b = n % 2
                    nk = 1 if i == "p" else 3
                    full(act, kind + "t", i, h)
                    if n >= 2:
                        full(act, kind + "o", *TURNS[n - 2])
                    A_(npt[:, b, 0:nk * P], bank(kind + "t", i, h)[:, 0:nk * P], ACT.Copy).then_inc(taken["act"], 1)

                def take_mixed(i, h):
                    full(act, kind + "o", i, h)
                    hp = slice((h % 2) * AD, (h % 2 + 1) * AD)
                    q0 = 0 if i == "p" else LP + i * P
                    A_(oT[hp, chunk0 + h // 2, q0:q0 + P], bank(kind + "o", i, h)[hp, 0:P], ACT.Copy).then_inc(taken["act"], 1)

                for n in range(-2, len(TURNS) + 1):
                    if 0 <= n < len(TURNS):
                        take_turned(n, *TURNS[n])
                    if n >= 1:
                        take_mixed(*TURNS[n - 1])
                    if n + 2 < len(TURNS):
                        exps(n + 2)

            heads("na", AD ** -0.5, 0, 0)
            act.wait_ge(S("cache_out"), 32)
            squares("q", latT, 2)
            A_(area(sq_at["kv"], T), latT[:, 2, :], ACT.Square).then_inc(S("sq"), 1)
            root("q", QR)
            full(act, "ss", "kv")
            A_(rkv, bank("ss", "kv")[:, 0:T], ACT.Sqrt, bias=eps[:, 0:1], scale=1.0 / P).then_inc(taken["act"], 1)
            full(act, "mctx")
            A_(ckvT[:, T:T + P], bank("mctx")[:, 0:P], ACT.Copy)
            for h in range(AH):
                last = A_(kmT[AD:QK, h, T:T + P], bank("mctx")[AD:QK, P:2 * P], ACT.Copy)
            last.then_inc(taken["act"], 1)
            full(act, "ckvtok")
            A_(ckto, bank("ckvtok")[:, 0:P], ACT.Copy)
            A_(krto, bank("ckvtok")[:, P:P + QK], ACT.Copy).then_inc(taken["act"], 1)
            took(act, "ckvtok")
            act.dma_start(outs[5][0, 0], ckto).then_inc(S("cache_out"), 16)
            act.dma_start(outs[6][0, 0], krto[:, AD:QK]).then_inc(S("cache_out"), 16)
            for h in range(AH):
                full(act, "qm", h)
                A_(qmT[0:QK, h, :], bank("qm", h)[0:QK, 0:T], ACT.Copy).then_inc(taken["act"], 1)
                full(act, "km", h)
                A_(kmT[0:AD, h, :], bank("km", h)[0:AD, :], ACT.Copy).then_inc(taken["act"], 1)
            for t in range(4):
                full(act, "vm", t)
                A_(vm[:, t, :], bank("vm", t)[:, :], ACT.Copy).then_inc(taken["act"], 1)
            heads("ml", QK ** -0.5, 4, len(TURNS))
            moe(1)
            squares("final", xT, KD, "yTr", 1)
            root("final", D)
            for t in range(NT):
                for h in range(2):
                    full(act, "out", t, h)
                    A_(fino[:, t, h * 512:(h + 1) * 512], bank("out", t, h)[:, :], ACT.Copy).then_inc(taken["act"], 1)
                took(act, "out", t, 1)
                dst = outs[0][0] if t == 0 else outs[1][0, (t - 1) * P:t * P, :]
                act.dma_start(dst, fino[:, t, :]).then_inc(S("y_out"), 16)
            act.wait_ge(S("y_out"), 16 * NT)
            act.wait_ge(S("cache_out"), 64)

        @block.vector
        def _(dve):
            TT, TS, STT = nc.vector.tensor_tensor, nc.vector.tensor_scalar, nc.vector.scalar_tensor_tensor
            COPY, RED = nc.vector.tensor_copy, nc.vector.tensor_reduce
            link = Chain(dve, "dve_chain")
            mult, add, sub = ALU.mult, ALU.add, ALU.subtract

            def col(name, i):
                return par[:, PAR[name] + i:PAR[name] + i + 1]

            def take(ins):
                ins.then_inc(taken["dve"], 1)

            def over(ap, n, last=True):
                if last:
                    return ap.unsqueeze(len(ap.shape)).to_broadcast(list(ap.shape) + [n])
                return ap.unsqueeze(1).to_broadcast([ap.shape[0], n] + list(ap.shape[1:]))

            def ada(l, b0):
                for b in (b0, b0 + 1):
                    full(dve, "ada", l, b)
                    bias = par[:, PAR["b_ada"] + l * 48 + 4 * b:PAR["b_ada"] + l * 48 + 4 * b + 4]
                    take(TT(mod[:, l, 4 * b:4 * b + 4, :], bank("ada", l, b)[:, 0:8].rearrange("p (m v) -> p m v", v=2),
                            over(bias, 2), add))

            def ada_after(*name):
                if name in ADA_AFTER:
                    ada(*ADA_AFTER[name])

            def gain(i, l, name, chunk0, last_block):
                took(dve, "ada", l, last_block)
                g = par[:, PAR[name] + l * KD:PAR[name] + (l + 1) * KD]
                link(STT(out=gmod[:, i, :, :], in0=mod[:, l, chunk0:chunk0 + KD, :], scalar=1.0, in1=over(g, 2),
                         op0=add, op1=mult))

            def norm(i):
                which = MODS[i]
                took(dve, "ss", which)
                link(nc.vector.reciprocal(rstd, rstd))
                dst = area(sq_at[which], KD, T)
                for k in range(KD):
                    for v, (a, b) in enumerate(SEGS):
                        last = STT(out=dst[:, k, a:b], in0=xT[:, k, a:b], scalar=gmod[:, i, k, v:v + 1], in1=rstd[:, a:b],
                                   op0=mult, op1=mult)
                    last.then_inc(S("nrm"), 1)

            def add_gated(name, l, chunk0):
                for m in range(KD):
                    full(dve, *name, m)
                    for v, (a, b) in enumerate(SEGS):
                        last = STT(out=xT[:, m, a:b], in0=bank(*name, m)[:, a:b], scalar=mod[:, l, chunk0 + m, v:v + 1],
                                   in1=xT[:, m, a:b], op0=mult, op1=add)
                    take(last)

            nc.vector.memset(eps[:, :], EPS)
            nc.vector.memset(cond[:, 2 * KD:], 0.0)
            nc.vector.memset(cpad, 0.0).then_inc(S("const"), 1)
            dve.wait_ge(S("d2_in"), 16)
            COPY(d8[0:KD, :].rearrange("c (h r) -> c h r", h=2), over(d2[0:KD, :], HDIM)).then_inc(S("d8"), 1)
            took(dve, "par", 3)
            dve.wait_ge(S("small_in"), 16)
            for b in (0, 2):
                ada(0, b)
            gain(0, 0, "norm_mix", 8, 3)
            norm(0)
            for c in range(KD):
                ada_after("z", c)
            full(dve, "dt")
            dve.wait_ge(S("dtin"), 16 * 3)
            dps = bank("dt")[:, 0:NT * HEADS].rearrange("p (t h) -> p t h", t=NT)
            for d in range(2):
                last = TT(dtw[:, 0, d * 48:(d + 1) * 48].rearrange("p (t h) -> p t h", t=NT), dps, over(brow[:, d, :], NT, False), add)
            take(last)
            took(dve, "dt")
            STT(out=dtw[:, 1, :], in0=dtw[:, 0, :], scalar=-1.0, in1=dtw[:, 0, :], op0=mult, op1=ALU.min).then_inc(S("dt_abs"), 1)
            dve.wait_ge(S("dt_exp"), 1)
            TS(dtw[:, 2, :], dtw[:, 1, :], 1.0, None, add).then_inc(S("dt_one"), 1)
            dve.wait_ge(S("dt_one"), 1)
            link(TS(dtw[:, 4, :], dtw[:, 2, :], -1.0, None, add))
            link(TT(dtw[:, 5, :], dtw[:, 1, :], dtw[:, 4, :], sub))
            dve.wait_ge(S("dt_ln"), 2)
            link(TT(dtw[:, 5, :], dtw[:, 5, :], dtw[:, 3, :], add))
            link(STT(out=dts.rearrange("p d t h -> p (d t h)"), in0=dtw[:, 0, :], scalar=0.0, in1=dtw[:, 5, :], op0=ALU.max, op1=add))
            for d in range(2):
                last = STT(out=dta[:, :, d, :], in0=dts[:, d, :, :], scalar=-1.0, in1=over(arow[:, d, :], NT, False), op0=mult, op1=mult)
            last.then_inc(S("dta"), 1)
            n = T + PAD
            for c in range(KX):
                took(dve, "xbc", c)
                if c >= 2:
                    dve.wait_ge(S("xbc"), c - 1)
                src, acc = cpad[:, c % 2, :], cacc[:, c % 2, 0:n]
                link(TS(acc, src[:, 0:n], col("ev_conv_w", c), col("ev_conv_b", c), mult, add))
                for k in range(1, TAPS):
                    last = STT(out=acc, in0=src[:, k:k + n], scalar=col("ev_conv_w", k * KX + c), in1=acc, op0=mult, op1=add)
                    if k < TAPS - 1:
                        link(last)
                last.then_inc(S("conv"), 1)
                ada_after("xbc", c)
            for t in range(NT):
                took(dve, "wt", t)
                for d in range(2):
                    last = TT(wsc[:, t, d, :], wexp[:, t, d * HEADS:(d + 1) * HEADS], dts[:, d, t, :], mult)
                link(last)
            for i, (t, d) in enumerate(((0, 0), (0, 1), (1, 0), (2, 1))):
                if i:
                    full(dve, *(("st0", i - 1, 1) if i < 3 else ("st", 0, 1)))
                TT(xw.rearrange("p (h c) -> p h c", h=HEADS), xtok[:, t, :].rearrange("p (h c) -> p h c", h=HEADS),
                   over(wsc[:, t, d, :], HDIM), mult).then_inc(S("xw"), 1)
                if i < 2:
                    continue
                d = i - 2
                src, dst, t = ((0, 1, 1), (3, 2, 2))[d]
                took(dve, "sinit", d, 1)
                for g in range(2):
                    gs = slice(g * 512, (g + 1) * 512)
                    tot = wexp[:, t, 32 + d * HEADS + g * 8:32 + d * HEADS + g * 8 + 8]
                    link(TT(sent[:, dst, gs].rearrange("p (h c) -> p h c", h=8), sent[:, src, gs].rearrange("p (h c) -> p h c", h=8),
                            over(tot, HDIM), mult))
                for g in range(2):
                    gs = slice(g * 512, (g + 1) * 512)
                    full(dve, "st", d, g)
                    take(TT(sent[:, dst, gs], sent[:, dst, gs], bank("st", d, g)[:, :], add))
            took(dve, "st", 1, 1)
            dve.wait_ge(S("state_out"), 64)
            def chunk_scores(t):
                full(dve, "cb", t)
                cps = bank("cb", t)[:, 0:2 * P].rearrange("p (g l) -> p g l", g=2)
                TT(cbf, cps, over(upto, 2, False), mult)
                take(TT(cbb, cps, over(since, 2, False), mult))
                took(dve, "cb", t)

            def weigh(step, t, q):
                hs, mdec = slice(4 * q, 4 * q + 4), mdecs[step % 2]
                TT(mdec, over(cbf[:, q // 2, :], 4, False), over(dts[:, 0, t, hs], P), mult)
                link(TT(m2, over(cbb[:, q // 2, :], 4, False), over(dts[:, 1, t, hs], P), mult))
                link(TT(mdec, mdec, m2, add))

            chunk_scores(0)
            weigh(0, *QUADS[0])
            for step, (t, q) in enumerate(QUADS):
                tt = slice(t * P, (t + 1) * P)
                took(dve, "E", t, q)
                TT(mdecs[step % 2], mdecs[step % 2], expE, mult).then_inc(S("mm"), 1)
                if t:
                    for d, ct in enumerate((ctf, ctb)):
                        took(dve, "cs", t, q, d)
                        TT(ct, ct, over(xbcT[:, KD + 2 + q // 2, tt], 4, False), mult).then_inc(S("ctd"), 1)
                if q == 3 and t + 1 < NT:
                    chunk_scores(t + 1)
                if step + 1 < len(QUADS):
                    weigh(step + 1, *QUADS[step + 1])
                full(dve, "y", t, q)
                for j in range(2):
                    last = STT(out=m2[:, j, :], in0=xbcT[:, 2 * q + j, tt], scalar=par[:, PAR["ssd_d"] + 2 * q + j:PAR["ssd_d"] + 2 * q + j + 1],
                               in1=bank("y", t, q)[:, j * P:(j + 1) * P], op0=mult, op1=add)
                take(last)
                took(dve, "y", t, q)
                TT(szT[:, 2 * q:2 * q + 2, tt], szT[:, 2 * q:2 * q + 2, tt], m2[:, 0:2, :], mult).then_inc(S("yz"), 1)
                dve.wait_ge(S("yz"), step + 1)
            took(dve, "ss", "ssd")
            link(nc.vector.reciprocal(rstd, rstd))
            for k in range(KD):
                STT(out=szT[:, k, :], in0=szT[:, k, :], scalar=col("ssd_norm", k), in1=rstd, op0=mult, op1=mult).then_inc(S("yn"), 1)
            nc.vector.memset(hpad, 0.0).then_inc(S("hpad0"), 1)
            n = T + 1
            for c in range(3 * KD):
                q, k = divmod(c, KD)
                took(dve, "hy", q, k)
                src, acc = hpad[:, c % 2, :], hacc[:, c % 2, 0:n]
                dst = (u0T, p1T, hyT)[q][:, k, :]
                link(TS(acc, src[:, 0:n], col("hy_conv_w", c), col("hy_conv_b", c), mult, add))
                link(STT(out=acc, in0=src[:, 1:1 + n], scalar=col("hy_conv_w", 3 * KD + c), in1=acc, op0=mult, op1=add))
                for v, (a, b) in enumerate(SEGS):
                    last = STT(out=dst[:, a:b], in0=src[:, 2 + a + v:2 + b + v], scalar=col("hy_conv_w", 6 * KD + c),
                               in1=acc[:, a + v:b + v], op0=mult, op1=add)
                last.then_inc(S("hconv"), 1)
                ada_after("hy", q, k)
            two_pi_hi = float(np.float32(6.28125))
            two_pi_lo = 2.0 * math.pi - two_pi_hi
            magic = 12582912.0
            for i in range(2):
                m = HY_HID if i == 0 else P
                a, k = farg[0:m, :], fk[0:m, :]
                full(dve, "f", i)
                if i:
                    dve.wait_ge(S("fsin"), 1)
                dve.wait_ge(S("hyc_in"), 16 * 11)
                take(TS(a, bank("f", i)[0:m, 0:T], fpar[0:m, 2 * i:2 * i + 1], fpar[0:m, 2 * i + 1:2 * i + 2], add, mult))
                took(dve, "f", i)
                link(TS(k, a, 1.0 / (2.0 * math.pi), magic, mult, add))
                link(TS(k, k, -magic, None, add))
                link(STT(out=a, in0=k, scalar=-two_pi_hi, in1=a, op0=mult, op1=add))
                link(STT(out=a, in0=k, scalar=-two_pi_lo, in1=a, op0=mult, op1=add))
                TS(a, a, 3.1415925, -3.1415925, ALU.min, ALU.max).then_inc(S("farg"), 1)
            dve.wait_ge(S("fsin"), 2)
            nc.vector.memset(hsP[HY_HID:P, 0:1], 0.0)
            link(nc.vector.memset(hsP[HY_HID:P, LP:LP + 1], 0.0))
            TS(hsQ, hsP, sgn[:, 0:1], None, mult).then_inc(S("hs"), 1)
            dve.wait_ge(S("hypar_in"), 16 * HY_LOADS)
            for b in range(2):
                for o in range(2):
                    for s in range(2):
                        for x in range(2):
                            for t in range(s + 1):
                                full(dve, "PQ", b, o, s, x, t)
                                take(TT(pq[s][:, x, t, :], bank("PQ", b, o, s, x, t)[:, :], decay[b][:, s + t, :], mult))
                    for s in range(2):
                        for k in range(s + 1):
                            full(dve, "H", b, o, s, k, 0)
                            take(TT(hh[s][0][:, k, :], bank("H", b, o, s, k, 0)[:, :], hyb[:, b, o, :], add))
                    for s in range(2):
                        for k in range(s + 1):
                            took(dve, "H", b, o, s, k, 0)
                            took(dve, "H", b, o, s, k, 1)
                            full(dve, "U", b, o, s, k, 1)
                            ure, uim = bank("U", b, o, s, k, 0)[:, :], bank("U", b, o, s, k, 1)[:, :]
                            hre, him = hh[s][0][:, k, :], hh[s][1][:, k, :]
                            yre, yim = pq[s][:, 0, k, :], pq[s][:, 1, k, :]
                            TT(yre, ure, hre, mult)
                            link(TT(ytmp[:, :], uim, him, mult))
                            TT(yre, yre, ytmp[:, :], sub)
                            link(TT(yim, ure, him, mult))
                            take(TT(ytmp[:, :], uim, hre, mult))
                            took(dve, "U", b, o, s, k, 1)
                            TT(yim, yim, ytmp[:, :], add).then_inc(S("spec"), 1)
                            dve.wait_ge(S("spec"), 3 * (2 * b + o) + s + k + 1)
                    for s in range(2):
                        a0, a1 = SEGS[s]
                        for c in range(4):
                            full(dve, "inv", b, o, s, c)
                            dst = (p1T if o == 0 else hyT)[:, b * 4 + c, a0:a1]
                            take(TT(dst, dst, bank("inv", b, o, s, c)[:, 0:(s + 1) * P], mult))
            add_gated(("wout",), 0, 16)

            def first_of(out, values, top, n):
                v = rsc[:, 1200:1200 + NT * n].rearrange("p (t n) -> p t n", t=NT)
                m = rsc[:, 1300:1300 + NT]
                link(TT(v, values, over(top, n), ALU.is_ge))
                link(TT(v, v, over(tie[:, 0:n], NT, False), mult))
                link(RED(m, v, AX_X, ALU.max))
                link(TT(out, v, over(m, n), ALU.is_equal))

            def moe(l):
                gain(1 + 2 * l, l, "norm_ffn", 32, 11)
                norm(1 + 2 * l)
                full(dve, "rt", l)
                lg = rsc[:, 0:108].rearrange("p (t n) -> p t n", t=NT)
                gl, el = lg[:, :, 0:NG], lg[:, :, NG:NG + E]
                go = rsc[:, 120:132].rearrange("p (t g) -> p t g", t=NT)
                gm_, gs_, m1, m2_, w_ = (rsc[:, 140 + 4 * i:140 + 4 * i + NT] for i in range(5))
                dve.wait_ge(S("router_in%d" % l), 16 * 5)
                rps = bank("rt", l)[:, 0:120].rearrange("p (t n) -> p t n", t=NT)[:, :, 0:NG + E]
                take(TT(lg, rps, over(rbias, NT, False), add))
                took(dve, "rt", l)
                link(RED(gm_, gl, AX_X, ALU.max))
                TT(rsc_g.rearrange("p (t g) -> p t g", t=NT), gl, over(gm_, NG), sub).then_inc(S("gl"), 1)
                first_of(go, gl, gm_, NG)
                pr = rsc[:, 200:296].rearrange("p (t g j) -> p t g j", t=NT, g=NG)
                for t in range(NT):
                    last = TT(pr[:, t], el[:, t, :].rearrange("p (g j) -> p g j", g=NG), over(go[:, t, :], PERG), mult)
                link(last)
                es = rsc[:, 300:324].rearrange("p (t j) -> p t j", t=NT)
                o1 = rsc[:, 330:354].rearrange("p (t j) -> p t j", t=NT)
                o2 = rsc[:, 360:384].rearrange("p (t j) -> p t j", t=NT)
                e2 = rsc[:, 390:414].rearrange("p (t j) -> p t j", t=NT)
                link(RED(es, pr.rearrange("p t g j -> p t j g"), AX_X, add))
                link(RED(m1, es, AX_X, ALU.max))
                first_of(o1, es, m1, PERG)
                link(STT(out=e2, in0=o1, scalar=-BIG, in1=es, op0=mult, op1=add))
                link(RED(m2_, e2, AX_X, ALU.max))
                TT(rsc_e, m2_, m1, sub).then_inc(S("el"), 1)
                first_of(o2, e2, m2_, PERG)
                ohs = rsc[:, 420:612].rearrange("p (c t e) -> p c t e", c=2, t=NT)
                for c, o in enumerate((o1, o2)):
                    for t in range(NT):
                        last = TT(ohs[:, c, t, :].rearrange("p (g j) -> p g j", g=NG), over(go[:, t, :], PERG),
                                  over(o[:, t, :], NG, False), mult)
                link(last)
                TT(rmask, ohs[:, 0], ohs[:, 1], add).then_inc(S("chosen"), 1)
                for c in range(2):
                    STT(out=rtok[:, c, :, :, 0], in0=over(tilestart, E), scalar=float(T * c), in1=ohs[:, c], op0=add, op1=mult)
                    last = TS(rtok[:, c, :, :, 1], ohs[:, c], tokin[:, 0:1], None, mult)
                link(last)
                dve.wait_ge(S("ge"), l + 1)
                link(RED(gs_, rsc_g.rearrange("p (t g) -> p t g", t=NT), AX_X, add))
                dve.wait_ge(S("ee"), l + 1)
                link(TS(w_, rsc_e, 1.0, None, add))
                link(TT(w_, w_, gs_, mult))
                link(nc.vector.reciprocal(ysw[:, 0:NT], w_))
                link(TT(ysw[:, NT:2 * NT], ysw[:, 0:NT], rsc_e, mult))
                full(dve, "pos", l)
                pps = bank("pos", l)[:, 0:NT * E].rearrange("p (t e) -> p t e", t=NT)
                pp = rsc[:, 620:812].rearrange("p (c t e) -> p c t e", c=2, t=NT)
                posn = rsc[:, 820:826]
                cm, cmp_ = rsc[:, 860:861], rsc[:, 862:868]
                link(RED(cm, bank("pos", l)[:, NT * E:(NT + 1) * E], AX_X, ALU.max))
                for c in range(2):
                    last = TT(pp[:, c], pps, ohs[:, c], mult)
                take(last)
                took(dve, "pos", l)
                link(TS(cmp_, thr, cm, float(PAIRS // 2), ALU.is_lt, mult))
                link(RED(cm, cmp_[:, 1:ROUNDS], AX_X, add))
                COPY(counti[:, :], cm).then_inc(S("trips%d" % l), 1)
                link(RED(posn.rearrange("p (c t) -> p c t", c=2), pp, AX_X, add))
                for c in range(2):
                    if c:
                        dve.wait_ge(S("tbl0"), l + 1)
                    for t in range(NT):
                        last = TS(onehot[:, t, :], slotrow, posn[:, c * NT + t:c * NT + t + 1], None, ALU.is_equal)
                    last.then_inc(S("onehot"), 1)
                full(dve, "tbl", l)
                tb, tb2 = rsc[:, 900:996], rsc[:, 1400:1496]
                tps = bank("tbl", l)[:, 0:384].rearrange("p (c r x) -> p c r x", c=2, x=2)
                link(RED(tb, tps[:, 0], AX_X, add))
                take(RED(tb2, tps[:, 1], AX_X, add))
                took(dve, "tbl", l)
                link(TT(tb, tb, tb2, add))
                empty, sf = rsc[:, 1200:1296], rsc[:, 1300:1396]
                link(TS(empty, tb, 0.0, 4096.0, ALU.is_equal, mult))
                link(STT(out=sf, in0=tb, scalar=-1.0, in1=empty, op0=add, op1=add))
                COPY(scati, sf)
                link(TS(empty, tb, float(T + 1), -float(T), ALU.is_ge, mult))
                link(TT(sf, sf, empty, add))
                COPY(tbli, sf).then_inc(S("table"), 1)
                r = trips(dve, l)
                s = {x: S("%s%d" % (x, l)) for x in
                     ("x_ps", "x_act", "x_dve", "gu_done", "silu", "hid", "ht_done", "ht_act", "down_done", "d_act", "d_dve")}

                def take_rows(n, b):
                    dve.wait_ge(s["x_ps"], n + 1)
                    COPY(xsT[:, b, 512:1024], banks[1][:, :]).then_inc(s["x_dve"], 1)

                def take_up(n, b):
                    dve.wait_ge(s["silu"], n + 1)
                    if not (isinstance(n, int) and n < 2):
                        dve.wait_ge(s["ht_done"], n - 1)
                    TT(hid[:, b, :], sg[:, b, :], banks[2 + b][:, HID:2 * HID], mult).then_inc(s["hid"], 1)

                def take_down(n, b, stored):
                    dve.wait_ge(s["down_done"], n + 1)
                    dve.wait_ge(S("stored%d_%d" % (l, b)), stored)
                    COPY(ob[:, b, 512:1024], banks[6][:, :]).then_inc(s["d_dve"], 1)

                take_rows(0, 0)
                take_up(0, 0)
                take_rows(1, 1)
                with dve.Fori(0, r - 1) as i:
                    for b in range(2):
                        n = 2 * i + 1 + b
                        take_up(n, 1 - b)
                        take_down(n - 1, b, 16 * i)
                        take_rows(n + 1, b)
                n = 2 * r - 1
                take_up(n, 1)
                take_down(n - 1, 0, 16 * (r - 1))
                take_down(n, 1, 16 * (r - 1))
                for t in range(NT):
                    dve.wait_ge(S("yg%d" % t), 16 * (l + 1))
                    link(TS(yc[:, t, :], yg[t][:, 0, :], ysw[:, t:t + 1], None, mult))
                    STT(out=yc[:, t, :], in0=yg[t][:, 1, :], scalar=ysw[:, NT + t:NT + t + 1], in1=yc[:, t, :], op0=mult, op1=add)\
                        .then_inc(S("yc"), 1)
                add_gated(("yTr", l), l, 40)

            def heads(kind, scale, first):
                def scores(n):
                    i, h = TURNS[n]
                    b = n % 3
                    nk = 1 if i == "p" else 3
                    full(dve, kind, i, h)
                    if n >= 3:
                        full(dve, kind + "t", *TURNS[n - 3])
                    ps = bank(kind, i, h)
                    if kind == "na" and i != "p":
                        TT(ncsc[b][:, 0:LS], ps[:, 0:LS], nmask[:, i, :], add)
                        take(COPY(ncsc[b][:, LS:T], ps[:, LS:T]))
                    else:
                        take(COPY(ncsc[b][:, 0:nk * P], ps[:, 0:nk * P]))
                    took(dve, kind, i, h)
                    link(RED(nrows[:, b, 2:3], ncsc[b][:, 0:nk * P], AX_X, ALU.max))
                    TS(nrows[:, b, 0:1], nrows[:, b, 2:3], -scale, None, mult).then_inc(S("negm"), 1)

                def normalise(n):
                    b = n % 3
                    nk = 1 if TURNS[n][0] == "p" else 3
                    dve.wait_ge(S("expd"), first + n + 1)
                    link(nc.vector.reciprocal(nrows[:, b, 3:4], nrows[:, b, 1:2]))
                    TS(ncsc[b][:, 0:nk * P], ncsc[b][:, 0:nk * P], nrows[:, b, 3:4], None, mult).then_inc(S("prob"), 1)

                for n in range(-2, len(TURNS)):
                    if n >= 0:
                        normalise(n)
                    if n + 2 < len(TURNS):
                        scores(n + 2)

            moe(0)
            gain(2, 1, "norm_mix", 8, 11)
            norm(2)
            dve.wait_ge(S("nactx_in"), 16 * 5)
            heads("na", AD ** -0.5, 0)
            took(dve, "lat", 3)
            took(dve, "nao", 1, AH - 1)
            cos, sin = rope[AD:QK, 0, :], rope[AD:QK, 1, :]
            kr = latT[AD:QK, 3, LP:T]
            link(nc.vector.stream_shuffle(krot[AD:QK, :], kr, SWAP))
            TT(krot[AD:QK, :], krot[AD:QK, :], sin, mult)
            link(TT(kr, kr, cos, mult))
            link(TT(kr, kr, krot[AD:QK, :], add))
            full(dve, "nao", 1, AH - 1)
            dve.wait_ge(S("cache_out"), 32)
            COPY(kmT[AD:QK, :, 0:T], over(latT[AD:QK, 3, :], AH, False)).then_inc(S("roped"), 1)
            took(dve, "ss", "q")
            link(nc.vector.reciprocal(rstd, rstd))
            for k in range(2):
                STT(out=latT[:, k, :], in0=latT[:, k, :], scalar=col("mla_q_norm", k), in1=rstd, op0=mult, op1=mult).then_inc(S("qn"), 1)
            took(dve, "ss", "kv")
            link(nc.vector.reciprocal(rkv, rkv))
            STT(out=ckvT[:, 0:T], in0=latT[:, 2, :], scalar=col("mla_kv_norm", 0), in1=rkv, op0=mult, op1=mult).then_inc(S("ckvn"), 1)
            took(dve, "qm", AH - 1)
            qr = qmT[AD:QK, :, LP:T]
            qrv = qrot[AD:QK, :].rearrange("p (h n) -> p h n", h=AH)
            for h in range(AH):
                last = nc.vector.stream_shuffle(qrv[:, h, :], qr[:, h, :], SWAP)
            link(last)
            TT(qrv, qrv, over(sin, AH, False), mult)
            link(TT(qr, qr, over(cos, AH, False), mult))
            TT(qr, qr, qrv, add).then_inc(S("roped"), 1)
            heads("ml", QK ** -0.5, len(TURNS))
            add_gated(("odout",), 1, 16)
            moe(1)
            took(dve, "ss", "final")
            link(nc.vector.reciprocal(rstd, rstd))
            for k in range(KD):
                STT(out=hT[:, k, :], in0=xT[:, k, :], scalar=col("norm_final", k), in1=rstd, op0=mult, op1=mult).then_inc(S("fin"), 1)

        @block.gpsimd
        def _(pool):
            dma = pool.dma_start
            dma(small[:, 0:-1], K["k_small"]).then_inc(S("small_in"), 16)
            with nc.allow_non_contiguous_dma(reason="a few small parameters"):
                dma(d2[0:KD, :], A["ssd_d"][0].rearrange("(c h) -> c h", h=2)).then_inc(S("d2_in"), 16)
            dma(wdtt, A["ev_w_in"][0, :, COL_DT:COL_DT + HEADS].rearrange("(k p) n -> p k n", p=P)).then_inc(S("dtin"), 16)
            dma(brow, A["ssd_dt_bias"][0].partition_broadcast(P)).then_inc(S("dtin"), 16)
            dma(arow, A["ssd_A_log"][0].partition_broadcast(P)).then_inc(S("dtin"), 16)
            full(pool, "par", 4)
            for d in range(2):
                dma(stok[d], A["state_ssd"][0, 0, d].rearrange("(c h) q n -> (h q) c n", h=2)).then_inc(S("sinit_in%d" % d), 16)
            full(pool, "st", 1, 1)
            step = 0
            for t in range(NT):
                for q in range(4):
                    if step:
                        pt, pq_ = divmod(step - 1, 4)
                        full(pool, *(("cs", pt, pq_, 1) if pt else ("E", pt, pq_)))
                    for d, (dst, m) in enumerate(((rf, upto), (rb, since))):
                        nc.gpsimd.tensor_tensor(dst, m.unsqueeze(1).to_broadcast([P, 4, P]),
                                                dta[:, t, d, 4 * q:4 * q + 4].unsqueeze(2).to_broadcast([P, 4, P]), ALU.mult)\
                            .then_inc(S("rfb"), 1)
                    step += 1
            full(pool, "y", 2, 3)
            with nc.allow_non_contiguous_dma(reason="a few small parameters"):
                dma(dft, K["k_dft"]).then_inc(S("hyc_in"), 16)
                dma(w1t[0:HY_FEAT, :], A["hy_w1"][0]).then_inc(S("hyc_in"), 16)
                dma(featt[0:HY_FEAT, :], K["k_feat"]).then_inc(S("hyc_in"), 16)
                for j in range(2):
                    dma(w2t[0:HY_HID, j * HY_HID:(j + 1) * HY_HID], A["hy_w2"][0]).then_inc(S("hyc_in"), 16)
                for src, c, n in ((A["hy_b1"][0], 0, 1), (A["hy_freq"][0, 0], 1, 1), (A["hy_b2"][0], 2, 2), (A["hy_freq"][0, 1], 3, 2)):
                    for j in range(n):
                        dma(fpar[j * HY_HID:(j + 1) * HY_HID, c:c + 1], src.rearrange("(p o) -> p o", o=1)).then_inc(S("hyc_in"), 16)
            w3 = A["hy_w3"][0].rearrange("a (o d n) -> a d o n", o=2, d=2)
            for which, (block, b) in enumerate(((LOADS[len(FIRST) - 6], 0), (LOADS[len(FIRST) - 5], 1))):
                pool.wait_ge(done, LAST_USE[block] + 1)
                if which == 0:
                    for j in range(2):
                        for o in range(2):
                            dma(w3s[j * HY_HID:(j + 1) * HY_HID, :, o, :], w3[:, j, o, :].rearrange("a (b n) -> a b n", b=2))\
                                .then_inc(S("hypar_in"), 16)
                else:
                    for o in range(2):
                        dma(hyb[:, :, o, :], A["hy_bias"][0, o].rearrange("(b n) -> b n", b=2).partition_broadcast(P))\
                            .then_inc(S("hypar_in"), 16)
                dma(decay[b], K["k_decay"][:, :, b * 512:(b + 1) * 512].rearrange("t p n -> p t n")).then_inc(S("hypar_in"), 16)

            def moe(l):
                took(pool, *(("inv", 1, 1, 1, 3) if l == 0 else ("mlo", 1, AH - 1)))
                full(pool, "inv", 1, 1, 1, 3)
                sem = S("router_in%d" % l)
                dma(wr[:, :, 0:NG], A["moe_w_gr"][l].rearrange("(k p) n -> p k n", p=P)).then_inc(sem, 16)
                dma(wr[:, :, NG:NG + E], A["moe_w_er"][l].rearrange("(k p) n -> p k n", p=P)).then_inc(sem, 16)
                dma(rbias[:, 0:NG], A["moe_b_gr"][l].partition_broadcast(P)).then_inc(sem, 16)
                dma(rbias[:, NG:NG + E], A["moe_b_er"][l].partition_broadcast(P)).then_inc(sem, 16)
                dma(slotrow, K["k_slots"]).then_inc(sem, 16)
                sq = area(sq_at["ffn%d" % l], KD, T)
                for k in range(1, KD):
                    pool.wait_ge(S("sq"), sq_base("ffn%d" % l) + k + 1)
                    if k > 1:
                        pool.wait_ge(S("sqsum"), l * (KD - 1) + k - 1)
                    nc.gpsimd.tensor_tensor(sq[:, 0, :], sq[:, 0, :], sq[:, k, :], ALU.add).then_inc(S("sqsum"), 1)

                pool.wait_ge(S("table"), l + 1)
                nc.gpsimd.memset(xs, 0.0).then_inc(S("xs0"), 1)
                pool.wait_ge(S("xs0"), l + 1)

                def gather(n, b):
                    if not (isinstance(n, int) and n < 2):
                        pool.wait_ge(S("x_ps%d" % l), n - 1)
                    pool.wait_ge(S("table"), l + 1)
                    at = tbli[:, n:n + 1] if isinstance(n, int) else tbli[:, bass.ds(n, 1)]
                    need = pool.to_reg(n + 1)
                    nc.gpsimd.tensor_copy(idxc[:, b:b + 1], at).then_inc(S("idx%d" % l), 1)
                    pool.wait_ge(S("rows_out"), 16 * NT * (l + 1))
                    pool.wait_ge(S("idx%d" % l), need)
                    nc.gpsimd.indirect_dma_start(xs[:, b, :], None, rows_d[l], bass.IndirectOffsetOnAxis(ap=idxc[:, b:b + 1], axis=0),
                                                 bounds_check=T - 1, oob_is_err=False)\
                        .then_inc(S("gather%d_%d" % (l, b)), 16)

                def scatter(n, b):
                    for who in ("d_act", "d_dve"):
                        pool.wait_ge(S("%s%d" % (who, l)), n + 1)
                    pool.wait_ge(S("table"), l + 1)
                    need = pool.to_reg(n + 1)
                    nc.gpsimd.tensor_copy(idxc[:, 2 + b:3 + b], scati[:, bass.ds(n, 1)]).then_inc(S("sidx%d" % l), 1)
                    pool.wait_ge(S("rows_out"), 16 * NT * (l + 1))
                    pool.wait_ge(S("sidx%d" % l), need)
                    nc.gpsimd.indirect_dma_start(outs_d[l], bass.IndirectOffsetOnAxis(ap=idxc[:, 2 + b:3 + b], axis=0), ob[:, b, :], None,
                                                 bounds_check=2 * T - 1, oob_is_err=False)\
                        .then_inc(S("stored%d_%d" % (l, b)), 16)

                for n in range(4):
                    gather(n, n % 2)
                r = trips(pool, l)
                with pool.Fori(0, r - 2) as i:
                    for b in range(2):
                        scatter(2 * i + b, b)
                        gather(2 * i + b + 4, b)
                for n in range(4):
                    scatter(2 * r - 4 + n, n % 2)
                need = pool.to_reg(16 * r)
                pool.wait_ge(S("table"), l + 1)
                for b in range(2):
                    pool.wait_ge(S("stored%d_%d" % (l, b)), need)
                src = outs_d[l].rearrange("(c t p) n -> t p c n", c=2, p=P)
                for t in range(NT):
                    dma(yg[t], src[t]).then_inc(S("yg%d" % t), 16)

            moe(0)
            full(pool, "yTr", 0, KD - 1)
            dma(kctok.rearrange("p (h c) -> p h c", h=AH), A["cache_na_k"][0, 0].rearrange("h t c -> t h c")).then_inc(S("nactx_in"), 16)
            dma(vctok.rearrange("p (h c) -> p h c", h=AH), A["cache_na_v"][0, 0].rearrange("h t c -> t h c")).then_inc(S("nactx_in"), 16)
            dma(nmask, K["k_mask"].rearrange("i p n -> p i n")).then_inc(S("nactx_in"), 16)
            dma(rope[AD:QK, :, :], K["k_rope"]).then_inc(S("nactx_in"), 16)
            dma(rev, K["k_rev"]).then_inc(S("nactx_in"), 16)

            def bias_load(i, h):
                tab = A["na_rel_bias"]
                for pr_ in range(2):
                    base = h * 465 + (6 - 2 * i + pr_) * 31 - (GRID_W - WIN_C)
                    src = bass.AP(tab.tensor, base, [[1, GRID_W], [31, LS // GRID_W], [1, GRID_W]])
                    dst = nbias[pr_ * GRID_W:(pr_ + 1) * GRID_W, i, :].rearrange("p (a c) -> p a c", a=LS // GRID_W)
                    dma(dst, src).then_inc(S("nbias%d" % i), 16)

            bias_load(0, 0)
            bias_load(1, 0)
            nc.gpsimd.memset(kr96[:, 0:AD], 0.0).then_inc(S("kr0"), 1)
            dma(ckctok, A["cache_mla_ckv"][0, 0]).then_inc(S("mctx_in"), 16)
            dma(kr96[:, AD:QK], A["cache_mla_krope"][0, 0]).then_inc(S("mctx_in"), 16)
            dma(wuq, A["mla_w_uq"][0].rearrange("(k p) n -> p k n", p=P)).then_inc(S("wmla_in"), 16)
            dma(wukv, A["mla_w_ukv"][0]).then_inc(S("wmla_in"), 16)
            for h in range(1, AH):
                for i in range(2):
                    full(pool, "na", i, h - 1)
                    bias_load(i, h)
            moe(1)


_INS = ['x_prompt', 'x_sample', 'state_ssd', 'cache_na_k', 'cache_na_v', 'cache_mla_ckv', 'cache_mla_krope', 'c', 'c_ctx',
        'w_ada', 'b_ada', 'norm_mix', 'norm_ffn', 'norm_final', 'ev_w_in', 'ev_conv_w', 'ev_conv_b', 'ssd_A_log',
        'ssd_dt_bias', 'ssd_d', 'ssd_norm', 'hy_conv_w', 'hy_conv_b', 'hy_w1', 'hy_b1', 'hy_w2', 'hy_b2', 'hy_w3',
        'hy_freq', 'hy_bias', 'ev_w_out', 'od_w_in', 'mla_q_norm', 'mla_w_uq', 'mla_kv_norm', 'mla_w_ukv',
        'na_rel_bias', 'od_w_out', 'moe_w_gr', 'moe_b_gr', 'moe_w_er', 'moe_b_er', 'moe_w_gate', 'moe_w_up', 'moe_w_down']
_OUTS = [(1, LP, D), (1, LS, D), (1, 1, 2, HEADS, HDIM, STATE), (1, 1, AH, LP, AD), (1, 1, AH, LP, AD),
         (1, 1, LP, P), (1, 1, LP, ROPE)]


def kernel(**inputs):
    import numpy as _np
    import concourse.bacc as _bacc
    from concourse import mybir as _mybir
    from concourse.bass_utils import run_bass_kernel_spmd as _run

    nc = _bacc.Bacc("TRN2", target_bir_lowering=False, num_devices=1)
    arrays, given, consts, outs = {}, {}, {}, []
    for name in _INS:
        a = _np.ascontiguousarray(inputs[name])
        arrays[f"in_{name}_dram"] = a
        given[name] = nc.dram_tensor(f"in_{name}_dram", a.shape, _mybir.dt.from_np(a.dtype), kind="ExternalInput").ap()
    for name, a in host_constants().items():
        a = _np.ascontiguousarray(a)
        arrays[f"in_{name}_dram"] = a
        consts[name] = nc.dram_tensor(f"in_{name}_dram", a.shape, _mybir.dt.from_np(a.dtype), kind="ExternalInput").ap()
    for i, shape in enumerate(_OUTS):
        outs.append(nc.dram_tensor(f"out_{i}_dram", shape, _mybir.dt.float32, kind="ExternalOutput").ap())
    build_kernel(nc, given, consts, outs)
    r = _run(nc, [arrays], core_ids=[0])
    return tuple(r.results[0][f"out_{i}_dram"] for i in range(len(_OUTS)))
```
